# Optimizing a Trainium2 kernel written in Bass

```python
import jax, jax.numpy as jnp
from jax import lax
import numpy as np

D_MODEL = 1024
BATCH = 1
SEQ = 256
DEPTH = 2

N_EVEN = (DEPTH + 1) // 2
N_ODD = DEPTH // 2
N_VRES = max(N_ODD - 1, 0)

POOL_WINDOWS = (2, 4, 8, 16)
N_POOL_GROUPS = len(POOL_WINDOWS)
POOL_GROUP_DIM = D_MODEL // 8
POOL_DIM = N_POOL_GROUPS * POOL_GROUP_DIM
SGU_CHUNK = 128
N_SGU_HEADS = 4
SGU_HEAD_DIM = D_MODEL // 8
SGU_DIM = N_SGU_HEADS * SGU_HEAD_DIM
IN_PROJ_DIM = POOL_DIM + 2 * SGU_DIM
MIX_DIM = POOL_DIM + SGU_DIM
RWKV_HEAD_DIM = 64
RWKV_HEADS = D_MODEL // RWKV_HEAD_DIM
DECAY_LORA = 64
AAA_LORA = 64
MV_LORA = 32
GATE_LORA = 160
D_FF = 2816
N_EXPERTS = 8
TOP_K = 2
D_FF_EXPERT = 3584

RMS_EPS = 1e-6
LN_EPS = 1e-5
GN_EPS = 64e-5

kernel_name = "hybrid_pool_sgu_rwkv7_moe_trunk"

F32 = jnp.float32

def rmsnorm(x, g):
    xf = x.astype(F32)
    y = xf * lax.rsqrt(jnp.mean(xf * xf, axis=-1, keepdims=True) + RMS_EPS)
    return (y * g.astype(F32)).astype(x.dtype)

def pool_mixer(a, pool_w, pool_scale):
    b, n_t, _ = a.shape
    af = a.astype(F32).reshape(b, n_t, N_POOL_GROUPS, POOL_GROUP_DIM)
    csum = jnp.cumsum(af, axis=1)
    pos = jnp.arange(1, n_t + 1, dtype=F32)
    outs = []
    for gi, w in enumerate(POOL_WINDOWS):
        cg = csum[:, :, gi]
        lagged = jnp.pad(cg[:, :n_t - w], ((0, 0), (w, 0), (0, 0)))
        cnt = jnp.minimum(pos, float(w))[None, :, None]
        outs.append((cg - lagged) / cnt - af[:, :, gi])
    pooled = jnp.stack(outs, axis=2)
    y = jnp.einsum('btgc,gcd->btgd', pooled, pool_w.astype(F32))
    return y.reshape(b, n_t, POOL_DIM) * pool_scale.astype(F32)

def spatial_gating(z, ln_g, ln_b, ws, bias):
    b, n_t, _ = z.shape
    u = z[..., :SGU_DIM].astype(F32)
    v = z[..., SGU_DIM:].astype(F32).reshape(b, n_t, N_SGU_HEADS, SGU_HEAD_DIM)
    mu = jnp.mean(v, axis=-1, keepdims=True)
    var = jnp.mean(jnp.square(v - mu), axis=-1, keepdims=True)
    vn = (v - mu) * lax.rsqrt(var + LN_EPS)
    vn = vn * ln_g.astype(F32).reshape(N_SGU_HEADS, SGU_HEAD_DIM) + ln_b.astype(F32).reshape(N_SGU_HEADS, SGU_HEAD_DIM)
    vc = vn.reshape(b, n_t // SGU_CHUNK, SGU_CHUNK, N_SGU_HEADS, SGU_HEAD_DIM)
    mask = jnp.tril(jnp.ones((SGU_CHUNK, SGU_CHUNK), F32))
    mixed = jnp.einsum('hts,bnshc->bnthc', ws.astype(F32) * mask, vc)
    mixed = mixed + bias.astype(F32).T[None, None, :, :, None]
    return u * mixed.reshape(b, n_t, SGU_DIM)

def swiglu(x, wg, wu, wd):
    return (jax.nn.silu(x @ wg) * (x @ wu)) @ wd

def moe_swiglu(xn, router, wg, wu, wd):
    b, n_t, d = xn.shape
    xt = xn.reshape(b * n_t, d)
    logits = xt.astype(F32) @ router.astype(F32)
    top_vals, top_idx = lax.top_k(logits, TOP_K)
    top_w = jax.nn.softmax(top_vals, axis=-1)
    gates = jnp.sum(jax.nn.one_hot(top_idx, N_EXPERTS, dtype=F32) * top_w[..., None], axis=1)
    out = jnp.zeros((b * n_t, d), F32)
    for e in range(N_EXPERTS):
        out = out + gates[:, e:e + 1] * swiglu(xt, wg[e], wu[e], wd[e]).astype(F32)
    return out.reshape(b, n_t, d)

def rwkv7_time_mix(xn, v_first, mu, wr, wk, wv, wo, w0, w1, w2, a0, a1, a2,
                   g1, g2, k_k, k_a, r_k, lnx_w, lnx_b, vres):
    b, n_t, d = xn.shape
    xf = xn.astype(F32)
    x_prev = jnp.pad(xf[:, :-1], ((0, 0), (1, 0), (0, 0)))
    xx = x_prev - xf
    xr, xw, xk, xv, xa, xg = [xf + xx * mu[i] for i in range(6)]
    r = xr @ wr
    k = xk @ wk
    v = xv @ wv
    w_log = -jax.nn.softplus(-(w0 + jnp.tanh(xw @ w1) @ w2)) - 0.5
    decay = jnp.exp(-jnp.exp(w_log))
    if vres is None:
        v_first = v
    else:
        v0, v1, v2 = vres
        v = v + (v_first - v) * jax.nn.sigmoid(v0 + (xv @ v1) @ v2)
    a = jax.nn.sigmoid(a0 + (xa @ a1) @ a2)
    g = jax.nn.sigmoid(xg @ g1) @ g2

    def heads(t):
        return t.astype(F32).reshape(b, n_t, RWKV_HEADS, RWKV_HEAD_DIM)

    kk = heads(k * k_k)
    kk = kk / jnp.maximum(jnp.linalg.norm(kk, axis=-1, keepdims=True), 1e-12)
    k = k * (1.0 + (a - 1.0) * k_a)
    rh, kh, vh, ah, wh = heads(r), heads(k), heads(v), heads(a), heads(decay)

    def tmajor(t):
        return jnp.moveaxis(t, 1, 0)

    def step(S, inp):
        r_t, w_t, k_t, v_t, kk_t, a_t = inp
        sa = jnp.einsum('bhij,bhj->bhi', S, -kk_t)
        S = (S * w_t[:, :, None, :]
             + sa[..., None] * (kk_t * a_t)[:, :, None, :]
             + v_t[..., None] * k_t[:, :, None, :])
        y = jnp.einsum('bhij,bhj->bhi', S, r_t)
        return S, y

    S0 = jnp.zeros((b, RWKV_HEADS, RWKV_HEAD_DIM, RWKV_HEAD_DIM), F32)
    _, ys = lax.scan(step, S0, (tmajor(rh), tmajor(wh), tmajor(kh), tmajor(vh), tmajor(kk), tmajor(ah)))
    y = jnp.moveaxis(ys, 0, 1)
    ym = jnp.mean(y, axis=-1, keepdims=True)
    yv = jnp.mean(jnp.square(y - ym), axis=-1, keepdims=True)
    yn = ((y - ym) * lax.rsqrt(yv + GN_EPS)).reshape(b, n_t, d) * lnx_w + lnx_b
    bonus = jnp.sum(rh * kh * r_k.astype(F32), axis=-1, keepdims=True) * vh
    out = ((yn + bonus.reshape(b, n_t, d)) * g) @ wo
    return out.astype(F32), v_first

def setup_inputs(seed: int = 0) -> dict:
    key = jax.random.key(seed)
    ks = iter(jax.random.split(key, 48))
    D = D_MODEL
    NE, NO, NV = N_EVEN, N_ODD, N_VRES

    def nrm(shape, scale):
        return scale * jax.random.normal(next(ks), shape, F32)

    def near(shape, center, scale):
        return center + nrm(shape, scale)

    def unif(shape, lo, hi):
        return jax.random.uniform(next(ks), shape, F32, lo, hi)

    return {
        "x": nrm((BATCH, SEQ, D), 1.0),
        "e_norm_mix": near((NE, D), 1.0, 0.02),
        "e_w_in": nrm((NE, D, IN_PROJ_DIM), D ** -0.5),
        "e_pool_w": nrm((NE, N_POOL_GROUPS, POOL_GROUP_DIM, POOL_GROUP_DIM), POOL_GROUP_DIM ** -0.5),
        "e_pool_scale": near((NE, POOL_DIM), 1.0, 0.1),
        "e_sgu_ln_g": near((NE, SGU_DIM), 1.0, 0.02),
        "e_sgu_ln_b": nrm((NE, SGU_DIM), 0.02),
        "e_sgu_ws": nrm((NE, N_SGU_HEADS, SGU_CHUNK, SGU_CHUNK), SGU_CHUNK ** -0.5),
        "e_sgu_bias": near((NE, N_SGU_HEADS, SGU_CHUNK), 1.0, 0.1),
        "e_w_out": nrm((NE, MIX_DIM, D), MIX_DIM ** -0.5),
        "e_norm_ffn": near((NE, D), 1.0, 0.02),
        "e_ffn_wg": nrm((NE, D, D_FF), D ** -0.5),
        "e_ffn_wu": nrm((NE, D, D_FF), D ** -0.5),
        "e_ffn_wd": nrm((NE, D_FF, D), D_FF ** -0.5),
        "o_norm_mix": near((NO, D), 1.0, 0.02),
        "o_mu": unif((NO, 6, D), 0.0, 1.0),
        "o_wr": nrm((NO, D, D), D ** -0.5),
        "o_wk": nrm((NO, D, D), D ** -0.5),
        "o_wv": nrm((NO, D, D), D ** -0.5),
        "o_wo": nrm((NO, D, D), D ** -0.5),
        "o_w0": unif((NO, D), -6.0, -0.5),
        "o_w1": nrm((NO, D, DECAY_LORA), D ** -0.5),
        "o_w2": nrm((NO, DECAY_LORA, D), 0.1 * DECAY_LORA ** -0.5),
        "o_a0": nrm((NO, D), 0.1),
        "o_a1": nrm((NO, D, AAA_LORA), D ** -0.5),
        "o_a2": nrm((NO, AAA_LORA, D), 0.1 * AAA_LORA ** -0.5),
        "o_v0": near((NV, D), 1.0, 0.1),
        "o_v1": nrm((NV, D, MV_LORA), D ** -0.5),
        "o_v2": nrm((NV, MV_LORA, D), 0.1 * MV_LORA ** -0.5),
        "o_g1": nrm((NO, D, GATE_LORA), D ** -0.5),
        "o_g2": nrm((NO, GATE_LORA, D), GATE_LORA ** -0.5),
        "o_k_k": near((NO, D), 0.85, 0.05),
        "o_k_a": near((NO, D), 1.0, 0.05),
        "o_r_k": nrm((NO, RWKV_HEADS, RWKV_HEAD_DIM), 0.1),
        "o_lnx_w": near((NO, D), 1.0, 0.02),
        "o_lnx_b": nrm((NO, D), 0.02),
        "o_norm_ffn": near((NO, D), 1.0, 0.02),
        "o_router": nrm((NO, D, N_EXPERTS), D ** -0.5),
        "o_moe_wg": nrm((NO, N_EXPERTS, D, D_FF_EXPERT), D ** -0.5),
        "o_moe_wu": nrm((NO, N_EXPERTS, D, D_FF_EXPERT), D ** -0.5),
        "o_moe_wd": nrm((NO, N_EXPERTS, D_FF_EXPERT, D), D_FF_EXPERT ** -0.5),
        "final_norm": near((D,), 1.0, 0.02),
    }

def reference(x, e_norm_mix, e_w_in, e_pool_w, e_pool_scale, e_sgu_ln_g, e_sgu_ln_b,
              e_sgu_ws, e_sgu_bias, e_w_out, e_norm_ffn, e_ffn_wg, e_ffn_wu, e_ffn_wd,
              o_norm_mix, o_mu, o_wr, o_wk, o_wv, o_wo, o_w0, o_w1, o_w2, o_a0, o_a1, o_a2,
              o_v0, o_v1, o_v2, o_g1, o_g2, o_k_k, o_k_a, o_r_k, o_lnx_w, o_lnx_b,
              o_norm_ffn, o_router, o_moe_wg, o_moe_wu, o_moe_wd, final_norm):
    h = x
    v_first = None
    for layer in range(DEPTH):
        i = layer // 2
        if layer % 2 == 0:
            p = rmsnorm(h, e_norm_mix[i]) @ e_w_in[i]
            a_in = p[..., :POOL_DIM]
            z = jax.nn.gelu(p[..., POOL_DIM:], approximate=False)
            y_a = pool_mixer(a_in, e_pool_w[i], e_pool_scale[i])
            y_b = spatial_gating(z, e_sgu_ln_g[i], e_sgu_ln_b[i], e_sgu_ws[i], e_sgu_bias[i])
            h = h + jnp.concatenate([y_a, y_b], axis=-1) @ e_w_out[i]
            hn = rmsnorm(h, e_norm_ffn[i])
            h = h + swiglu(hn, e_ffn_wg[i], e_ffn_wu[i], e_ffn_wd[i])
        else:
            vres = None if i == 0 else (o_v0[i - 1], o_v1[i - 1], o_v2[i - 1])
            y, v_first = rwkv7_time_mix(
                rmsnorm(h, o_norm_mix[i]), v_first, o_mu[i], o_wr[i], o_wk[i], o_wv[i], o_wo[i],
                o_w0[i], o_w1[i], o_w2[i], o_a0[i], o_a1[i], o_a2[i], o_g1[i], o_g2[i],
                o_k_k[i], o_k_a[i], o_r_k[i], o_lnx_w[i], o_lnx_b[i], vres)
            h = h + y
            hn = rmsnorm(h, o_norm_ffn[i])
            h = h + moe_swiglu(hn, o_router[i], o_moe_wg[i], o_moe_wu[i], o_moe_wd[i])
    return rmsnorm(h, final_norm).astype(x.dtype)


_drawn_inputs = setup_inputs


def setup_inputs(seed=0):
    import zlib

    import numpy as np

    out = dict(_drawn_inputs(seed))
    spreads = {}
    factors = {'e_sgu_ln_g': 4.316,
     'e_sgu_ln_b': 10.165,
     'o_w1': 5.09,
     'o_w2': 4.058,
     'o_lnx_w': 13.422,
     'final_norm': 24.223,
     'e_norm_ffn': 3.552,
     'o_lnx_b': 36.973,
     'o_norm_ffn': 4.24}
    for name, (base, spread) in spreads.items():
        noise = np.random.default_rng([zlib.crc32(name.encode()), seed]).standard_normal(out[name].shape)
        drawn = base * np.exp(spread * noise) if base else spread * noise
        out[name] = __import__('jax').numpy.asarray(drawn.astype(out[name].dtype))
    for name, factor in factors.items():
        out[name] = (out[name] * factor).astype(out[name].dtype)
    return out
```

```python
from contextlib import ExitStack

import numpy as np
import concourse.bass as bass
from concourse import mybir

F32 = mybir.dt.float32
I32 = mybir.dt.int32
ALU = mybir.AluOpType
ACT = mybir.ActivationFunctionType
AX = mybir.AxisListType

P = 128
D = 1024
KT = D // P
T = 256
TB = T // P
WINDOWS = (2, 4, 8, 16)
PAD = 16
F = 2816
FC = 256
NFC = F // FC
NE = 8
FE = 3584
EC = 512
NEC = FE // EC
HD = 64
SQRT_E_INV = float(np.exp(-0.5))
RMS_EPS, LN_EPS, GN_EPS = 1e-6, 1e-5, 64e-5
LEVELS = (1, 2, 4, 8, 16, 32, 64)

CONST = {}
CW = 0
for _name, _w in (("ident", 128), ("upto", 128), ("before", 128), ("heads", 128), ("iota", 128),
                  ("cum", 256), ("level", 128 * len(LEVELS)), ("invcnt", 4 * T), ("ones", 128)):
    CONST[_name] = (CW, CW + _w)
    CW += _w


def constants():
    s = np.arange(P)[:, None]
    t = np.arange(P)[None, :]
    c = np.zeros((P, CW), np.float32)

    def put(name, v):
        c[:, CONST[name][0]:CONST[name][1]] = v

    put("ident", s == t)
    put("upto", s <= t)
    put("before", s < t)
    put("heads", s // HD == t // HD)
    put("iota", np.broadcast_to(t, (P, P)))
    mid = (s < P // 2).astype(np.float32)
    put("cum", np.concatenate([(s <= t) - mid, (s < t) - mid], 1))
    put("level", np.concatenate([(s // (2 * b) == t // (2 * b)) & (s // b % 2 == 0) & (t // b % 2 == 1)
                                 for b in LEVELS], 1))
    tok = np.arange(T)
    put("invcnt", np.concatenate([np.broadcast_to(1.0 / np.minimum(tok + 1, w), (P, T)) for w in WINDOWS], 1))
    put("ones", 1.0)
    return c


COLUMNS = (("e_norm_mix", 8), ("e_norm_ffn", 8), ("o_norm_mix", 8), ("o_norm_ffn", 8), ("e_pool_scale", 4),
           ("e_sgu_bias", 4), ("o_mu", 48), ("o_w0", 8), ("o_a0", 8), ("o_k_k", 8), ("o_k_a", 8), ("o_r_k", 8))
COLUMNS2 = (("o_lnx_w", 8), ("o_lnx_b", 8))
COL = {}
for _group, _base in ((COLUMNS, 0), (COLUMNS2, 128)):
    for _name, _n in _group:
        COL[_name] = _base
        _base += _n


def trunk(nc, I, cst_dram, out, stop=None, probe=None):
    ctx = ExitStack()
    with ctx:
        def sb(name, shape, dt=F32):
            return ctx.enter_context(nc.sbuf_tensor(name, shape, dt))

        def sem(name):
            return ctx.enter_context(nc.semaphore(name))

        U = 2048
        cst = sb("cst", [P, CW])
        colsrc = sb("colsrc", [P, 256])
        cols = sb("cols", [P, 144])
        h = sb("h", [P, TB, D])
        xn = sb("xn", [P, TB * D])
        xnT = sb("xnT", [P, KT, T])
        ring = sb("ring", [P, 14 * U])
        work = sb("work", [P, 7 * U])
        small = sb("small", [P, 256])
        psum = ctx.enter_context(nc.psum_tensor("psum", [P, 8, 512], F32))

        def C(name):
            return cst[:, CONST[name][0]:CONST[name][1]]

        def col(name, k, n=1, p=P):
            return cols[0:p, COL[name] + k:COL[name] + k + n]

        def ru(u, w=U, o=0):
            return ring[:, u * U + o:u * U + o + w]

        def wu(u, w=U, o=0):
            return work[:, u * U + o:u * U + o + w]

        def slot(k):
            return ring[:, 2 * U * k:2 * U * (k + 1)]

        def w8(k):
            return slot(k).rearrange("p (k n) -> p k n", k=KT)

        def r3(ap, a):
            return ap.rearrange("p (a b) -> p a b", a=a)

        ident = C("ident")
        xn3 = r3(xn[:, :], TB)

        E_ = {}
        o = 0
        for name, w in (("a", 4 * (T + PAD)), ("s", 4 * (T + PAD)), ("t", 4 * (T + PAD)), ("uT", 4 * T), ("v", 4 * T),
                        ("vc", 4 * T), ("sq", 4 * T), ("lng", 512), ("lnb", 512), ("bias", 512), ("ws", 512),
                        ("wsT", 512), ("pw", 512)):
            E_[name] = work[:, o:o + w]
            o += w
        mixT = ring[:, 10 * U:11 * U].rearrange("p (k t) -> p k t", k=KT)
        pooled = ring[:, 11 * U:11 * U + 4 * T].rearrange("p (g t) -> p g t", g=4)
        assert o <= 7 * U

        s_cst, s_colsrc, s_x, s_small = sem("cst_in"), sem("colsrc_in"), sem("x_in"), sem("small_in")
        slot_in = [sem(f"slot{k}_in") for k in range(7)]
        ffn_in = [sem(f"ffn{k}_in") for k in range(4)]
        cols_done = sem("cols_copied")
        colT = sem("cols_transposed")
        n_ss, n_ms, n_sd, n_xn = sem("norm_squares"), sem("norm_mean"), sem("norm_sqrt"), sem("norm_rows")
        n_r = sem("norm_recip")
        n_tr, n_eva, n_evd = sem("norm_transposed"), sem("norm_cols_act"), sem("norm_cols_dve")
        dvc = sem("dve_chain")
        acc_ = sem("act_chain")
        plc = sem("pool_chain")
        p_in, a_ev, g_ev = sem("in_proj"), sem("pool_in_copied"), sem("gelu_done")
        z_pad = sem("pads_zeroed")
        s_pooled, s_ymm, s_yev = sem("pooled"), sem("pool_mm"), sem("pool_out")
        s_wsT, s_wsTm, s_vn, s_mm, s_mix = sem("ws_transposed"), sem("ws_masked"), sem("v_normed"), sem("mixed"), sem("mix_out")
        s_wo, s_h = sem("out_proj"), sem("h_added")
        f_gu, f_sil, f_h, f_used = sem("ffn_gate_up"), sem("ffn_silu"), sem("ffn_hidden"), sem("ffn_used")
        s_out = sem("out_written")
        s_dbg = sem("dbg")

        chain = {"dve": 0, "act": 0, "pool": 0}
        CH = {"dve": dvc, "act": acc_, "pool": plc}

        def link(eng, which, ins):
            chain[which] += 1
            ins.then_inc(CH[which], 1)
            eng.wait_ge(CH[which], chain[which])

        def reached(k):
            return stop is None or stop >= k

        def ffn_slot(k):
            b = ring[:, 3 * U * k:3 * U * (k + 1)]
            return (b[:, 0:U].rearrange("p (k f) -> p k f", k=KT), b[:, U:2 * U].rearrange("p (k f) -> p k f", k=KT),
                    b[:, 2 * U:3 * U].rearrange("p (j n) -> p j n", j=2))

        P_ = locals()
        block = ctx.enter_context(nc.Block())

        def norm_act(act, i, s_at=None):
            if i == 0:
                act.wait_ge(s_x, 16)
            else:
                act.wait_ge(s_h, H_AT[i] if s_at is None else s_at)
            if i >= 1:
                act.wait_ge(n_tr, 4 * i)
            for b in range(TB):
                nc.scalar.activation(xn3[:, b, :], h[:, b, :], ACT.Square,
                                     accum_out=small[:, b:b + 1]).then_inc(n_ss, 1)
            act.wait_ge(n_ms, i + 1)
            nc.scalar.activation(small[:, 4:6], small[:, 2:4], ACT.Sqrt).then_inc(n_sd, 1)

        def norm_dve(dve, i):
            dve.wait_ge(n_ss, 2 * i + 2)
            nc.vector.tensor_scalar(small[:, 2:4], small[:, 0:2], 1.0 / D, RMS_EPS, ALU.mult, ALU.add).then_inc(n_ms, 1)
            dve.wait_ge(n_sd, i + 1)
            nc.vector.reciprocal(small[:, 6:8], small[:, 4:6]).then_inc(n_r, 1)
            dve.wait_ge(n_r, i + 1)
            for b in range(TB):
                nc.vector.tensor_scalar(xn3[:, b, :], h[:, b, :], small[:, 6 + b:7 + b], None, ALU.mult).then_inc(n_xn, 1)

        def norm_pe(pe, i):
            pe.wait_ge(n_xn, 2 * i + 2)
            for q in range(4):
                for j in range(2):
                    for b in range(TB):
                        k = 2 * q + j
                        last = nc.tensor.transpose(psum[:, q, j * T + b * P:j * T + b * P + P],
                                                   xn3[:, b, k * P:(k + 1) * P], ident)
                last.then_inc(n_tr, 1)

        def norm_cols(i, gain):
            def act_part(act):
                for q in (0, 2):
                    act.wait_ge(n_tr, 4 * i + q + 1)
                    for j in range(2):
                        k = 2 * q + j
                        nc.scalar.activation(xnT[:, k, :], psum[:, q, j * T:j * T + T], ACT.Copy,
                                             scale=col(gain, k)).then_inc(n_eva, 1)

            def dve_part(dve):
                for q in (1, 3):
                    dve.wait_ge(n_tr, 4 * i + q + 1)
                    for j in range(2):
                        k = 2 * q + j
                        nc.vector.tensor_scalar(xnT[:, k, :], psum[:, q, j * T:j * T + T], col(gain, k), None,
                                                ALU.mult).then_inc(n_evd, 1)
            return act_part, dve_part

        def norm_ready(eng, i):
            eng.wait_ge(n_eva, 4 * i + 4)
            eng.wait_ge(n_evd, 4 * i + 4)

        H_AT = {0: 0, 1: 4, 2: 8, 3: 12, 4: 12}

        def add_to_h(dve, ready, base, bank, one=False):
            for q in range(4):
                dve.wait_ge(ready, base + (1 if one else q + 1))
                hs = h[:, q // 2, 512 * (q % 2):512 * (q % 2) + 512]
                nc.vector.tensor_tensor(hs, hs, psum[:, bank + q, :], ALU.add).then_inc(s_h, 1)

        def rows_product(pe, lhs, w, bank, done):
            for b in range(TB):
                for q in range(2):
                    for k in range(KT):
                        last = nc.tensor.matmul(psum[:, bank + 2 * b + q, :], lhs[:, k, b * P:(b + 1) * P],
                                                w(q)[:, k, :], start=(k == 0), stop=(k == KT - 1))
                    last.then_inc(done, 1)

        lora_in, mix_ready, mix_used = sem("lora_in"), sem("mix_ready"), sem("mix_used")
        o_mm, o_act, o_dve = sem("rwkv_product"), sem("rwkv_evac_act"), sem("rwkv_evac_dve")
        ones_row = sem("ones_row")
        k_sq, k_sd, rk_done, v_rows, bk_rows = sem("k_squares"), sem("k_norms"), sem("rk_done"), sem("v_rows"), sem("bk_rows")
        bk_cols = sem("bk_cols")
        ar_done = sem("scan_operands")
        v_tr, bk_tr = sem("v_transposed"), sem("bk_transposed")
        bonus_done = sem("bonus_done")
        a_mm, a_mask, x_seed, x_tr, x_ev = sem("scan_A"), sem("scan_A_masked"), sem("inverse_seed"), sem("inverse_seed_T"), sem("inverse_seed_copied")
        al_done = sem("level_mask")
        lv_y, lv_yc, lv_x, lv_xa = sem("level_Y"), sem("level_Y_copied"), sem("level_X"), sem("level_X_added")
        t_r, t_rc, t_u, t_uc, t_y, t_yc, t_s, t_sc = (sem(x) for x in (
            "R", "R_copied", "U", "U_copied", "Y", "Y_copied", "S", "S_copied"))
        gn_m, gn_c, gn_q, gn_v, gn_ve, gn_sd, gn_o = (sem(x) for x in (
            "gn_mean", "gn_centred", "gn_squares", "gn_var", "gn_var_copied", "gn_sqrt", "gn_out"))
        wo_done = sem("wo_product")

        w1s = wu(2, 512).rearrange("p (k n) -> p k n", k=KT)
        a1s = wu(2, 512, 512).rearrange("p (k n) -> p k n", k=KT)
        g1s = wu(3, 1280).rearrange("p (k n) -> p k n", k=KT)
        w2s, a2s = wu(5, 1024), wu(5, 1024, 1024)
        g2a, g2b = wu(4, 1024), wu(4, 1024, 1024)
        tw, ta, sga, sgb = (ru(13, 256, 256 * i) for i in range(4))
        mix = [r3(wu(0), KT), r3(wu(1), KT)]
        xx = r3(xn[:, :], KT)
        rT, kT, vT, aT = (r3(wu(i), KT) for i in (2, 3, 5, 6))
        gT, Wi, We, Wv = (r3(ru(i), KT) for i in (8, 9, 10, 11))
        v_row = wu(4)
        sig = r3(ru(12), TB)
        kk, tmp = r3(ru(13), KT), r3(ru(12), KT)
        ARf = work[:, 0:2 * U]
        AR = ARf.rearrange("p (k c a t) -> p k c a t", k=KT, c=2, a=2)
        fac = small[:, 64:72]
        omk = small[:, 72:80]
        b_row, k_row = xn[:, 0:1024], xn[:, 1024:2048]
        A_sb = [ru(9).rearrange("p (l m t) -> p l m t", l=4, m=4), ru(10).rearrange("p (l m t) -> p l m t", l=4, m=4)]
        Xs, XTs, Ys = ([r3(ru(11 + q, 512, 512 * i), 4) for q in range(2)] for i in range(3))
        ALs = [[r3(ru(11 + q, 512, 1536), 4), r3(ru(q, 512), 4)] for q in range(2)]
        Rs = [wu(2, 256, 256 * q) for q in range(2)]
        Us = [wu(2, 256, 512 + 256 * q) for q in range(2)]
        ST = wu(2, 512, 1024).rearrange("p (k i) -> p k i", k=KT)
        YT = aT
        sqT = xnT[:, :, :]
        MIX = (1, 4, 5, 0, 2, 3)

        def evacuated(eng, n):
            if n < 16:
                eng.wait_ge(o_act, n + 1)
            elif n < 24:
                eng.wait_ge(o_dve, n - 15)
            elif n < 32:
                eng.wait_ge(o_act, n - 7)
            else:
                eng.wait_ge(o_dve, n - 23)

        def rwkv_lora_sp(sp):
            sp.wait_ge(s_h, 4)
            one = lambda name: I[name].rearrange("a (k p) n -> p (a k) n", p=P)
            two = lambda name: I[name].rearrange("a k n -> (a k) n")
            g2 = two("o_g2")
            for dst, src in ((w1s, one("o_w1")), (a1s, one("o_a1")), (g1s, one("o_g1")), (w2s[0:64, :], two("o_w2")),
                             (w2s[64:65, :], I["o_w0"]), (a2s[0:64, :], two("o_a2")), (g2a, g2[0:P, :]),
                             (g2b[0:32, :], g2[P:160, :])):
                sp.dma_start(dst, src).then_inc(lora_in, 16)

        def rwkv_sp(sp):
            for n, (name, q) in enumerate((("o_wr", 0), ("o_wr", 1), ("o_wk", 0), ("o_wk", 1),
                                           ("o_wv", 0), ("o_wv", 1), ("o_wo", 0), ("o_wo", 1))):
                if n < 4:
                    sp.wait_ge(f_used, (9, 10, 10, 11)[n])
                else:
                    sp.wait_ge(o_mm, 32 + 4 * (n - 3))
                w = I[name].rearrange("a (k p) n -> p (a k) n", p=P)
                sp.dma_start(w8(n % 4), w[:, :, 512 * q:512 * q + 512]).then_inc(slot_in[n % 4], 16)

        def rwkv_pe(pe):
            pe.wait_ge(s_h, 8)
            norm_pe(pe, 2)
            norm_ready(pe, 2)
            pe.wait_ge(lora_in, 16 * 8)
            pe.wait_ge(f_h, NFC)

            def product(n, lhs_rhs, rows=P, width=T):
                if n >= 8:
                    evacuated(pe, n - 8)
                for i, (l, r) in enumerate(lhs_rhs):
                    last = nc.tensor.matmul(psum[0:rows, n % 8, 0:width], l, r, start=(i == 0), stop=(i == len(lhs_rhs) - 1))
                last.then_inc(o_mm, 1)
                return last

            def used():
                pass
            pe.wait_ge(mix_ready, 1)
            product(0, [(w1s[:, k, :], mix[0][:, k, :]) for k in range(KT)], 64)
            pe.wait_ge(mix_ready, 2)
            product(1, [(a1s[:, k, :], mix[1][:, k, :]) for k in range(KT)], 64)
            pe.wait_ge(mix_ready, 3)
            product(2, [(g1s[:, k, 0:P], mix[0][:, k, :]) for k in range(KT)])
            product(3, [(g1s[:, k, P:160], mix[0][:, k, :]) for k in range(KT)], 32)
            pe.wait_ge(o_act, 1)
            pe.wait_ge(ones_row, 1)
            for b in range(TB):
                for q in range(2):
                    product(4 + 2 * b + q, [(tw[0:65, b * P:(b + 1) * P], w2s[0:65, 512 * q:512 * q + 512])], width=512)
            pe.wait_ge(o_act, 4)
            for k in range(KT):
                product(8 + k, [(a2s[0:64, k * P:(k + 1) * P], ta[0:64, :])])
            for k in range(KT):
                product(16 + k, [(g2a[:, k * P:(k + 1) * P], sga), (g2b[0:32, k * P:(k + 1) * P], sgb[0:32, :])])
            pe.wait_ge(o_act, 8)
            for k in range(KT):
                evacuated(pe, 16 + k)
                for b in range(TB):
                    last = nc.tensor.matmul(psum[:, k, b * T:(b + 1) * T], sig[:, b, k * P:(k + 1) * P], C("cum"),
                                            start=True, stop=True)
                last.then_inc(o_mm, 1)
            for i in range(3):
                pe.wait_ge(mix_ready, 4 + i)
                for q in range(2):
                    s_ = (2 * i + q) % 4
                    pe.wait_ge(slot_in[s_], 32 + 16 * (i == 2))
                    for m in range(4):
                        product(32 + 8 * i + 4 * q + m,
                                [(w8(s_)[:, k, m * P:(m + 1) * P], mix[(3 + i) % 2][:, k, :]) for k in range(KT)])
            pe.wait_ge(k_sq, 1)
            for k in range(KT):
                evacuated(pe, 48 + k)
                nc.tensor.matmul(psum[:, k, 0:T], C("heads"), sqT[:, k, :], start=True, stop=True).then_inc(o_mm, 1)
            for b in range(TB):
                for q in range(2):
                    n = 2 * b + q
                    pe.wait_ge(k_sd, 8)
                    for j in range(4):
                        last = nc.tensor.transpose(psum[:, n, j * P:(j + 1) * P], vT[:, 4 * q + j, b * P:(b + 1) * P], ident)
                    last.then_inc(v_tr, 1)
            pe.wait_ge(rk_done, 1)
            for k in range(KT):
                if k == 4:
                    pe.wait_ge(v_rows, 4)
                nc.tensor.matmul(psum[:, (4 + k) % 8, 0:T], C("heads"), tmp[:, k, :], start=True, stop=True).then_inc(o_mm, 1)
            pe.wait_ge(bk_cols, 2)
            pe.wait_ge(bonus_done, 8)
            for i, src in enumerate((kk, kT)):
                for q in range(2):
                    for j in range(4):
                        last = nc.tensor.transpose(psum[:, 4 + 2 * i + q, j * P:(j + 1) * P], src[:, 4 * q + j, 0:P], ident)
                    last.then_inc(bk_tr, 1)
            pe.wait_ge(bk_rows, 4)
            pe.wait_ge(ar_done, 2)

            for s_ in range(4):
                c = s_ // 2
                heads_ = [[(2 * (2 * s_ % 4 + q) + l // 2, HD * (l % 2)) for l in range(4)] for q in range(2)]
                for q in range(2):
                    if s_ >= 1:
                        pe.wait_ge(t_yc, 2 * (s_ - 1) + q + 1)
                        if c == 0 or s_ == 2:
                            pe.wait_ge(t_sc, 2 * min(s_ - 1, 1) + q + 1)
                    for l, (k, o) in enumerate(heads_[q]):
                        rhs = AR[o:o + HD, k, c, :, :]
                        nc.tensor.matmul(psum[:, 4 * q + l, 0:T], kk[o:o + HD, k, c * P:(c + 1) * P], rhs, start=True, stop=True)
                        last = nc.tensor.matmul(psum[:, 4 * q + l, T:2 * T], kT[o:o + HD, k, c * P:(c + 1) * P], rhs,
                                                start=True, stop=True)
                    last.then_inc(a_mm, 1)
                for q in range(2):
                    g = 2 * s_ + q
                    pe.wait_ge(x_seed, g + 1)
                    pe.wait_ge(a_mask, g + 1)
                    for l in range(4):
                        last = nc.tensor.transpose(psum[:, 4 * q, l * P:(l + 1) * P], XTs[q][:, l, :], ident)
                    last.then_inc(x_tr, 1)
                for li in range(1, 7):
                    for q in range(2):
                        g = 2 * s_ + q
                        n = 6 * g + li - 1
                        pe.wait_ge(al_done, lev(s_, li, q))
                        if li == 1:
                            pe.wait_ge(x_ev, g + 1)
                        else:
                            pe.wait_ge(lv_xa, lev(s_, li - 1, q))
                        for l in range(4):
                            last = nc.tensor.matmul(psum[:, 4 * q + 1, l * P:(l + 1) * P], ALs[q][li % 2][:, l, :],
                                                    Xs[q][:, l, :], start=True, stop=True)
                        last.then_inc(lv_y, 1)
                    for q in range(2):
                        pe.wait_ge(lv_yc, lev(s_, li, q))
                        for l in range(4):
                            last = nc.tensor.matmul(psum[:, 4 * q + 2, l * P:(l + 1) * P], Ys[q][:, l, :], XTs[q][:, l, :],
                                                    start=True, stop=True)
                        if li < 6:
                            for l in range(4):
                                last = nc.tensor.matmul(psum[:, 4 * q + 3, l * P:(l + 1) * P], XTs[q][:, l, :],
                                                        Ys[q][:, l, :], start=True, stop=True)
                        last.then_inc(lv_x, 1)
                for q in range(2):
                    g = 2 * s_ + q
                    for l, (k, o) in enumerate(heads_[q]):
                        dst = psum[:, 4 * q + 3 * (l % 2), (l // 2) * HD:(l // 2 + 1) * HD]
                        last = nc.tensor.matmul(dst, A_sb[q][:, l, 2, :], v_row[:, c * D + k * P + o:c * D + k * P + o + HD],
                                                start=True, stop=(c == 0))
                        if c == 1:
                            pe.wait_ge(t_sc, 4)
                            last = nc.tensor.matmul(dst, AR[o:o + HD, k, c, 0, :], ST[o:o + HD, k, :], start=False, stop=True)
                    last.then_inc(t_r, 1)
                for q in range(2):
                    g = 2 * s_ + q
                    pe.wait_ge(t_rc, g + 1)
                    pe.wait_ge(lv_xa, lev(s_, 6, q))
                    for l in range(4):
                        last = nc.tensor.matmul(psum[:, 4 * q + 1, l * HD:(l + 1) * HD], XTs[q][:, l, :],
                                                Rs[q][:, l * HD:(l + 1) * HD], start=True, stop=True)
                    last.then_inc(t_u, 1)
                for q in range(2):
                    g = 2 * s_ + q
                    pe.wait_ge(t_uc, g + 1)
                    for l, (k, o) in enumerate(heads_[q]):
                        dst = psum[o:o + HD, 4 * q + 2, (l // 2) * P:(l // 2 + 1) * P]
                        vv = v_row[:, c * D + k * P + o:c * D + k * P + o + HD]
                        uu = Us[q][:, l * HD:(l + 1) * HD]
                        nc.tensor.matmul(dst, uu, A_sb[q][:, l, 1, :], start=True, stop=False)
                        last = nc.tensor.matmul(dst, vv, A_sb[q][:, l, 3, :], start=False, stop=(c == 0))
                        if c == 1:
                            last = nc.tensor.matmul(dst, ST[o:o + HD, k, :], AR[o:o + HD, k, c, 1, :], start=False, stop=True)
                    last.then_inc(t_y, 1)
                    if c == 0:
                        for l, (k, o) in enumerate(heads_[q]):
                            dst = psum[o:o + HD, 4 * q + 3, (l // 2) * HD:(l // 2 + 1) * HD]
                            vv = v_row[:, k * P + o:k * P + o + HD]
                            uu = Us[q][:, l * HD:(l + 1) * HD]
                            nc.tensor.matmul(dst, b_row[:, k * P + o:k * P + o + HD], uu, start=True, stop=False)
                            last = nc.tensor.matmul(dst, k_row[:, k * P + o:k * P + o + HD], vv, start=False, stop=True)
                        last.then_inc(t_s, 1)
            pe.wait_ge(t_yc, 8)
            pe.wait_ge(lv_xa, lev(3, 6, 1))
            for k in range(KT):
                nc.tensor.matmul(psum[:, k, 0:T], C("heads"), YT[:, k, :], start=True, stop=True).then_inc(gn_m, 1)
            pe.wait_ge(gn_q, 1)
            for k in range(KT):
                nc.tensor.matmul(psum[:, k, 0:T], C("heads"), sqT[:, k, :], start=True, stop=True).then_inc(gn_v, 1)
            pe.wait_ge(gn_o, 1)
            for n in (2, 3):
                pe.wait_ge(slot_in[n], 48)
            rows_product(pe, YT, lambda q: w8(2 + q), 0, wo_done)

        def lev(s_, li, q):
            return 12 * s_ + 2 * (li - 1) + q + 1

        def rwkv_act(act):
            norm_act(act, 2)
            norm_cols(2, "o_norm_mix")[0](act)
            for n in range(16):
                act.wait_ge(o_mm, n + 1)
                ps = psum[:, n, :] if n < 8 else psum[:, n - 8, 0:T]
                if n == 0:
                    i_ = nc.scalar.activation(tw[0:64, :], ps[0:64, 0:T], ACT.Tanh)
                elif n == 1:
                    i_ = nc.scalar.activation(ta[0:64, :], ps[0:64, 0:T], ACT.Copy)
                elif n == 2:
                    i_ = nc.scalar.activation(sga, ps[:, 0:T], ACT.Sigmoid)
                elif n == 3:
                    i_ = nc.scalar.activation(sgb[0:32, :], ps[0:32, 0:T], ACT.Sigmoid)
                elif n < 8:
                    i_ = nc.scalar.activation(sig[:, (n - 4) // 2, (n % 2) * 512:(n % 2) * 512 + 512], ps, ACT.Sigmoid)
                else:
                    i_ = nc.scalar.activation(aT[:, n - 8, :], ps, ACT.Sigmoid, bias=col("o_a0", n - 8))
                i_.then_inc(o_act, 1)
            for k in range(KT):
                act.wait_ge(o_mm, 25 + k)
                ps = psum[:, k, :].rearrange("p (b a t) -> p b a t", b=TB, a=2)
                two = lambda x: x[:, k, :].rearrange("p (b t) -> p b t", b=TB)
                nc.scalar.activation(two(Wi), ps[:, :, 0, :], ACT.Exp, scale=-SQRT_E_INV)
                nc.scalar.activation(two(We), ps[:, :, 1, :], ACT.Exp, scale=-SQRT_E_INV)
                nc.scalar.activation(two(Wv), ps[:, :, 0, :], ACT.Exp, scale=SQRT_E_INV).then_inc(o_act, 1)
            for k in range(KT):
                act.wait_ge(o_mm, 57 + k)
                nc.scalar.activation(xx[:, k, :], psum[:, k, 0:T], ACT.Sqrt).then_inc(k_sd, 1)
            for n in range(4):
                act.wait_ge(v_tr, n + 1)
                nc.scalar.activation(v_row[:, 512 * n:512 * n + 512], psum[:, n, :], ACT.Copy).then_inc(v_rows, 1)
            for n in range(4):
                act.wait_ge(bk_tr, n + 1)
                nc.scalar.activation(xn[:, 512 * n:512 * n + 512], psum[:, 4 + n, :], ACT.Copy).then_inc(bk_rows, 1)
            for s_ in range(4):
                c = s_ // 2
                for q in range(2):
                    act.wait_ge(x_tr, 2 * s_ + q + 1)
                    if s_ >= 1:
                        act.wait_ge(lv_x, lev(s_ - 1, 6, q))
                    nc.scalar.activation(Xs[q], r3(psum[:, 4 * q, :], 4), ACT.Copy).then_inc(x_ev, 1)
                for li in range(1, 7):
                    for q in range(2):
                        act.wait_ge(lv_y, lev(s_, li, q))
                        nc.scalar.activation(Ys[q], r3(psum[:, 4 * q + 1, :], 4), ACT.Copy).then_inc(lv_yc, 1)
                for q in range(2):
                    act.wait_ge(t_r, 2 * s_ + q + 1)
                    for e in range(2):
                        last = nc.scalar.activation(Rs[q].rearrange("p (j e i) -> p e j i", j=2, e=2)[:, e],
                                                    r3(psum[:, 4 * q + 3 * e, 0:2 * HD], 2), ACT.Copy)
                    last.then_inc(t_rc, 1)
                for q in range(2):
                    act.wait_ge(t_y, 2 * s_ + q + 1)
                    k = 2 * (2 * s_ % 4 + q)
                    nc.scalar.activation(YT[:, k:k + 2, c * P:(c + 1) * P], r3(psum[:, 4 * q + 2, 0:256], 2),
                                         ACT.Copy).then_inc(t_yc, 1)
            act.wait_ge(gn_c, 8)
            nc.scalar.activation(sqT, YT, ACT.Square).then_inc(gn_q, 1)
            act.wait_ge(gn_ve, 8)
            nc.scalar.activation(tmp, tmp, ACT.Sqrt).then_inc(gn_sd, 1)

        def rwkv_dve(dve):
            norm_dve(dve, 2)
            norm_cols(2, "o_norm_mix")[1](dve)
            nc.vector.tensor_scalar(omk, col("o_k_a", 0, 8), -1.0, 1.0, ALU.mult, ALU.add)
            nc.vector.memset(tw[64:65, :], 1.0).then_inc(ones_row, 1)
            norm_ready(dve, 2)
            nc.vector.tensor_tensor(xx[:, :, 1:], xnT[:, :, 0:T - 1], xnT[:, :, 1:], ALU.subtract)
            link(dve, "dve", nc.vector.tensor_scalar(xx[:, :, 0:1], xnT[:, :, 0:1], -1.0, None, ALU.mult))
            dve.wait_ge(f_used, NFC)

            def mixed(j):
                if j >= 2:
                    dve.wait_ge(o_mm, (1, 2, 4, 40)[j - 2] if j < 5 else 40)
                for k in range(KT):
                    last = nc.vector.scalar_tensor_tensor(out=mix[j % 2][:, k, :], in0=xx[:, k, :],
                                                          scalar=col("o_mu", 8 * MIX[j] + k), in1=xnT[:, k, :],
                                                          op0=ALU.mult, op1=ALU.add)
                last.then_inc(mix_ready, 1)

            def copies(dst, n0):
                for k in range(KT):
                    dve.wait_ge(o_mm, n0 + k + 1)
                    nc.vector.tensor_copy(dst[:, k, :], psum[:, k, 0:T]).then_inc(o_dve, 1)

            for j in range(5):
                mixed(j)
            copies(gT, 16)
            copies(rT, 32)
            mixed(5)
            copies(kT, 40)
            dve.wait_ge(o_dve, 24)
            for k in range(KT):
                last = nc.vector.tensor_scalar(kk[:, k, :], kT[:, k, :], col("o_k_k", k), None, ALU.mult)
            link(dve, "dve", last)
            nc.vector.tensor_tensor(sqT, kk, kk, ALU.mult).then_inc(k_sq, 1)
            copies(vT, 48)
            dve.wait_ge(o_act, 24)
            for k in range(KT):
                last = nc.vector.tensor_scalar(tmp[:, k, :], aT[:, k, :], col("o_k_a", k), omk[:, k:k + 1], ALU.mult, ALU.add)
            link(dve, "dve", last)
            link(dve, "dve", nc.vector.tensor_tensor(kT, kT, tmp, ALU.mult))
            for k in range(KT):
                last = nc.vector.scalar_tensor_tensor(out=tmp[:, k, :], in0=rT[:, k, :], scalar=col("o_r_k", k),
                                                      in1=kT[:, k, :], op0=ALU.mult, op1=ALU.mult)
            last.then_inc(rk_done, 1)
            dve.wait_ge(k_sd, 8)
            link(dve, "dve", nc.vector.tensor_scalar(xx, xx, 1e-12, None, ALU.max))
            link(dve, "dve", nc.vector.reciprocal(xx, xx))
            link(dve, "dve", nc.vector.tensor_tensor(kk, kk, xx, ALU.mult))
            kct = lambda x: x.rearrange("p k (c t) -> p k c t", c=2)
            for c in range(2):
                sl = slice(c * P, (c + 1) * P)
                last = nc.vector.scalar_tensor_tensor(out=AR[:, :, c, 0, :], in0=kk[:, :, sl], scalar=-1.0,
                                                      in1=We[:, :, sl], op0=ALU.mult, op1=ALU.mult)
            link(dve, "dve", last)
            link(dve, "dve", nc.vector.tensor_tensor(kk, kk, aT, ALU.mult))
            nc.vector.tensor_tensor(kk, kk, Wv, ALU.mult).then_inc(bk_cols, 1)
            dve.wait_ge(v_tr, 4)
            for k in range(KT):
                dve.wait_ge(o_mm, 65 + k)
                nc.vector.tensor_tensor(vT[:, k, :], vT[:, k, :], psum[:, (4 + k) % 8, 0:T], ALU.mult).then_inc(bonus_done, 1)
            dve.wait_ge(rk_done, 1)
            nc.vector.tensor_tensor(kT, kT, Wv, ALU.mult).then_inc(bk_cols, 1)
            for c in range(2):
                sl = slice(c * P, (c + 1) * P)
                nc.vector.tensor_tensor(AR[:, :, c, 1, :], rT[:, :, sl], Wi[:, :, sl], ALU.mult).then_inc(ar_done, 1)
            link(dve, "dve", nc.vector.reciprocal(fac, We[:, :, P]))
            link(dve, "dve", nc.vector.tensor_tensor(fac, fac, Wi[:, :, P - 1], ALU.mult))
            dve.wait_ge(ar_done, 2)
            mask = cst[:, CONST["upto"][0]:CONST["before"][1]]
            for s_ in range(4):
                c = s_ // 2
                for q in range(2):
                    g = 2 * s_ + q
                    dve.wait_ge(a_mm, g + 1)
                    if s_ >= 1:
                        dve.wait_ge(al_done, lev(s_ - 1, 6, q))
                        dve.wait_ge(t_y, 2 * (s_ - 1) + q + 1)
                    for l in range(4):
                        for m, name in ((0, "before"), (1, "upto")):
                            src = psum[:, 4 * q + l, :].rearrange("p (a m t) -> p a m t", a=2, m=2)[:, :, m, :]
                            dst = A_sb[q][:, l, :, :].rearrange("p (a m) t -> p a m t", a=2)[:, :, m, :]
                            last = nc.vector.tensor_tensor(dst, src, C(name).unsqueeze(1).to_broadcast([P, 2, P]), ALU.mult)
                    last.then_inc(a_mask, 1)
                    dve.wait_ge(a_mask, g + 1)
                    four = lambda x: x.unsqueeze(1).to_broadcast([P, 4, P])
                    lv = C("level")[:, 0:P]
                    if s_ >= 1:
                        dve.wait_ge(t_u, 2 * (s_ - 1) + q + 1)
                    link(dve, "dve", nc.vector.tensor_tensor(XTs[q], A_sb[q][:, :, 0, :], four(lv), ALU.mult))
                    nc.vector.tensor_tensor(XTs[q], XTs[q], four(ident), ALU.add).then_inc(x_seed, 1)
                for li in range(1, 7):
                    for q in range(2):
                        dve.wait_ge(lv_x, lev(s_, li, q))
                        if li < 6:
                            nc.vector.tensor_tensor(Xs[q], Xs[q], r3(psum[:, 4 * q + 3, :], 4), ALU.add)
                        nc.vector.tensor_tensor(XTs[q], XTs[q], r3(psum[:, 4 * q + 2, :], 4), ALU.add).then_inc(lv_xa, 1)
                for q in range(2):
                    g = 2 * s_ + q
                    dve.wait_ge(t_u, g + 1)
                    nc.vector.tensor_copy(Us[q], psum[:, 4 * q + 1, 0:256]).then_inc(t_uc, 1)
                if c == 0:
                    for q in range(2):
                        g = 2 * s_ + q
                        dve.wait_ge(t_s, g + 1)
                        for j in range(2):
                            k = 2 * (2 * s_ % 4 + q) + j
                            last = nc.vector.tensor_scalar(ST[:, k, :], psum[:, 4 * q + 3, j * HD:(j + 1) * HD],
                                                           fac[:, k:k + 1], None, ALU.mult)
                        last.then_inc(t_sc, 1)
            for k in range(KT):
                dve.wait_ge(gn_m, k + 1)
                nc.vector.scalar_tensor_tensor(out=YT[:, k, :], in0=psum[:, k, 0:T], scalar=-1.0 / HD, in1=YT[:, k, :],
                                               op0=ALU.mult, op1=ALU.add).then_inc(gn_c, 1)
            for k in range(KT):
                dve.wait_ge(gn_v, k + 1)
                nc.vector.tensor_scalar(tmp[:, k, :], psum[:, k, 0:T], 1.0 / HD, GN_EPS, ALU.mult, ALU.add).then_inc(gn_ve, 1)
            dve.wait_ge(gn_sd, 1)
            link(dve, "dve", nc.vector.reciprocal(tmp, tmp))
            link(dve, "dve", nc.vector.tensor_tensor(YT, YT, tmp, ALU.mult))
            for k in range(KT):
                last = nc.vector.tensor_scalar(YT[:, k, :], YT[:, k, :], col("o_lnx_w", k), col("o_lnx_b", k), ALU.mult, ALU.add)
            link(dve, "dve", last)
            link(dve, "dve", nc.vector.tensor_tensor(YT, YT, vT, ALU.add))
            nc.vector.tensor_tensor(YT, YT, gT, ALU.mult).then_inc(gn_o, 1)
            add_to_h(dve, wo_done, 0, 0)

        def rwkv_pool(pool):
            for s_ in range(4):
                for li in range(1, 7):
                    for q in range(2):
                        if li == 1:
                            pool.wait_ge(a_mask, 2 * s_ + q + 1)
                        if li >= 3:
                            pool.wait_ge(lv_y, lev(s_, li - 2, q))
                        elif s_ >= 1:
                            pool.wait_ge(lv_y, lev(s_ - 1, li + 4, q))
                        m = C("level")[:, li * P:(li + 1) * P].unsqueeze(1).to_broadcast([P, 4, P])
                        nc.gpsimd.tensor_tensor(ALs[q][li % 2], A_sb[q][:, :, 0, :], m, ALU.mult).then_inc(al_done, 1)
        r_in, r_mm, r_lg, r_ex, r_exd, r_sel, r_rank, r_jobs = (sem(x) for x in (
            "router_in", "router_product", "logits", "gate_exp_in", "gate_exp", "selected", "ranks", "jobs_ready"))
        m_dn, m_gu, m_sil, m_h, m_T, m_hT = (sem(x) for x in (
            "expert_down", "expert_gate_up", "expert_silu", "expert_hidden", "expert_hidden_T", "expert_hidden_cols"))
        m_p, m_pt, m_pte, m_ga, m_xg, m_y, m_yc, m_sc = (sem(x) for x in (
            "onehot_ready", "gates_transposed", "gates_copied", "gathered", "gathered_cols", "expert_out", "expert_out_copied",
            "scattered"))
        jobs = sb("jobs", [P, 32], I32)
        XgT = wu(0, 1024).rearrange("p (k s) -> p k s", k=KT)
        Pm, Pg, PgT = wu(1, 256), wu(1, 256, 256), wu(1, 256, 512)
        Ysb = wu(1, 1024, 1024)
        SIL = [wu(2, 512, 512 * i) for i in range(2)]
        HS = [wu(2, 512, 1024 + 512 * i) for i in range(2)]
        HT = [wu(3, 512, 512 * i) for i in range(2)]
        gain = wu(5, 1024)
        tb_ = {}
        o = 0
        for name, w in (("rw", 64), ("L", 16), ("L2", 16), ("m1", 2), ("m2", 2), ("i1", 2), ("i2", 2), ("eq", 16), ("oh1", 16),
                        ("oh2", 16), ("ex", 2), ("w1", 2), ("w2", 2), ("g2", 16), ("sel", 16), ("rk", 32), ("gt", 32),
                        ("ova", 12), ("ovb", 12), ("ovc", 12), ("io8", 8), ("pick", 8), ("jf", 32), ("d", 2)):
            tb_[name] = wu(4, w, o)
            o += w
        router = tb_["rw"].rearrange("p (k e) -> p k e", k=KT)

        LOADS = [("g", 0), ("u", 0)]
        for c in range(1, NEC):
            LOADS += [("g", c), ("u", c), ("d", c - 1)]
        LOADS += [("d", NEC - 1)]
        NL = len(LOADS)
        assert NL % 7 == 0
        AT = {x: i for i, x in enumerate(LOADS)}
        LANDED = (48, 48, 48, 48, 16, 0, 0)

        def loaded(eng, j, x):
            i = AT[x]
            eng.wait_ge(slot_in[i % 7], LANDED[i % 7] + 16 * (i // 7 + 1) + j * (16 * NL // 7))

        def moe_sp(sp):
            sp.wait_ge(gn_o, 1)
            sp.dma_start(router, I["o_router"].rearrange("a (k p) e -> p (a k) e", p=P)).then_inc(r_in, 16)
            sp.dma_start(gain, I["final_norm"].partition_broadcast(P)).then_inc(r_in, 16)
            wg = I["o_moe_wg"].rearrange("a e (k p) f -> (a e) p k f", p=P)
            wup = I["o_moe_wu"].rearrange("a e (k p) f -> (a e) p k f", p=P)
            wd = I["o_moe_wd"].rearrange("a e (k p) n -> (a e) p k n", p=P)

            def load(i, e):
                what, c = LOADS[i]
                if what == "d":
                    src = wd[bass.ds(e, 1), :, 4 * c:4 * c + 4, :]
                    dst = slot(i % 7).rearrange("p (k n) -> p k n", k=4)
                else:
                    src = (wg if what == "g" else wup)[bass.ds(e, 1), :, :, EC * c:EC * c + EC]
                    dst = w8(i % 7)
                sp.dma_start(dst, src.rearrange("o p k n -> (o p) k n")).then_inc(slot_in[i % 7], 16)

            def free(i, j):
                what, c = LOADS[i]
                if what == "d":
                    sp.wait_ge(m_dn, j * NEC + (c + 1))
                else:
                    sp.wait_ge(m_gu, j * (2 * NEC) + (2 * c + 1 + (what == "u")))

            for i in range(NL):
                if i == 2:
                    sp.wait_ge(wo_done, 4)
                if i >= 7:
                    free(i - 7, 0)
                load(i, 0)
            sp.wait_ge(r_jobs, 2)
            J = sp.value_load(jobs[0:1, 12:13], min_val=NE, max_val=NE + 3)
            with sp.Fori(1, J) as j:
                e = sp.value_load(jobs[0:1, bass.ds(j + 16, 1)], min_val=0, max_val=NE - 1)
                for i in range(NL):
                    if i >= 7:
                        free(i - 7, j)
                    else:
                        free(i - 7 + NL, j - 1)
                    load(i, e)

        def gather(pe, ready):
            pe.wait_ge(m_p, ready)
            for q in range(2):
                for kk_ in range(4):
                    k = 4 * q + kk_
                    for b in range(TB):
                        last = nc.tensor.matmul(psum[:, 2 + q, kk_ * P:(kk_ + 1) * P], xn3[:, b, k * P:(k + 1) * P],
                                                Pm[:, b * P:(b + 1) * P], start=(b == 0), stop=(b == TB - 1))
                last.then_inc(m_ga, 1)

        def moe_pe(pe):
            pe.wait_ge(s_h, 12)
            norm_pe(pe, 3)
            norm_ready(pe, 3)
            pe.wait_ge(r_in, 32)
            for b in range(TB):
                for k in range(KT):
                    last = nc.tensor.matmul(psum[:, 4, 8 * b:8 * b + 8], xnT[:, k, b * P:(b + 1) * P], router[:, k, :],
                                            start=(k == 0), stop=(k == KT - 1))
            last.then_inc(r_mm, 1)
            pe.wait_ge(r_sel, 1)
            sel = r3(tb_["sel"], TB)
            nc.tensor.matmul(psum[:, 5, 0:8], C("before"), sel[:, 0, :], start=True, stop=True)
            nc.tensor.matmul(psum[:, 5, 8:16], C("before"), sel[:, 1, :], start=True, stop=False)
            nc.tensor.matmul(psum[:, 5, 8:16], C("ones"), sel[:, 0, :], start=False, stop=True)
            nc.tensor.matmul(psum[:, 5, 16:24], C("ones"), sel[:, 0, :], start=True, stop=False)
            nc.tensor.matmul(psum[:, 5, 16:24], C("ones"), sel[:, 1, :], start=False, stop=True).then_inc(r_mm, 1)
            gather(pe, 1)

            def hidden(j, x, c):
                what = "gu"[x]
                loaded(pe, j, (what, c))
                w = w8(AT[what, c] % 7)
                for k in range(KT):
                    last = nc.tensor.matmul(psum[:, 2 * (c % 2) + x, :], XgT[:, k, :], w[:, k, :],
                                            start=(k == 0), stop=(k == KT - 1))
                last.then_inc(m_gu, 1)

            def turned(j, c):
                pe.wait_ge(m_h, j * NEC + (c + 1))
                for f in range(4):
                    last = nc.tensor.transpose(psum[:, 6, f * P:(f + 1) * P], HS[c % 2][:, f * P:(f + 1) * P], ident)
                last.then_inc(m_T, 1)

            def down(j, c):
                loaded(pe, j, ("d", c))
                pe.wait_ge(m_hT, j * NEC + (c + 1))
                w = slot(AT["d", c] % 7).rearrange("p (k n) -> p k n", k=4)
                for q in range(2):
                    for f in range(4):
                        last = nc.tensor.matmul(psum[:, 4 + q, :], HT[c % 2][:, f * P:(f + 1) * P],
                                                w[:, f, 512 * q:512 * q + 512], start=(c == 0 and f == 0),
                                                stop=(c == NEC - 1 and f == 3))
                    if q == 0 and c == NEC - 1:
                        last.then_inc(m_y, 1)
                last.then_inc(m_dn, 1)

            pe.wait_ge(r_jobs, 2)
            J = pe.value_load(jobs[0:1, 12:13], min_val=NE, max_val=NE + 3)
            with pe.Fori(0, J) as j:
                pe.wait_ge(m_xg, j + 1)
                pe.wait_ge(s_h, j * 4 + 12)
                for c in range(NEC):
                    hidden(j, 0, c)
                    if c == 1:
                        for b in range(TB):
                            last = nc.tensor.transpose(psum[:, 7, b * P:(b + 1) * P], Pg[:, b * P:(b + 1) * P], ident)
                        last.then_inc(m_pt, 1)
                    if c >= 1:
                        turned(j, c - 1)
                    hidden(j, 1, c)
                    if c >= 1:
                        down(j, c - 1)
                turned(j, NEC - 1)
                gather(pe, j + 2)
                down(j, NEC - 1)
                pe.wait_ge(m_pte, j + 1)
                for q in range(2):
                    pe.wait_ge(m_yc, j * 2 + (q + 1))
                    for b in range(TB):
                        nc.tensor.matmul(psum[:, 6 * q + b, :], PgT[:, b * P:(b + 1) * P], Ysb[:, 512 * q:512 * q + 512],
                                         start=True, stop=True).then_inc(m_sc, 1)

        def moe_act(act):
            norm_act(act, 3)
            norm_cols(3, "o_norm_ffn")[0](act)
            act.wait_ge(r_ex, 1)
            nc.scalar.activation(tb_["ex"], tb_["d"], ACT.Exp).then_inc(r_exd, 1)
            act.wait_ge(r_jobs, 2)
            J = act.value_load(jobs[0:1, 12:13], min_val=NE, max_val=NE + 3)
            with act.Fori(0, J) as j:
                def turned(c):
                    act.wait_ge(m_T, j * NEC + (c + 1))
                    nc.scalar.activation(HT[c % 2], psum[:, 6, :], ACT.Copy).then_inc(m_hT, 1)
                for c in range(NEC):
                    act.wait_ge(m_gu, j * (2 * NEC) + (2 * c + 1))
                    nc.scalar.activation(SIL[c % 2], psum[:, 2 * (c % 2), :], ACT.Silu).then_inc(m_sil, 1)
                    if c >= 1:
                        turned(c - 1)
                turned(NEC - 1)
                for q in range(2):
                    if q == 0:
                        act.wait_ge(m_y, j + 1)
                    else:
                        act.wait_ge(m_dn, j * NEC + NEC)
                    nc.scalar.activation(Ysb[:, 512 * q:512 * q + 512], psum[:, 4 + q, :], ACT.Copy).then_inc(m_yc, 1)
            norm_act(act, 4, s_at=J * 4 + 12)

        def moe_dve(dve):
            norm_dve(dve, 3)
            norm_cols(3, "o_norm_ffn")[1](dve)
            L, L2, eq, oh1, oh2, g2_, sel = (r3(tb_[x], TB) for x in ("L", "L2", "eq", "oh1", "oh2", "g2", "sel"))
            wide = lambda x: tb_[x].unsqueeze(2).to_broadcast([P, TB, NE])
            iota8 = C("iota")[:, 0:NE]
            io = iota8.unsqueeze(1).to_broadcast([P, TB, NE])
            go = lambda ins: link(dve, "dve", ins)
            V = nc.vector
            dve.wait_ge(r_mm, 1)
            go(V.tensor_copy(L, r3(psum[:, 4, 0:16], TB)))
            go(V.tensor_reduce(tb_["m1"], L, AX.X, ALU.max))
            go(V.tensor_tensor(eq, L, wide("m1"), ALU.is_equal))
            go(V.scalar_tensor_tensor(out=eq, in0=eq, scalar=-float(NE), in1=io, op0=ALU.mult, op1=ALU.add))
            go(V.tensor_reduce(tb_["i1"], eq, AX.X, ALU.min))
            go(V.tensor_tensor(oh1, eq, wide("i1"), ALU.is_equal))
            go(V.scalar_tensor_tensor(out=L2, in0=oh1, scalar=-1e30, in1=L, op0=ALU.mult, op1=ALU.add))
            go(V.tensor_reduce(tb_["m2"], L2, AX.X, ALU.max))
            go(V.tensor_tensor(eq, L2, wide("m2"), ALU.is_equal))
            go(V.scalar_tensor_tensor(out=eq, in0=eq, scalar=-float(NE), in1=io, op0=ALU.mult, op1=ALU.add))
            go(V.tensor_reduce(tb_["i2"], eq, AX.X, ALU.min))
            go(V.tensor_tensor(oh2, eq, wide("i2"), ALU.is_equal))
            V.tensor_tensor(tb_["d"], tb_["m2"], tb_["m1"], ALU.subtract).then_inc(r_ex, 1)
            V.tensor_tensor(sel, oh1, oh2, ALU.add).then_inc(r_sel, 1)
            dve.wait_ge(r_exd, 1)
            go(V.tensor_scalar(tb_["w2"], tb_["ex"], 1.0, None, ALU.add))
            go(V.reciprocal(tb_["w1"], tb_["w2"]))
            go(V.tensor_tensor(tb_["w2"], tb_["ex"], tb_["w1"], ALU.mult))
            go(V.tensor_tensor(oh1, oh1, wide("w1"), ALU.mult))
            go(V.tensor_tensor(oh2, oh2, wide("w2"), ALU.mult))
            gt, rk = r3(tb_["gt"], TB), r3(tb_["rk"], TB)
            V.tensor_tensor(gt[:, :, 0:NE], oh1, oh2, ALU.add)
            V.tensor_tensor(gt[:, :, NE:2 * NE], oh1, oh2, ALU.add)
            dve.wait_ge(r_mm, 2)
            dve.wait_ge(r_sel, 1)
            go(V.scalar_tensor_tensor(out=g2_, in0=r3(psum[:, 5, 0:16], TB), scalar=1.0, in1=sel, op0=ALU.add, op1=ALU.mult))
            V.tensor_scalar(rk[:, :, 0:NE], g2_, -1.0, None, ALU.add)
            V.tensor_scalar(rk[:, :, NE:2 * NE], g2_, -1.0 - P, None, ALU.add)
            A_, B_, O_ = tb_["ova"], tb_["ovb"], tb_["ovc"]
            V.memset(A_, 0.0)
            V.memset(B_, 0.0)
            go(V.memset(tb_["jf"], 0.0))
            go(V.tensor_scalar(O_[:, 4:12], psum[:, 5, 16:24], P + 0.5, None, ALU.is_gt))
            go(V.tensor_copy(A_[:, 4:12], O_[:, 4:12]))
            go(V.tensor_tensor(B_[:, 4:12], A_[:, 4:12], A_[:, 3:11], ALU.add))
            go(V.tensor_tensor(A_[:, 4:12], B_[:, 4:12], B_[:, 2:10], ALU.add))
            go(V.tensor_tensor(B_[:, 4:12], A_[:, 4:12], A_[:, 0:8], ALU.add))
            go(V.tensor_tensor(A_[:, 4:12], B_[:, 4:12], O_[:, 4:12], ALU.mult))
            jf, pick = tb_["jf"], tb_["pick"]
            V.tensor_copy(jf[:, 0:NE], iota8)
            V.tensor_copy(jf[:, 16:16 + NE], iota8)
            go(V.tensor_scalar(jf[:, 12:13], B_[:, 11:12], float(NE), None, ALU.add))
            for i in range(3):
                go(V.scalar_tensor_tensor(out=pick, in0=A_[:, 4:12], scalar=float(i + 1), in1=iota8, op0=ALU.is_equal, op1=ALU.mult))
                go(V.tensor_reduce(jf[:, 24 + i:25 + i], pick, AX.X, ALU.add))
                go(V.tensor_scalar(jf[:, NE + i:NE + i + 1], B_[:, 11:12], i + 0.5, float(NE), ALU.is_gt, ALU.mult))
                go(V.tensor_tensor(jf[:, NE + i:NE + i + 1], jf[:, NE + i:NE + i + 1], jf[:, 24 + i:25 + i], ALU.add))
            V.tensor_copy(jobs[:, :], jf).then_inc(r_jobs, 1)
            dve.wait_ge(r_jobs, 1)
            V.tensor_copy(jobs[:, 31:32], jf[:, 31:32]).then_inc(r_jobs, 1)
            dve.wait_ge(r_jobs, 2)

            def onehot(col_):
                for b in range(TB):
                    r_ = rk[:, b, bass.ds(col_, 1)]
                    g_ = gt[:, b, bass.ds(col_, 1)]
                    V.tensor_scalar(Pm[:, b * P:(b + 1) * P], C("iota"), r_, None, ALU.is_equal)
                    last = V.tensor_scalar(Pg[:, b * P:(b + 1) * P], C("iota"), r_, g_, ALU.is_equal, ALU.mult)
                last.then_inc(m_p, 1)

            def gathered(n):
                for k in range(KT):
                    if k % 4 == 0:
                        dve.wait_ge(m_ga, n + k // 4)
                    last = V.tensor_scalar(XgT[:, k, :], psum[:, 2 + k // 4, (k % 4) * P:(k % 4 + 1) * P],
                                           col("o_norm_ffn", k), None, ALU.mult)
                last.then_inc(m_xg, 1)

            onehot(0)
            gathered(1)
            J = dve.value_load(jobs[0:1, 12:13], min_val=NE, max_val=NE + 3)
            with dve.Fori(0, J) as j:
                for c in range(NEC):
                    dve.wait_ge(m_gu, j * (2 * NEC) + (2 * c + 2))
                    dve.wait_ge(m_sil, j * NEC + (c + 1))
                    V.tensor_tensor(HS[c % 2], SIL[c % 2], psum[:, 2 * (c % 2) + 1, :], ALU.mult).then_inc(m_h, 1)
                    if c == 2:
                        dve.wait_ge(m_pt, j + 1)
                        V.tensor_copy(PgT, psum[:, 7, 0:256]).then_inc(m_pte, 1)
                    if c == 4:
                        nxt = dve.value_load(jobs[0:1, bass.ds(j + 1, 1)], min_val=0, max_val=2 * NE - 1)
                        onehot(nxt)
                gathered(j * 2 + 3)
                for q in range(2):
                    for b in range(TB):
                        dve.wait_ge(m_sc, j * 4 + (2 * q + b + 1))
                        hs = h[:, b, 512 * q:512 * q + 512]
                        V.tensor_tensor(hs, hs, psum[:, 6 * q + b, :], ALU.add).then_inc(s_h, 1)
            norm_dve(dve, 4)
            for b in range(TB):
                dve.wait_ge(n_xn, 9 + b)
                V.tensor_tensor(h[:, b, :], xn3[:, b, :], gain, ALU.mult).then_inc(y_done, 1)

        def moe_pool(pool):
            for b in range(TB):
                pool.wait_ge(y_done, b + 1)
                pool.dma_start(out[0, b * P:(b + 1) * P, :], h[:, b, :]).then_inc(s_out, 16)
            pool.wait_ge(s_out, 32)
        y_done = sem("y_done")



        @block.sync
        def _(sp):
            sp.dma_start(h[:, :, :], I["x"].rearrange("b (n p) d -> p (b n) d", p=P)).then_inc(s_x, 16)
            sp.dma_start(cst[:, :], cst_dram).then_inc(s_cst, 16)
            at = 0
            for group, base in ((COLUMNS, 0), (COLUMNS2, 1)):
                at = 0
                for name, n in group:
                    a = I[name]
                    dims = " ".join("abcd"[:len(a.shape)])
                    flat = a.rearrange(f"{dims} -> ({dims})").rearrange("(r c) -> r c", c=P)
                    sp.dma_start(colsrc[at:at + n, base * P:base * P + P], flat).then_inc(s_colsrc, 16)
                    at += n
            win = I["e_w_in"].rearrange("a (k p) n -> p (a k) n", p=P)
            for k in range(3):
                sp.dma_start(w8(k), win[:, :, 512 * k:512 * k + 512]).then_inc(slot_in[k], 16)
            wout = I["e_w_out"].rearrange("a (k p) n -> p (a k) n", p=P)
            for k in range(2):
                sp.dma_start(w8(3 + k), wout[:, :, 512 * k:512 * k + 512]).then_inc(slot_in[3 + k], 16)
            if not reached(2):
                return
            wg = I["e_ffn_wg"].rearrange("a (k p) f -> p (a k) f", p=P)
            wup = I["e_ffn_wu"].rearrange("a (k p) f -> p (a k) f", p=P)
            wd = I["e_ffn_wd"].rearrange("a (k p) n -> p (a k) n", p=P)
            for c in range(NFC):
                if c == 0:
                    sp.wait_ge(p_in, 8)
                if c == 1:
                    sp.wait_ge(p_in, 10)
                if c == 2:
                    sp.wait_ge(s_wo, 4)
                if c == 3:
                    sp.wait_ge(s_h, 4)
                if c >= 4:
                    sp.wait_ge(f_used, c - 3)
                if c == 4 and reached(3):
                    rwkv_lora_sp(sp)
                k = c % 4
                g, u, d = ffn_slot(k)
                sp.dma_start(g, wg[:, :, FC * c:FC * c + FC]).then_inc(ffn_in[k], 16)
                sp.dma_start(u, wup[:, :, FC * c:FC * c + FC]).then_inc(ffn_in[k], 16)
                sp.dma_start(d, wd[:, 2 * c:2 * c + 2, :]).then_inc(ffn_in[k], 16)
            if reached(3):
                rwkv_sp(sp)
            if reached(4):
                moe_sp(sp)

        @block.scalar
        def _(act):
            bc = lambda name, n: I[name].rearrange("a n -> (a n)").partition_broadcast(P)
            act.dma_start(E_["lng"], bc("e_sgu_ln_g", 512)).then_inc(s_small, 16)
            act.dma_start(E_["lnb"], bc("e_sgu_ln_b", 512)).then_inc(s_small, 16)
            act.dma_start(E_["bias"], I["e_sgu_bias"].rearrange("a h t -> (a h t)").partition_broadcast(P)).then_inc(s_small, 16)
            act.dma_start(r3(E_["ws"], 4), I["e_sgu_ws"].rearrange("a h t s -> t (a h) s")).then_inc(s_small, 16)
            act.dma_start(r3(E_["pw"], 4), I["e_pool_w"].rearrange("a g c d -> c (a g) d")).then_inc(s_small, 16)
            norm_act(act, 0)
            act.wait_ge(cols_done, 1)
            norm_cols(0, "e_norm_mix")[0](act)
            uT = r3(E_["uT"], 4)
            for g in range(4):
                act.wait_ge(p_in, 5 + g)
                nc.scalar.activation(uT[:, g, :], psum[:, 4 + g, 0:T], ACT.Gelu).then_inc(g_ev, 1)
            v = r3(E_["v"], 2)
            for b in range(TB):
                act.wait_ge(p_in, 9 + b)
                nc.scalar.activation(v[:, b, :], psum[:, b, :], ACT.Gelu).then_inc(g_ev, 1)
            act.wait_ge(s_vn, 1)
            nc.scalar.activation(small[:, 32:40], small[:, 24:32], ACT.Sqrt).then_inc(g_ev, 1)
            for g in range(4):
                act.wait_ge(s_ymm, g + 1)
                nc.scalar.activation(mixT[:, g, :], psum[:, 2 + g, 0:T], ACT.Copy, scale=col("e_pool_scale", g)).then_inc(s_yev, 1)
            if not reached(2):
                return
            norm_act(act, 1)
            norm_cols(1, "e_norm_ffn")[0](act)
            for c in range(NFC):
                act.wait_ge(f_gu, 2 * c + 1)
                if c >= 2:
                    act.wait_ge(f_h, c - 1)
                nc.scalar.activation(wu(0, 512, 512 * (c % 2)), psum[:, 4 + 2 * (c % 2), :], ACT.Silu).then_inc(f_sil, 1)
            if reached(3):
                rwkv_act(act)
            if reached(4):
                moe_act(act)

        @block.vector
        def _(dve):
            a, s, t = (r3(E_[x], 4) for x in "ast")
            for x in (a, s, t):
                nc.vector.memset(x[:, :, 0:PAD], 0.0).then_inc(z_pad, 1)
            norm_dve(dve, 0)
            dve.wait_ge(colT, 2)
            nc.vector.tensor_copy(cols[:, :], psum[:, 7, 0:144]).then_inc(cols_done, 1)
            dve.wait_ge(cols_done, 1)
            norm_cols(0, "e_norm_mix")[1](dve)
            for g in range(4):
                dve.wait_ge(p_in, 1 + g)
                nc.vector.tensor_copy(a[:, g, PAD:], psum[:, g, 0:T]).then_inc(a_ev, 1)
            dve.wait_ge(a_ev, 4)
            dve.wait_ge(z_pad, 3)
            n = T + PAD
            link(dve, "dve", nc.vector.tensor_tensor(s[:, :, PAD:], a[:, :, PAD:], a[:, :, PAD - 1:n - 1], ALU.add))
            link(dve, "dve", nc.vector.tensor_tensor(t[:, 1:, PAD:], s[:, 1:, PAD:], s[:, 1:, PAD - 2:n - 2], ALU.add))
            link(dve, "dve", nc.vector.tensor_tensor(s[:, 2:, PAD:], t[:, 2:, PAD:], t[:, 2:, PAD - 4:n - 4], ALU.add))
            link(dve, "dve", nc.vector.tensor_tensor(t[:, 3:, PAD:], s[:, 3:, PAD:], s[:, 3:, PAD - 8:n - 8], ALU.add))
            inv = r3(C("invcnt"), 4)
            for g, src in enumerate((s, t, s, t)):
                last = nc.vector.tensor_tensor(pooled[:, g, :], src[:, g, PAD:], inv[:, g, :], ALU.mult)
            link(dve, "dve", last)
            nc.vector.tensor_tensor(pooled[:, :, :], pooled[:, :, :], a[:, :, PAD:], ALU.subtract).then_inc(s_pooled, 1)
            dve.wait_ge(s_wsT, 1)
            nc.vector.tensor_tensor(r3(E_["wsT"], 4), r3(psum[:, 6, :], 4),
                                    C("upto").unsqueeze(1).to_broadcast([P, 4, P]), ALU.mult).then_inc(s_wsTm, 1)
            dve.wait_ge(g_ev, 6)
            v8, c8, q8 = (r3(E_[x], 8) for x in ("v", "vc", "sq"))

            def per_head(x):
                return x.unsqueeze(2).to_broadcast([P, 8, P])
            link(dve, "dve", nc.vector.tensor_reduce(small[:, 8:16], v8, AX.X, ALU.add))
            link(dve, "dve", nc.vector.tensor_scalar(small[:, 8:16], small[:, 8:16], 1.0 / P, None, ALU.mult))
            link(dve, "dve", nc.vector.tensor_tensor(c8, v8, per_head(small[:, 8:16]), ALU.subtract))
            link(dve, "dve", nc.vector.tensor_tensor(q8, c8, c8, ALU.mult))
            link(dve, "dve", nc.vector.tensor_reduce(small[:, 16:24], q8, AX.X, ALU.add))
            nc.vector.tensor_scalar(small[:, 24:32], small[:, 16:24], 1.0 / P, LN_EPS, ALU.mult, ALU.add).then_inc(s_vn, 1)
            dve.wait_ge(g_ev, 7)
            link(dve, "dve", nc.vector.reciprocal(small[:, 40:48], small[:, 32:40]))
            link(dve, "dve", nc.vector.tensor_tensor(c8, c8, per_head(small[:, 40:48]), ALU.mult))
            c2 = r3(E_["vc"], 2)
            dve.wait_ge(s_small, 80)
            bc = lambda x: x.unsqueeze(1).to_broadcast([P, 2, 512])
            link(dve, "dve", nc.vector.tensor_tensor(c2, c2, bc(E_["lng"]), ALU.mult))
            nc.vector.tensor_tensor(c2, c2, bc(E_["lnb"]), ALU.add).then_inc(s_vn, 1)
            for q in range(2):
                dve.wait_ge(s_mm, q + 1)
                dst = mixT[:, 4 + 2 * q:6 + 2 * q, :].rearrange("p g (n t) -> p g n t", n=2)
                src = psum[:, 6 + q, :].rearrange("p (g n t) -> p g n t", g=2, n=2)
                b4 = r3(E_["bias"], 4)[:, 2 * q:2 * q + 2, :].unsqueeze(2).to_broadcast([P, 2, 2, P])
                link(dve, "dve", nc.vector.tensor_tensor(dst, src, b4, ALU.add))
                nc.vector.tensor_tensor(mixT[:, 4 + 2 * q:6 + 2 * q, :], mixT[:, 4 + 2 * q:6 + 2 * q, :],
                                        r3(E_["uT"], 4)[:, 2 * q:2 * q + 2, :], ALU.mult).then_inc(s_mix, 1)
            add_to_h(dve, s_wo, 0, 0)
            if not reached(2):
                return
            norm_dve(dve, 1)
            norm_cols(1, "e_norm_ffn")[1](dve)
            for c in range(NFC):
                dve.wait_ge(f_gu, 2 * c + 2)
                dve.wait_ge(f_sil, c + 1)
                if c >= 2:
                    dve.wait_ge(f_used, c - 1)
                nc.vector.tensor_tensor(wu(0, 512, 1024 + 512 * (c % 2)), wu(0, 512, 512 * (c % 2)),
                                        psum[:, 5 + 2 * (c % 2), :], ALU.mult).then_inc(f_h, 1)
            add_to_h(dve, f_used, NFC - 1, 0, one=True)
            if reached(3):
                rwkv_dve(dve)
            if reached(4):
                moe_dve(dve)

        @block.tensor
        def _(pe):
            pe.wait_ge(s_cst, 16)
            pe.wait_ge(s_colsrc, 16 * (len(COLUMNS) + len(COLUMNS2)))
            nc.tensor.transpose(psum[:, 7, 0:P], colsrc[:, 0:P], ident).then_inc(colT, 1)
            nc.tensor.transpose(psum[:, 7, P:P + 16], colsrc[0:16, P:2 * P], cst[0:16, 0:16]).then_inc(colT, 1)
            norm_pe(pe, 0)
            norm_ready(pe, 0)
            pe.wait_ge(slot_in[0], 16)
            pe.wait_ge(cols_done, 1)
            for g in range(8):
                if g == 4:
                    pe.wait_ge(slot_in[1], 16)
                for k in range(KT):
                    last = nc.tensor.matmul(psum[:, g, 0:T], w8(g // 4)[:, k, (g % 4) * P:(g % 4 + 1) * P],
                                            xnT[:, k, :], start=(k == 0), stop=(k == KT - 1))
                last.then_inc(p_in, 1)
            pe.wait_ge(slot_in[2], 16)
            for b in range(TB):
                pe.wait_ge(a_ev, b + 1)
                for k in range(KT):
                    last = nc.tensor.matmul(psum[:, b, :], xnT[:, k, b * P:(b + 1) * P], w8(2)[:, k, :],
                                            start=(k == 0), stop=(k == KT - 1))
                last.then_inc(p_in, 1)
            pe.wait_ge(s_small, 80)
            pe.wait_ge(g_ev, 4)
            for g in range(4):
                last = nc.tensor.transpose(psum[:, 6, g * P:(g + 1) * P], r3(E_["ws"], 4)[:, g, :], ident)
            last.then_inc(s_wsT, 1)
            pe.wait_ge(s_pooled, 1)
            pe.wait_ge(a_ev, 4)
            for g in range(4):
                nc.tensor.matmul(psum[:, 2 + g, 0:T], r3(E_["pw"], 4)[:, g, :], pooled[:, g, :],
                                 start=True, stop=True).then_inc(s_ymm, 1)
            pe.wait_ge(s_vn, 2)
            pe.wait_ge(s_wsTm, 1)
            for q in range(2):
                for g in (2 * q, 2 * q + 1):
                    for b in range(TB):
                        o = (g % 2) * T + b * P
                        last = nc.tensor.matmul(psum[:, 6 + q, o:o + P],
                                                E_["vc"][:, b * 512 + g * P:b * 512 + (g + 1) * P],
                                                r3(E_["wsT"], 4)[:, g, :], start=True, stop=True)
                last.then_inc(s_mm, 1)
            pe.wait_ge(slot_in[3], 16)
            pe.wait_ge(slot_in[4], 16)
            pe.wait_ge(s_mix, 2)
            pe.wait_ge(s_yev, 4)
            pe.wait_ge(g_ev, 6)
            rows_product(pe, mixT, lambda q: w8(3 + q), 0, s_wo)
            if not reached(2):
                return
            pe.wait_ge(s_h, 4)
            norm_pe(pe, 1)
            norm_ready(pe, 1)

            def gate_up(c):
                g, u, _ = ffn_slot(c % 4)
                pe.wait_ge(ffn_in[c % 4], 48 * (c // 4 + 1))
                for w, (m, bank) in enumerate(((g, 4), (u, 5))):
                    bank += 2 * (c % 2)
                    if c >= 2:
                        pe.wait_ge(f_sil if w == 0 else f_h, c - 1)
                    for j in range(2):
                        for k in range(KT):
                            last = nc.tensor.matmul(psum[:, bank, j * T:(j + 1) * T], m[:, k, j * P:(j + 1) * P],
                                                    xnT[:, k, :], start=(k == 0), stop=(k == KT - 1))
                    last.then_inc(f_gu, 1)

            def down(c):
                _, _, d = ffn_slot(c % 4)
                pe.wait_ge(f_h, c + 1)
                hid = wu(0, 512, 1024 + 512 * (c % 2))
                for j in range(2):
                    for b in range(TB):
                        for q in range(2):
                            last = nc.tensor.matmul(psum[:, 2 * b + q, :], hid[:, j * T + b * P:j * T + (b + 1) * P],
                                                    d[:, j, 512 * q:512 * q + 512], start=(c == 0 and j == 0),
                                                    stop=(c == NFC - 1 and j == 1))
                last.then_inc(f_used, 1)

            for c in range(NFC + 1):
                if c < NFC:
                    gate_up(c)
                if c >= 1:
                    down(c - 1)
            if reached(3):
                rwkv_pe(pe)
            if reached(4):
                moe_pe(pe)

        @block.gpsimd
        def _(pool):
            if reached(3):
                rwkv_pool(pool)
            if reached(4):
                moe_pool(pool)
            if probe is not None:
                where, s_, v_ = probe(P_)
                pool.wait_ge(s_, v_)
                pool.dma_start(out, where).then_inc(s_dbg, 16)
                pool.wait_ge(s_dbg, 16)


_OUT = (1, T, D)


def kernel(**inputs):
    from concourse import bacc
    from concourse.bass_utils import run_bass_kernel_spmd
    nc = bacc.Bacc("TRN2", target_bir_lowering=False, num_devices=1)
    arrays, aps = {}, {}
    for name, a in inputs.items():
        if a.size:
            a = np.ascontiguousarray(a)
            arrays[name + "_dram"] = a
            aps[name] = nc.dram_tensor(name + "_dram", a.shape, mybir.dt.from_np(a.dtype), kind="ExternalInput").ap()
    arrays["constants_dram"] = constants()
    cst = nc.dram_tensor("constants_dram", (P, CW), F32, kind="ExternalInput").ap()
    out = nc.dram_tensor("out_dram", _OUT, F32, kind="ExternalOutput").ap()
    trunk(nc, aps, cst, out)
    return run_bass_kernel_spmd(nc, [arrays], core_ids=[0]).results[0]["out_dram"]
```

```python
from contextlib import ExitStack

import numpy as np
import concourse.bass as bass
from concourse import mybir

F32 = mybir.dt.float32
FR = mybir.dt.float32r
I32 = mybir.dt.int32
ALU = mybir.AluOpType
ACT = mybir.ActivationFunctionType
AX = mybir.AxisListType

P = 128
D = 1024
KT = D // P
T = 256
TB = T // P
WINDOWS = (2, 4, 8, 16)
PAD = 16
F = 2816
FC = 256
NFC = F // FC
NE = 8
FE = 3584
EC = 512
NEC = FE // EC
HD = 64
SQRT_E_INV = float(np.exp(-0.5))
RMS_EPS, LN_EPS, GN_EPS = 1e-6, 1e-5, 64e-5
LEVELS = (1, 2, 4, 8, 16, 32, 64)

CONST = {}
CW = 0
for _name, _w in (("ident", 128), ("upto", 128), ("before", 128), ("heads", 128), ("iota", 128),
                  ("cum", 256), ("level", 128 * len(LEVELS)), ("invcnt", 4 * T), ("ones", 128)):
    CONST[_name] = (CW, CW + _w)
    CW += _w


def constants():
    s = np.arange(P)[:, None]
    t = np.arange(P)[None, :]
    c = np.zeros((P, CW), np.float32)

    def put(name, v):
        c[:, CONST[name][0]:CONST[name][1]] = v

    put("ident", s == t)
    put("upto", s <= t)
    put("before", s < t)
    put("heads", s // HD == t // HD)
    put("iota", np.broadcast_to(t, (P, P)))
    mid = (s < P // 2).astype(np.float32)
    put("cum", np.concatenate([(s <= t) - mid, (s < t) - mid], 1))
    put("level", np.concatenate([(s // (2 * b) == t // (2 * b)) & (s // b % 2 == 0) & (t // b % 2 == 1)
                                 for b in LEVELS], 1))
    tok = np.arange(T)
    put("invcnt", np.concatenate([np.broadcast_to(1.0 / np.minimum(tok + 1, w), (P, T)) for w in WINDOWS], 1))
    put("ones", 1.0)
    return c


COLUMNS = (("e_norm_mix", 8), ("e_norm_ffn", 8), ("o_norm_mix", 8), ("o_norm_ffn", 8), ("e_pool_scale", 4),
           ("e_sgu_bias", 4), ("o_mu", 48), ("o_w0", 8), ("o_a0", 8), ("o_k_k", 8), ("o_k_a", 8), ("o_r_k", 8))
COLUMNS2 = (("o_lnx_w", 8), ("o_lnx_b", 8))
COL = {}
for _group, _base in ((COLUMNS, 0), (COLUMNS2, 128)):
    for _name, _n in _group:
        COL[_name] = _base
        _base += _n


def trunk(nc, I, cst_dram, out, stop=None, probe=None):
    ctx = ExitStack()
    with ctx:
        def sb(name, shape, dt=F32):
            return ctx.enter_context(nc.sbuf_tensor(name, shape, dt))

        def sem(name):
            return ctx.enter_context(nc.semaphore(name))

        U = 2048
        cst = sb("cst", [P, CW])
        colsrc = sb("colsrc", [P, 256])
        cols = sb("cols", [P, 144])
        h = sb("h", [P, TB, D])
        with nc.sbuf_tensor("x_split", [P, 2, KT, T], FR) as x_split:
            pass
        xn = sb("xn", [P, TB * D])
        xnT = sb("xnT", [P, KT, T])
        with nc.sbuf_tensor("ffn_slots", [P, 12 * U], F32), nc.sbuf_tensor("f_hi", [P, 4, 1024], FR) as f_hi, \
                nc.sbuf_tensor("f_lo", [P, 4, 1024], FR) as f_lo, nc.sbuf_tensor("lora_place", [P, 4 * U], F32), \
                nc.sbuf_tensor("fh_split", [P, 2, 2, 512], FR) as fh_split:
            pass
        ring = sb("ring", [P, 14 * U])
        with nc.sbuf_tensor("w_hi", [P, 4, 1024], FR) as w_hi, nc.sbuf_tensor("w_lo", [P, 4, 1024], FR) as w_lo, \
                nc.sbuf_tensor("xg_split", [P, 2, KT, P], FR) as xg_split, \
                nc.sbuf_tensor("ht_split", [P, 2, 2, 512], FR) as ht_split:
            pass
        work = sb("work", [P, 7 * U])
        small = sb("small", [P, 512])
        psum = ctx.enter_context(nc.psum_tensor("psum", [P, 8, 512], F32))

        def C(name):
            return cst[:, CONST[name][0]:CONST[name][1]]

        def col(name, k, n=1, p=P):
            return cols[0:p, COL[name] + k:COL[name] + k + n]

        def ru(u, w=U, o=0):
            return ring[:, u * U + o:u * U + o + w]

        def wu(u, w=U, o=0):
            return work[:, u * U + o:u * U + o + w]

        def slot(k):
            return ring[:, 2 * U * k:2 * U * (k + 1)]

        def w8(k):
            return slot(k).rearrange("p (k n) -> p k n", k=KT)

        def r3(ap, a):
            return ap.rearrange("p (a b) -> p a b", a=a)

        ident = C("ident")
        xn3 = r3(xn[:, :], TB)

        E_ = {}
        o = 0
        for name, w in (("a", 4 * (T + PAD)), ("s", 4 * (T + PAD)), ("t", 4 * (T + PAD)), ("uT", 4 * T), ("v", 4 * T),
                        ("vc", 4 * T), ("sq", 4 * T), ("lng", 512), ("lnb", 512), ("bias", 512), ("ws", 512),
                        ("wsT", 512), ("pw", 512)):
            E_[name] = work[:, o:o + w]
            o += w
        mixT = ring[:, 10 * U:11 * U].rearrange("p (k t) -> p k t", k=KT)
        pooled = ring[:, 11 * U:11 * U + 4 * T].rearrange("p (g t) -> p g t", g=4)
        assert o <= 7 * U

        s_cst, s_colsrc, s_x, s_small = sem("cst_in"), sem("colsrc_in"), sem("x_in"), sem("small_in")
        slot_in = [sem(f"slot{k}_in") for k in range(7)]
        ffn_in = [sem(f"ffn{k}_in") for k in range(4)]
        cols_done = sem("cols_copied")
        colT = sem("cols_transposed")
        n_ss, n_ms, n_sd, n_xn = sem("norm_squares"), sem("norm_mean"), sem("norm_sqrt"), sem("norm_rows")
        n_r = sem("norm_recip")
        n_tr, n_eva, n_evd = sem("norm_transposed"), sem("norm_cols_act"), sem("norm_cols_dve")
        dvc = sem("dve_chain")
        acc_ = sem("act_chain")
        plc = sem("pool_chain")
        p_in, a_ev, g_ev = sem("in_proj"), sem("pool_in_copied"), sem("gelu_done")
        z_pad = sem("pads_zeroed")
        s_pooled, s_ymm, s_yev = sem("pooled"), sem("pool_mm"), sem("pool_out")
        s_wsT, s_wsTm, s_vn, s_mm, s_mix = sem("ws_transposed"), sem("ws_masked"), sem("v_normed"), sem("mixed"), sem("mix_out")
        s_wo, s_h = sem("out_proj"), sem("h_added")
        f_sil, f_h = sem("ffn_silu"), sem("ffn_hidden")
        f_hh, f_hT = sem("ffn_hidden_hi"), sem("ffn_hidden_split")
        f_phi, f_plo, f_pc = sem("ffn_pieces_hi"), sem("ffn_pieces_split"), sem("ffn_pieces_used")
        s_out = sem("out_written")
        s_dbg = sem("dbg")

        chain = {"dve": 0, "act": 0, "pool": 0}
        CH = {"dve": dvc, "act": acc_, "pool": plc}

        def link(eng, which, ins):
            chain[which] += 1
            ins.then_inc(CH[which], 1)
            eng.wait_ge(CH[which], chain[which])

        def reached(k):
            return stop is None or stop >= k

        def ffn_slot(k):
            b = ring[:, 3 * U * k:3 * U * (k + 1)]
            return (b[:, 0:U].rearrange("p (k f) -> p k f", k=KT), b[:, U:2 * U].rearrange("p (k f) -> p k f", k=KT),
                    b[:, 2 * U:3 * U].rearrange("p (j n) -> p j n", j=2))

        FPIECES = [(w, 0, n) for w in "gu" for n in range(2)]
        for c in range(1, NFC):
            FPIECES += [(w, c - (w == "d"), n) for w in "gud" for n in range(2)]
        FPIECES += [("d", NFC - 1, n) for n in range(2)]
        FAT = {x: i for i, x in enumerate(FPIECES)}
        f_sil_buf = [work[:, 2 * U + 1024 + 512 * i:2 * U + 1536 + 512 * i] for i in range(2)]

        def ffn_piece(what, c, n):
            g, u, d = ffn_slot(c % 4)
            return d[:, n, :] if what == "d" else (g if what == "g" else u)[:, :, n * P:(n + 1) * P]

        def as_piece(w, i, what):
            return w[:, i % 4, :] if what == "d" else w[:, i % 4, :].rearrange("p (k f) -> p k f", k=KT)

        def ffn_split(eng, c):
            eng.wait_ge(f_plo, FAT["d", c, 1] + 1)

        def ffn_product(eng, what, c):
            eng.wait_ge(f_pc, FAT[what, c, 1] + 1)

        P_ = locals()
        block = ctx.enter_context(nc.Block())

        def norm_act(act, i, s_at=None):
            if i == 0:
                act.wait_ge(s_x, 16)
            else:
                act.wait_ge(s_h, H_AT[i] if s_at is None else s_at)
            if i >= 1:
                act.wait_ge(n_tr, 4 * i)
            for b in range(TB):
                nc.scalar.activation(xn3[:, b, :], h[:, b, :], ACT.Square,
                                     accum_out=small[:, b:b + 1]).then_inc(n_ss, 1)
            act.wait_ge(n_ms, i + 1)
            nc.scalar.activation(small[:, 4:6], small[:, 2:4], ACT.Sqrt).then_inc(n_sd, 1)

        def norm_dve(dve, i):
            dve.wait_ge(n_ss, 2 * i + 2)
            nc.vector.tensor_scalar(small[:, 2:4], small[:, 0:2], 1.0 / D, RMS_EPS, ALU.mult, ALU.add).then_inc(n_ms, 1)
            dve.wait_ge(n_sd, i + 1)
            nc.vector.reciprocal(small[:, 6:8], small[:, 4:6]).then_inc(n_r, 1)
            dve.wait_ge(n_r, i + 1)
            for b in range(TB):
                nc.vector.tensor_scalar(xn3[:, b, :], h[:, b, :], small[:, 6 + b:7 + b], None, ALU.mult).then_inc(n_xn, 1)

        def norm_pe(pe, i):
            pe.wait_ge(n_xn, 2 * i + 2)
            for q in range(4):
                for j in range(2):
                    for b in range(TB):
                        k = 2 * q + j
                        last = nc.tensor.transpose(psum[:, q, j * T + b * P:j * T + b * P + P],
                                                   xn3[:, b, k * P:(k + 1) * P], ident)
                last.then_inc(n_tr, 1)

        def norm_cols(i, gain):
            def act_part(act):
                for q in (0, 2):
                    act.wait_ge(n_tr, 4 * i + q + 1)
                    for j in range(2):
                        k = 2 * q + j
                        nc.scalar.activation(xnT[:, k, :], psum[:, q, j * T:j * T + T], ACT.Copy,
                                             scale=col(gain, k)).then_inc(n_eva, 1)

            def dve_part(dve):
                for q in (1, 3):
                    dve.wait_ge(n_tr, 4 * i + q + 1)
                    for j in range(2):
                        k = 2 * q + j
                        nc.vector.tensor_scalar(xnT[:, k, :], psum[:, q, j * T:j * T + T], col(gain, k), None,
                                                ALU.mult).then_inc(n_evd, 1)
            return act_part, dve_part

        def norm_split_act(act):
            for q in range(4):
                act.wait_ge(n_tr, 4 + q + 1)
                for k in (2 * q, 2 * q + 1):
                    last = nc.scalar.activation(x_split[:, 1, k, :], psum[:, q, (k % 2) * T:(k % 2) * T + T], ACT.Copy,
                                                scale=col("e_norm_ffn", k))
                last.then_inc(n_eva, 1)

        def norm_split_dve(dve):
            dve.wait_ge(n_tr, 8)
            for q in range(4):
                dve.wait_ge(n_eva, 4 + q + 1)
                for k in (2 * q, 2 * q + 1):
                    last = nc.vector.scalar_tensor_tensor(
                        out=x_split[:, 0, k, :], in0=psum[:, q, (k % 2) * T:(k % 2) * T + T], scalar=col("e_norm_ffn", k),
                        in1=x_split[:, 1, k, :].bitcast(F32), op0=ALU.mult, op1=ALU.subtract)
                last.then_inc(n_evd, 1)

        def norm_ready(eng, i):
            eng.wait_ge(n_eva, 4 * i + 4)
            eng.wait_ge(n_evd, 4 * i + 4)

        H_AT = {0: 0, 1: 4, 2: 8, 3: 12, 4: 12}

        def add_to_h(dve, ready, base, bank, one=False):
            for q in range(4):
                dve.wait_ge(ready, base + (1 if one else q + 1))
                hs = h[:, q // 2, 512 * (q % 2):512 * (q % 2) + 512]
                nc.vector.tensor_tensor(hs, hs, psum[:, bank + q, :], ALU.add).then_inc(s_h, 1)

        def rows_product(pe, lhs, w, bank, done):
            for b in range(TB):
                for q in range(2):
                    for k in range(KT):
                        last = nc.tensor.matmul(psum[:, bank + 2 * b + q, :], lhs[:, k, b * P:(b + 1) * P],
                                                w(q)[:, k, :], start=(k == 0), stop=(k == KT - 1))
                    last.then_inc(done, 1)

        lora_in, mix_ready, mix_used = sem("lora_in"), sem("mix_ready"), sem("mix_used")
        o_mm, o_act, o_dve = sem("rwkv_product"), sem("rwkv_evac_act"), sem("rwkv_evac_dve")
        ones_row = sem("ones_row")
        k_sq, k_sd, rk_done, v_rows, bk_rows = sem("k_squares"), sem("k_norms"), sem("rk_done"), sem("v_rows"), sem("bk_rows")
        bk_cols = sem("bk_cols")
        ar_done = sem("scan_operands")
        v_tr, bk_tr = sem("v_transposed"), sem("bk_transposed")
        bonus_done = sem("bonus_done")
        a_mm, a_mask, x_seed, x_tr, x_ev = sem("scan_A"), sem("scan_A_masked"), sem("inverse_seed"), sem("inverse_seed_T"), sem("inverse_seed_copied")
        al_done = sem("level_mask")
        lv_y, lv_yc, lv_x, lv_xa = sem("level_Y"), sem("level_Y_copied"), sem("level_X"), sem("level_X_added")
        t_r, t_rc, t_u, t_uc, t_y, t_yc, t_s, t_sc = (sem(x) for x in (
            "R", "R_copied", "U", "U_copied", "Y", "Y_copied", "S", "S_copied"))
        gn_m, gn_c, gn_q, gn_v, gn_ve, gn_sd, gn_o = (sem(x) for x in (
            "gn_mean", "gn_centred", "gn_squares", "gn_var", "gn_var_copied", "gn_sqrt", "gn_out"))
        wo_done = sem("wo_product")

        w1s = wu(2, 512).rearrange("p (k n) -> p k n", k=KT)
        a1s = wu(2, 512, 512).rearrange("p (k n) -> p k n", k=KT)
        g1s = wu(3, 1280).rearrange("p (k n) -> p k n", k=KT)
        w2s, a2s = wu(5, 1024), wu(5, 1024, 1024)
        g2a, g2b = wu(4, 1024), wu(4, 1024, 1024)
        tw, ta, sga, sgb = (ru(13, 256, 256 * i) for i in range(4))
        mix = [r3(wu(0), KT), r3(wu(1), KT)]
        xx = r3(xn[:, :], KT)
        rT, kT, vT, aT = (r3(wu(i), KT) for i in (2, 3, 5, 6))
        gT, Wi, We, Wv = (r3(ru(i), KT) for i in (8, 9, 10, 11))
        v_row = wu(4)
        sig = r3(ru(12), TB)
        kk, tmp = r3(ru(13), KT), r3(ru(12), KT)
        ARf = work[:, 0:2 * U]
        AR = ARf.rearrange("p (k c a t) -> p k c a t", k=KT, c=2, a=2)
        fac = small[:, 64:72]
        omk = small[:, 72:80]
        b_row, k_row = xn[:, 0:1024], xn[:, 1024:2048]
        A_sb = [ru(9).rearrange("p (l m t) -> p l m t", l=4, m=4), ru(10).rearrange("p (l m t) -> p l m t", l=4, m=4)]
        Xs, XTs, Ys = ([r3(ru(11 + q, 512, 512 * i), 4) for q in range(2)] for i in range(3))
        ALs = [[r3(ru(11 + q, 512, 1536), 4), r3(ru(q, 512), 4)] for q in range(2)]
        Rs = [wu(2, 256, 256 * q) for q in range(2)]
        Us = [wu(2, 256, 512 + 256 * q) for q in range(2)]
        ST = wu(2, 512, 1024).rearrange("p (k i) -> p k i", k=KT)
        YT = aT
        sqT = xnT[:, :, :]
        MIX = (1, 4, 5, 0, 2, 3)

        def evacuated(eng, n):
            if n < 16:
                eng.wait_ge(o_act, n + 1)
            elif n < 24:
                eng.wait_ge(o_dve, n - 15)
            elif n < 32:
                eng.wait_ge(o_act, n - 7)
            else:
                eng.wait_ge(o_dve, n - 23)

        def rwkv_lora_sp(sp):
            sp.wait_ge(s_h, 4)
            one = lambda name: I[name].rearrange("a (k p) n -> p (a k) n", p=P)
            two = lambda name: I[name].rearrange("a k n -> (a k) n")
            g2 = two("o_g2")
            for dst, src in ((w1s, one("o_w1")), (a1s, one("o_a1")), (g1s, one("o_g1")), (w2s[0:64, :], two("o_w2")),
                             (w2s[64:65, :], I["o_w0"]), (a2s[0:64, :], two("o_a2")), (g2a, g2[0:P, :]),
                             (g2b[0:32, :], g2[P:160, :])):
                sp.dma_start(dst, src).then_inc(lora_in, 16)

        def rwkv_sp(sp):
            for n, (name, q) in enumerate((("o_wr", 0), ("o_wr", 1), ("o_wk", 0), ("o_wk", 1),
                                           ("o_wv", 0), ("o_wv", 1), ("o_wo", 0), ("o_wo", 1))):
                if n < 4:
                    ffn_split(sp, (8, 9, 9, 10)[n])
                else:
                    sp.wait_ge(o_mm, 32 + 4 * (n - 3))
                w = I[name].rearrange("a (k p) n -> p (a k) n", p=P)
                sp.dma_start(w8(n % 4), w[:, :, 512 * q:512 * q + 512]).then_inc(slot_in[n % 4], 16)

        def rwkv_pe(pe):
            pe.wait_ge(s_h, 8)
            norm_pe(pe, 2)
            norm_ready(pe, 2)
            pe.wait_ge(lora_in, 16 * 8)
            pe.wait_ge(f_h, NFC)

            def product(n, lhs_rhs, rows=P, width=T):
                if n >= 8:
                    evacuated(pe, n - 8)
                for i, (l, r) in enumerate(lhs_rhs):
                    last = nc.tensor.matmul(psum[0:rows, n % 8, 0:width], l, r, start=(i == 0), stop=(i == len(lhs_rhs) - 1))
                last.then_inc(o_mm, 1)
                return last

            def used():
                pass
            pe.wait_ge(mix_ready, 1)
            product(0, [(w1s[:, k, :], mix[0][:, k, :]) for k in range(KT)], 64)
            pe.wait_ge(mix_ready, 2)
            product(1, [(a1s[:, k, :], mix[1][:, k, :]) for k in range(KT)], 64)
            pe.wait_ge(mix_ready, 3)
            product(2, [(g1s[:, k, 0:P], mix[0][:, k, :]) for k in range(KT)])
            product(3, [(g1s[:, k, P:160], mix[0][:, k, :]) for k in range(KT)], 32)
            pe.wait_ge(o_act, 1)
            pe.wait_ge(ones_row, 1)
            for b in range(TB):
                for q in range(2):
                    product(4 + 2 * b + q, [(tw[0:65, b * P:(b + 1) * P], w2s[0:65, 512 * q:512 * q + 512])], width=512)
            pe.wait_ge(o_act, 4)
            for k in range(KT):
                product(8 + k, [(a2s[0:64, k * P:(k + 1) * P], ta[0:64, :])])
            for k in range(KT):
                product(16 + k, [(g2a[:, k * P:(k + 1) * P], sga), (g2b[0:32, k * P:(k + 1) * P], sgb[0:32, :])])
            pe.wait_ge(o_act, 8)
            for k in range(KT):
                evacuated(pe, 16 + k)
                for b in range(TB):
                    last = nc.tensor.matmul(psum[:, k, b * T:(b + 1) * T], sig[:, b, k * P:(k + 1) * P], C("cum"),
                                            start=True, stop=True)
                last.then_inc(o_mm, 1)
            for i in range(3):
                pe.wait_ge(mix_ready, 4 + i)
                for q in range(2):
                    s_ = (2 * i + q) % 4
                    pe.wait_ge(slot_in[s_], 32 + 16 * (i == 2))
                    for m in range(4):
                        product(32 + 8 * i + 4 * q + m,
                                [(w8(s_)[:, k, m * P:(m + 1) * P], mix[(3 + i) % 2][:, k, :]) for k in range(KT)])
            pe.wait_ge(k_sq, 1)
            for k in range(KT):
                evacuated(pe, 48 + k)
                nc.tensor.matmul(psum[:, k, 0:T], C("heads"), sqT[:, k, :], start=True, stop=True).then_inc(o_mm, 1)
            for b in range(TB):
                for q in range(2):
                    n = 2 * b + q
                    pe.wait_ge(k_sd, 8)
                    for j in range(4):
                        last = nc.tensor.transpose(psum[:, n, j * P:(j + 1) * P], vT[:, 4 * q + j, b * P:(b + 1) * P], ident)
                    last.then_inc(v_tr, 1)
            pe.wait_ge(rk_done, 1)
            for k in range(KT):
                if k == 4:
                    pe.wait_ge(v_rows, 4)
                nc.tensor.matmul(psum[:, (4 + k) % 8, 0:T], C("heads"), tmp[:, k, :], start=True, stop=True).then_inc(o_mm, 1)
            pe.wait_ge(bk_cols, 2)
            pe.wait_ge(bonus_done, 8)
            for i, src in enumerate((kk, kT)):
                for q in range(2):
                    for j in range(4):
                        last = nc.tensor.transpose(psum[:, 4 + 2 * i + q, j * P:(j + 1) * P], src[:, 4 * q + j, 0:P], ident)
                    last.then_inc(bk_tr, 1)
            pe.wait_ge(bk_rows, 4)
            pe.wait_ge(ar_done, 2)

            for s_ in range(4):
                c = s_ // 2
                heads_ = [[(2 * (2 * s_ % 4 + q) + l // 2, HD * (l % 2)) for l in range(4)] for q in range(2)]
                for q in range(2):
                    if s_ >= 1:
                        pe.wait_ge(t_yc, 2 * (s_ - 1) + q + 1)
                        if c == 0 or s_ == 2:
                            pe.wait_ge(t_sc, 2 * min(s_ - 1, 1) + q + 1)
                    for l, (k, o) in enumerate(heads_[q]):
                        rhs = AR[o:o + HD, k, c, :, :]
                        nc.tensor.matmul(psum[:, 4 * q + l, 0:T], kk[o:o + HD, k, c * P:(c + 1) * P], rhs, start=True, stop=True)
                        last = nc.tensor.matmul(psum[:, 4 * q + l, T:2 * T], kT[o:o + HD, k, c * P:(c + 1) * P], rhs,
                                                start=True, stop=True)
                    last.then_inc(a_mm, 1)
                for q in range(2):
                    g = 2 * s_ + q
                    pe.wait_ge(x_seed, g + 1)
                    pe.wait_ge(a_mask, g + 1)
                    for l in range(4):
                        last = nc.tensor.transpose(psum[:, 4 * q, l * P:(l + 1) * P], XTs[q][:, l, :], ident)
                    last.then_inc(x_tr, 1)
                for li in range(1, 7):
                    for q in range(2):
                        g = 2 * s_ + q
                        n = 6 * g + li - 1
                        pe.wait_ge(al_done, lev(s_, li, q))
                        if li == 1:
                            pe.wait_ge(x_ev, g + 1)
                        else:
                            pe.wait_ge(lv_xa, lev(s_, li - 1, q))
                        for l in range(4):
                            last = nc.tensor.matmul(psum[:, 4 * q + 1, l * P:(l + 1) * P], ALs[q][li % 2][:, l, :],
                                                    Xs[q][:, l, :], start=True, stop=True)
                        last.then_inc(lv_y, 1)
                    for q in range(2):
                        pe.wait_ge(lv_yc, lev(s_, li, q))
                        for l in range(4):
                            last = nc.tensor.matmul(psum[:, 4 * q + 2, l * P:(l + 1) * P], Ys[q][:, l, :], XTs[q][:, l, :],
                                                    start=True, stop=True)
                        if li < 6:
                            for l in range(4):
                                last = nc.tensor.matmul(psum[:, 4 * q + 3, l * P:(l + 1) * P], XTs[q][:, l, :],
                                                        Ys[q][:, l, :], start=True, stop=True)
                        last.then_inc(lv_x, 1)
                for q in range(2):
                    g = 2 * s_ + q
                    for l, (k, o) in enumerate(heads_[q]):
                        dst = psum[:, 4 * q + 3 * (l % 2), (l // 2) * HD:(l // 2 + 1) * HD]
                        last = nc.tensor.matmul(dst, A_sb[q][:, l, 2, :], v_row[:, c * D + k * P + o:c * D + k * P + o + HD],
                                                start=True, stop=(c == 0))
                        if c == 1:
                            pe.wait_ge(t_sc, 4)
                            last = nc.tensor.matmul(dst, AR[o:o + HD, k, c, 0, :], ST[o:o + HD, k, :], start=False, stop=True)
                    last.then_inc(t_r, 1)
                for q in range(2):
                    g = 2 * s_ + q
                    pe.wait_ge(t_rc, g + 1)
                    pe.wait_ge(lv_xa, lev(s_, 6, q))
                    for l in range(4):
                        last = nc.tensor.matmul(psum[:, 4 * q + 1, l * HD:(l + 1) * HD], XTs[q][:, l, :],
                                                Rs[q][:, l * HD:(l + 1) * HD], start=True, stop=True)
                    last.then_inc(t_u, 1)
                for q in range(2):
                    g = 2 * s_ + q
                    pe.wait_ge(t_uc, g + 1)
                    for l, (k, o) in enumerate(heads_[q]):
                        dst = psum[o:o + HD, 4 * q + 2, (l // 2) * P:(l // 2 + 1) * P]
                        vv = v_row[:, c * D + k * P + o:c * D + k * P + o + HD]
                        uu = Us[q][:, l * HD:(l + 1) * HD]
                        nc.tensor.matmul(dst, uu, A_sb[q][:, l, 1, :], start=True, stop=False)
                        last = nc.tensor.matmul(dst, vv, A_sb[q][:, l, 3, :], start=False, stop=(c == 0))
                        if c == 1:
                            last = nc.tensor.matmul(dst, ST[o:o + HD, k, :], AR[o:o + HD, k, c, 1, :], start=False, stop=True)
                    last.then_inc(t_y, 1)
                    if c == 0:
                        for l, (k, o) in enumerate(heads_[q]):
                            dst = psum[o:o + HD, 4 * q + 3, (l // 2) * HD:(l // 2 + 1) * HD]
                            vv = v_row[:, k * P + o:k * P + o + HD]
                            uu = Us[q][:, l * HD:(l + 1) * HD]
                            nc.tensor.matmul(dst, b_row[:, k * P + o:k * P + o + HD], uu, start=True, stop=False)
                            last = nc.tensor.matmul(dst, k_row[:, k * P + o:k * P + o + HD], vv, start=False, stop=True)
                        last.then_inc(t_s, 1)
            pe.wait_ge(t_yc, 8)
            pe.wait_ge(lv_xa, lev(3, 6, 1))
            for k in range(KT):
                nc.tensor.matmul(psum[:, k, 0:T], C("heads"), YT[:, k, :], start=True, stop=True).then_inc(gn_m, 1)
            pe.wait_ge(gn_q, 1)
            for k in range(KT):
                nc.tensor.matmul(psum[:, k, 0:T], C("heads"), sqT[:, k, :], start=True, stop=True).then_inc(gn_v, 1)
            pe.wait_ge(gn_o, 1)
            for n in (2, 3):
                pe.wait_ge(slot_in[n], 48)
            rows_product(pe, YT, lambda q: w8(2 + q), 0, wo_done)

        def lev(s_, li, q):
            return 12 * s_ + 2 * (li - 1) + q + 1

        def rwkv_act(act):
            norm_act(act, 2)
            norm_cols(2, "o_norm_mix")[0](act)
            for n in range(16):
                act.wait_ge(o_mm, n + 1)
                ps = psum[:, n, :] if n < 8 else psum[:, n - 8, 0:T]
                if n == 0:
                    i_ = nc.scalar.activation(tw[0:64, :], ps[0:64, 0:T], ACT.Tanh)
                elif n == 1:
                    i_ = nc.scalar.activation(ta[0:64, :], ps[0:64, 0:T], ACT.Copy)
                elif n == 2:
                    i_ = nc.scalar.activation(sga, ps[:, 0:T], ACT.Sigmoid)
                elif n == 3:
                    i_ = nc.scalar.activation(sgb[0:32, :], ps[0:32, 0:T], ACT.Sigmoid)
                elif n < 8:
                    i_ = nc.scalar.activation(sig[:, (n - 4) // 2, (n % 2) * 512:(n % 2) * 512 + 512], ps, ACT.Sigmoid)
                else:
                    i_ = nc.scalar.activation(aT[:, n - 8, :], ps, ACT.Sigmoid, bias=col("o_a0", n - 8))
                i_.then_inc(o_act, 1)
            for k in range(KT):
                act.wait_ge(o_mm, 25 + k)
                ps = psum[:, k, :].rearrange("p (b a t) -> p b a t", b=TB, a=2)
                two = lambda x: x[:, k, :].rearrange("p (b t) -> p b t", b=TB)
                nc.scalar.activation(two(Wi), ps[:, :, 0, :], ACT.Exp, scale=-SQRT_E_INV)
                nc.scalar.activation(two(We), ps[:, :, 1, :], ACT.Exp, scale=-SQRT_E_INV)
                nc.scalar.activation(two(Wv), ps[:, :, 0, :], ACT.Exp, scale=SQRT_E_INV).then_inc(o_act, 1)
            for k in range(KT):
                act.wait_ge(o_mm, 57 + k)
                nc.scalar.activation(xx[:, k, :], psum[:, k, 0:T], ACT.Sqrt).then_inc(k_sd, 1)
            for n in range(4):
                act.wait_ge(v_tr, n + 1)
                nc.scalar.activation(v_row[:, 512 * n:512 * n + 512], psum[:, n, :], ACT.Copy).then_inc(v_rows, 1)
            for n in range(4):
                act.wait_ge(bk_tr, n + 1)
                nc.scalar.activation(xn[:, 512 * n:512 * n + 512], psum[:, 4 + n, :], ACT.Copy).then_inc(bk_rows, 1)
            for s_ in range(4):
                c = s_ // 2
                for q in range(2):
                    act.wait_ge(x_tr, 2 * s_ + q + 1)
                    if s_ >= 1:
                        act.wait_ge(lv_x, lev(s_ - 1, 6, q))
                    nc.scalar.activation(Xs[q], r3(psum[:, 4 * q, :], 4), ACT.Copy).then_inc(x_ev, 1)
                for li in range(1, 7):
                    for q in range(2):
                        act.wait_ge(lv_y, lev(s_, li, q))
                        nc.scalar.activation(Ys[q], r3(psum[:, 4 * q + 1, :], 4), ACT.Copy).then_inc(lv_yc, 1)
                for q in range(2):
                    act.wait_ge(t_r, 2 * s_ + q + 1)
                    for e in range(2):
                        last = nc.scalar.activation(Rs[q].rearrange("p (j e i) -> p e j i", j=2, e=2)[:, e],
                                                    r3(psum[:, 4 * q + 3 * e, 0:2 * HD], 2), ACT.Copy)
                    last.then_inc(t_rc, 1)
                for q in range(2):
                    act.wait_ge(t_y, 2 * s_ + q + 1)
                    k = 2 * (2 * s_ % 4 + q)
                    nc.scalar.activation(YT[:, k:k + 2, c * P:(c + 1) * P], r3(psum[:, 4 * q + 2, 0:256], 2),
                                         ACT.Copy).then_inc(t_yc, 1)
            act.wait_ge(gn_c, 8)
            nc.scalar.activation(sqT, YT, ACT.Square).then_inc(gn_q, 1)
            act.wait_ge(gn_ve, 8)
            nc.scalar.activation(tmp, tmp, ACT.Sqrt).then_inc(gn_sd, 1)

        def rwkv_dve(dve):
            norm_dve(dve, 2)
            norm_cols(2, "o_norm_mix")[1](dve)
            nc.vector.tensor_scalar(omk, col("o_k_a", 0, 8), -1.0, 1.0, ALU.mult, ALU.add)
            nc.vector.memset(tw[64:65, :], 1.0).then_inc(ones_row, 1)
            norm_ready(dve, 2)
            nc.vector.tensor_tensor(xx[:, :, 1:], xnT[:, :, 0:T - 1], xnT[:, :, 1:], ALU.subtract)
            link(dve, "dve", nc.vector.tensor_scalar(xx[:, :, 0:1], xnT[:, :, 0:1], -1.0, None, ALU.mult))
            ffn_product(dve, "d", NFC - 1)

            def mixed(j):
                if j >= 2:
                    dve.wait_ge(o_mm, (1, 2, 4, 40)[j - 2] if j < 5 else 40)
                for k in range(KT):
                    last = nc.vector.scalar_tensor_tensor(out=mix[j % 2][:, k, :], in0=xx[:, k, :],
                                                          scalar=col("o_mu", 8 * MIX[j] + k), in1=xnT[:, k, :],
                                                          op0=ALU.mult, op1=ALU.add)
                last.then_inc(mix_ready, 1)

            def copies(dst, n0):
                for k in range(KT):
                    dve.wait_ge(o_mm, n0 + k + 1)
                    nc.vector.tensor_copy(dst[:, k, :], psum[:, k, 0:T]).then_inc(o_dve, 1)

            for j in range(5):
                mixed(j)
            copies(gT, 16)
            copies(rT, 32)
            mixed(5)
            copies(kT, 40)
            dve.wait_ge(o_dve, 24)
            for k in range(KT):
                last = nc.vector.tensor_scalar(kk[:, k, :], kT[:, k, :], col("o_k_k", k), None, ALU.mult)
            link(dve, "dve", last)
            nc.vector.tensor_tensor(sqT, kk, kk, ALU.mult).then_inc(k_sq, 1)
            copies(vT, 48)
            dve.wait_ge(o_act, 24)
            for k in range(KT):
                last = nc.vector.tensor_scalar(tmp[:, k, :], aT[:, k, :], col("o_k_a", k), omk[:, k:k + 1], ALU.mult, ALU.add)
            link(dve, "dve", last)
            link(dve, "dve", nc.vector.tensor_tensor(kT, kT, tmp, ALU.mult))
            for k in range(KT):
                last = nc.vector.scalar_tensor_tensor(out=tmp[:, k, :], in0=rT[:, k, :], scalar=col("o_r_k", k),
                                                      in1=kT[:, k, :], op0=ALU.mult, op1=ALU.mult)
            last.then_inc(rk_done, 1)
            dve.wait_ge(k_sd, 8)
            link(dve, "dve", nc.vector.tensor_scalar(xx, xx, 1e-12, None, ALU.max))
            link(dve, "dve", nc.vector.reciprocal(xx, xx))
            link(dve, "dve", nc.vector.tensor_tensor(kk, kk, xx, ALU.mult))
            kct = lambda x: x.rearrange("p k (c t) -> p k c t", c=2)
            for c in range(2):
                sl = slice(c * P, (c + 1) * P)
                last = nc.vector.scalar_tensor_tensor(out=AR[:, :, c, 0, :], in0=kk[:, :, sl], scalar=-1.0,
                                                      in1=We[:, :, sl], op0=ALU.mult, op1=ALU.mult)
            link(dve, "dve", last)
            link(dve, "dve", nc.vector.tensor_tensor(kk, kk, aT, ALU.mult))
            nc.vector.tensor_tensor(kk, kk, Wv, ALU.mult).then_inc(bk_cols, 1)
            dve.wait_ge(v_tr, 4)
            for k in range(KT):
                dve.wait_ge(o_mm, 65 + k)
                nc.vector.tensor_tensor(vT[:, k, :], vT[:, k, :], psum[:, (4 + k) % 8, 0:T], ALU.mult).then_inc(bonus_done, 1)
            dve.wait_ge(rk_done, 1)
            nc.vector.tensor_tensor(kT, kT, Wv, ALU.mult).then_inc(bk_cols, 1)
            for c in range(2):
                sl = slice(c * P, (c + 1) * P)
                nc.vector.tensor_tensor(AR[:, :, c, 1, :], rT[:, :, sl], Wi[:, :, sl], ALU.mult).then_inc(ar_done, 1)
            link(dve, "dve", nc.vector.reciprocal(fac, We[:, :, P]))
            link(dve, "dve", nc.vector.tensor_tensor(fac, fac, Wi[:, :, P - 1], ALU.mult))
            dve.wait_ge(ar_done, 2)
            mask = cst[:, CONST["upto"][0]:CONST["before"][1]]
            for s_ in range(4):
                c = s_ // 2
                for q in range(2):
                    g = 2 * s_ + q
                    dve.wait_ge(a_mm, g + 1)
                    if s_ >= 1:
                        dve.wait_ge(al_done, lev(s_ - 1, 6, q))
                        dve.wait_ge(t_y, 2 * (s_ - 1) + q + 1)
                    for l in range(4):
                        for m, name in ((0, "before"), (1, "upto")):
                            src = psum[:, 4 * q + l, :].rearrange("p (a m t) -> p a m t", a=2, m=2)[:, :, m, :]
                            dst = A_sb[q][:, l, :, :].rearrange("p (a m) t -> p a m t", a=2)[:, :, m, :]
                            last = nc.vector.tensor_tensor(dst, src, C(name).unsqueeze(1).to_broadcast([P, 2, P]), ALU.mult)
                    last.then_inc(a_mask, 1)
                    dve.wait_ge(a_mask, g + 1)
                    four = lambda x: x.unsqueeze(1).to_broadcast([P, 4, P])
                    lv = C("level")[:, 0:P]
                    if s_ >= 1:
                        dve.wait_ge(t_u, 2 * (s_ - 1) + q + 1)
                    link(dve, "dve", nc.vector.tensor_tensor(XTs[q], A_sb[q][:, :, 0, :], four(lv), ALU.mult))
                    nc.vector.tensor_tensor(XTs[q], XTs[q], four(ident), ALU.add).then_inc(x_seed, 1)
                for li in range(1, 7):
                    for q in range(2):
                        dve.wait_ge(lv_x, lev(s_, li, q))
                        if li < 6:
                            nc.vector.tensor_tensor(Xs[q], Xs[q], r3(psum[:, 4 * q + 3, :], 4), ALU.add)
                        nc.vector.tensor_tensor(XTs[q], XTs[q], r3(psum[:, 4 * q + 2, :], 4), ALU.add).then_inc(lv_xa, 1)
                for q in range(2):
                    g = 2 * s_ + q
                    dve.wait_ge(t_u, g + 1)
                    nc.vector.tensor_copy(Us[q], psum[:, 4 * q + 1, 0:256]).then_inc(t_uc, 1)
                if c == 0:
                    for q in range(2):
                        g = 2 * s_ + q
                        dve.wait_ge(t_s, g + 1)
                        for j in range(2):
                            k = 2 * (2 * s_ % 4 + q) + j
                            last = nc.vector.tensor_scalar(ST[:, k, :], psum[:, 4 * q + 3, j * HD:(j + 1) * HD],
                                                           fac[:, k:k + 1], None, ALU.mult)
                        last.then_inc(t_sc, 1)
            for k in range(KT):
                dve.wait_ge(gn_m, k + 1)
                nc.vector.scalar_tensor_tensor(out=YT[:, k, :], in0=psum[:, k, 0:T], scalar=-1.0 / HD, in1=YT[:, k, :],
                                               op0=ALU.mult, op1=ALU.add).then_inc(gn_c, 1)
            for k in range(KT):
                dve.wait_ge(gn_v, k + 1)
                nc.vector.tensor_scalar(tmp[:, k, :], psum[:, k, 0:T], 1.0 / HD, GN_EPS, ALU.mult, ALU.add).then_inc(gn_ve, 1)
            dve.wait_ge(gn_sd, 1)
            link(dve, "dve", nc.vector.reciprocal(tmp, tmp))
            link(dve, "dve", nc.vector.tensor_tensor(YT, YT, tmp, ALU.mult))
            for k in range(KT):
                last = nc.vector.tensor_scalar(YT[:, k, :], YT[:, k, :], col("o_lnx_w", k), col("o_lnx_b", k), ALU.mult, ALU.add)
            link(dve, "dve", last)
            link(dve, "dve", nc.vector.tensor_tensor(YT, YT, vT, ALU.add))
            nc.vector.tensor_tensor(YT, YT, gT, ALU.mult).then_inc(gn_o, 1)
            add_to_h(dve, wo_done, 0, 0)

        def rwkv_pool(pool):
            for s_ in range(4):
                for li in range(1, 7):
                    for q in range(2):
                        if li == 1:
                            pool.wait_ge(a_mask, 2 * s_ + q + 1)
                        if li >= 3:
                            pool.wait_ge(lv_y, lev(s_, li - 2, q))
                        elif s_ >= 1:
                            pool.wait_ge(lv_y, lev(s_ - 1, li + 4, q))
                        m = C("level")[:, li * P:(li + 1) * P].unsqueeze(1).to_broadcast([P, 4, P])
                        nc.gpsimd.tensor_tensor(ALs[q][li % 2], A_sb[q][:, :, 0, :], m, ALU.mult).then_inc(al_done, 1)
        r_in, r_mm, r_lg, r_ex, r_exd, r_sel, r_rank, r_jobs = (sem(x) for x in (
            "router_in", "router_product", "logits", "gate_exp_in", "gate_exp", "selected", "ranks", "jobs_ready"))
        m_hi, m_lo, m_pc = sem("pieces_hi"), sem("pieces_split"), sem("pieces_used")
        m_zero = sem("outputs_zeroed")
        m_xf, m_xh, m_hh = sem("gathered_full"), sem("gathered_hi"), sem("expert_hidden_hi")
        m_sil, m_h, m_T, m_hT = (sem(x) for x in ("expert_silu", "expert_hidden", "expert_hidden_T", "expert_hidden_cols"))
        m_p, m_pt, m_pte, m_ga, m_xg, m_yc, m_sc = (sem(x) for x in (
            "onehot_ready", "gates_transposed", "gates_copied", "gathered", "gathered_split", "expert_out_copied",
            "scattered"))
        jobs = sb("jobs", [P, 32], I32)
        spare = xnT[:, :, :].rearrange("p k t -> p (k t)")
        Pm, Pg, PgT = spare[:, 0:256], spare[:, 256:512], spare[:, 512:768]
        XG = spare[:, 768:1792]
        SIL = [wu(6, 512, 512 * i) for i in range(2)]
        Ysb = wu(6, 1024, 1024)
        HT = [[ht_split[:, i, w, :] for w in range(2)] for i in range(2)]
        gain = C("invcnt")
        tb_ = {}
        o = 128
        for name, w in (("rw", 64), ("L", 16), ("L2", 16), ("m1", 2), ("m2", 2), ("i1", 2), ("i2", 2), ("eq", 16), ("oh1", 16),
                        ("oh2", 16), ("ex", 2), ("w1", 2), ("w2", 2), ("g2", 16), ("sel", 16), ("rk", 32), ("gt", 32),
                        ("ova", 12), ("ovb", 12), ("ovc", 12), ("pick", 8), ("jf", 32), ("d", 2)):
            tb_[name] = small[:, o:o + w]
            o += w
        assert o <= 512
        router = tb_["rw"].rearrange("p (k e) -> p k e", k=KT)

        LOADS = [("g", 0), ("u", 0)]
        for c in range(1, NEC):
            LOADS += [("g", c), ("u", c), ("d", c - 1)]
        LOADS += [("d", NEC - 1)]
        NL = len(LOADS)
        assert NL % 7 == 0
        AT = {x: i for i, x in enumerate(LOADS)}
        LANDED = (48, 48, 48, 48, 16, 0, 0)
        SLOTS = (1, 0, 5, 6, 4, 2, 3)

        NP = 4 * NL

        def loaded(eng, j, i):
            k = SLOTS[i % 7]
            eng.wait_ge(slot_in[k], LANDED[k] + 16 * (i // 7 + 1) + j * (16 * NL // 7))

        def piece(i, n):
            return slot(SLOTS[i % 7])[:, 1024 * n:1024 * n + 1024]

        def consumed(eng, j, x):
            eng.wait_ge(m_pc, j * NP + (4 + 4 * AT[x] + 4))

        def moe_sp(sp):
            sp.wait_ge(o_mm, 56)
            sp.dma_start(router, I["o_router"].rearrange("a (k p) e -> p (a k) e", p=P)).then_inc(r_in, 16)
            sp.dma_start(gain, I["final_norm"].partition_broadcast(P)).then_inc(r_in, 16)
            wg = I["o_moe_wg"].rearrange("a e (k p) f -> (a e) p k f", p=P)
            wup = I["o_moe_wu"].rearrange("a e (k p) f -> (a e) p k f", p=P)
            wd = I["o_moe_wd"].rearrange("a e (k p) n -> (a e) p k n", p=P)

            def load(i, e):
                what, c = LOADS[i]
                if what == "d":
                    src = wd[bass.ds(e, 1), :, 4 * c:4 * c + 4, :]
                    dst = slot(SLOTS[i % 7]).rearrange("p (k n) -> p k n", k=4)
                else:
                    src = (wg if what == "g" else wup)[bass.ds(e, 1), :, :, EC * c:EC * c + EC]
                    dst = w8(SLOTS[i % 7])
                sp.dma_start(dst, src.rearrange("o p k n -> (o p) k n")).then_inc(slot_in[SLOTS[i % 7]], 16)

            def free(i, j):
                sp.wait_ge(m_lo, j * NP + 4 * (i + 1))

            for i in range(NL):
                if i == 1:
                    sp.wait_ge(lv_y, lev(3, 6, 1))
                if i == 2:
                    sp.wait_ge(t_yc, 8)
                if i == 3:
                    sp.wait_ge(gn_o, 1)
                if i == 5:
                    sp.wait_ge(wo_done, 4)
                if i >= 7:
                    free(i - 7, 0)
                load(i, 0)
            sp.wait_ge(r_jobs, 2)
            J = sp.value_load(jobs[0:1, 12:13], min_val=NE, max_val=NE + 3)
            with sp.Fori(1, J) as j:
                e = sp.value_load(jobs[0:1, bass.ds(j + 16, 1)], min_val=0, max_val=NE - 1)
                for i in range(NL):
                    free(i - 7, j)
                    load(i, e)

        def gather(pe, q):
            for kk_ in range(4):
                k = 4 * q + kk_
                for b in range(TB):
                    last = nc.tensor.matmul(psum[:, 2 + q, kk_ * P:(kk_ + 1) * P], xn3[:, b, k * P:(k + 1) * P],
                                            Pm[:, b * P:(b + 1) * P], start=(b == 0), stop=(b == TB - 1))
            last.then_inc(m_ga, 1)

        def moe_pe(pe):
            pe.wait_ge(s_h, 12)
            norm_pe(pe, 3)
            norm_ready(pe, 3)
            pe.wait_ge(r_in, 32)
            for b in range(TB):
                for k in range(KT):
                    last = nc.tensor.matmul(psum[:, 4, 8 * b:8 * b + 8], xnT[:, k, b * P:(b + 1) * P], router[:, k, :],
                                            start=(k == 0), stop=(k == KT - 1))
            last.then_inc(r_mm, 1)
            pe.wait_ge(r_sel, 1)
            sel = r3(tb_["sel"], TB)
            nc.tensor.matmul(psum[:, 5, 0:8], C("before"), sel[:, 0, :], start=True, stop=True).then_inc(m_pc, 1)
            nc.tensor.matmul(psum[:, 5, 8:16], C("before"), sel[:, 1, :], start=True, stop=False).then_inc(m_pc, 1)
            nc.tensor.matmul(psum[:, 5, 8:16], C("ones"), sel[:, 0, :], start=False, stop=True).then_inc(m_pc, 1)
            nc.tensor.matmul(psum[:, 5, 16:24], C("ones"), sel[:, 0, :], start=True, stop=False).then_inc(m_pc, 1)
            nc.tensor.matmul(psum[:, 5, 16:24], C("ones"), sel[:, 1, :], start=False, stop=True).then_inc(r_mm, 1)
            pe.wait_ge(m_p, 1)
            for q in range(2):
                gather(pe, q)

            def three(dst, x_hi, x_lo, n, first, last_):
                hi, lo = n
                nc.tensor.matmul(dst, x_hi, hi, start=first, stop=False)
                nc.tensor.matmul(dst, x_lo, hi, start=False, stop=False)
                return nc.tensor.matmul(dst, x_hi, lo, start=False, stop=last_)

            def hidden(j, x, c):
                i = AT["gu"[x], c]
                for n in range(4):
                    pe.wait_ge(m_lo, j * NP + (4 * i + n + 1))
                    for m in range(2):
                        k = 2 * n + m
                        last = three(psum[:, 2 * (c % 2) + x, :], xg_split[:, 0, k, :], xg_split[:, 1, k, :],
                                     [w[:, (4 * i + n) % 4, 512 * m:512 * m + 512] for w in (w_hi, w_lo)], k == 0, k == KT - 1)
                    last.then_inc(m_pc, 1)

            def turned(j, c):
                pe.wait_ge(m_h, j * NEC + (c + 1))
                for f in range(4):
                    last = nc.tensor.transpose(psum[:, 6, f * P:(f + 1) * P], SIL[c % 2][:, f * P:(f + 1) * P], ident)
                last.then_inc(m_T, 1)

            def down(j, c):
                i = AT["d", c]
                pe.wait_ge(m_hT, j * NEC + (c + 1))
                for f in range(4):
                    pe.wait_ge(m_lo, j * NP + (4 * i + f + 1))
                    for q in range(2):
                        last = three(psum[:, 4 + q, :], HT[c % 2][0][:, f * P:(f + 1) * P], HT[c % 2][1][:, f * P:(f + 1) * P],
                                     [w[:, (4 * i + f) % 4, 512 * q:512 * q + 512] for w in (w_hi, w_lo)],
                                     c == 0 and f == 0, c == NEC - 1 and f == 3)
                    last.then_inc(m_pc, 1)

            def scattered(j):
                pe.wait_ge(m_pte, j + 1)
                for q in range(2):
                    pe.wait_ge(m_yc, j * 2 + 2)
                    for b in range(TB):
                        nc.tensor.matmul(psum[:, 6 - 2 * q + b, :], PgT[:, b * P:(b + 1) * P],
                                         Ysb[:, 512 * q:512 * q + 512], start=True, stop=True).then_inc(m_sc, 1)

            pe.wait_ge(r_jobs, 2)
            J = pe.value_load(jobs[0:1, 12:13], min_val=NE, max_val=NE + 3)
            with pe.Fori(0, J) as j:
                pe.wait_ge(m_xg, j + 1)
                for c in range(NEC):
                    hidden(j, 0, c)
                    if c == 0:
                        scattered(j)
                    if c == 1:
                        pe.wait_ge(s_h, j * 4 + 16)
                        for b in range(TB):
                            last = nc.tensor.transpose(psum[:, 7, b * P:(b + 1) * P], Pg[:, b * P:(b + 1) * P], ident)
                        last.then_inc(m_pt, 1)
                    if c >= 1:
                        turned(j, c - 1)
                    hidden(j, 1, c)
                    if c >= 1:
                        down(j, c - 1)
                turned(j, NEC - 1)
                pe.wait_ge(m_p, j + 2)
                gather(pe, 0)
                gather(pe, 1)
                down(j, NEC - 1)
            scattered(J)

        def moe_act(act):
            norm_act(act, 3)
            norm_cols(3, "o_norm_ffn")[0](act)
            act.wait_ge(r_ex, 1)
            nc.scalar.activation(tb_["ex"], tb_["d"], ACT.Exp).then_inc(r_exd, 1)
            act.wait_ge(r_jobs, 2)
            J = act.value_load(jobs[0:1, 12:13], min_val=NE, max_val=NE + 3)
            act.wait_ge(m_xf, 1)
            nc.scalar.activation(xg_split[:, 0, :, :], r3(XG, KT), ACT.Copy).then_inc(m_xh, 1)

            def outputs(j):
                act.wait_ge(m_pc, j * NP + 4)
                for q in range(2):
                    nc.scalar.activation(Ysb[:, 512 * q:512 * q + 512], psum[:, 4 + q, :], ACT.Copy).then_inc(m_yc, 1)

            act.wait_ge(m_zero, 1)
            with act.Fori(0, J) as j:
                def turned(c):
                    act.wait_ge(m_T, j * NEC + (c + 1))
                    nc.scalar.activation(HT[c % 2][0], psum[:, 6, :], ACT.Copy).then_inc(m_hh, 1)
                for i, (what, c) in enumerate(LOADS):
                    loaded(act, j, i)
                    for n in range(4):
                        act.wait_ge(m_pc, j * NP + (4 * i + n + 1))
                        nc.scalar.activation(w_hi[:, (4 * i + n) % 4, :], piece(i, n), ACT.Copy).then_inc(m_hi, 1)
                    if i == 0:
                        outputs(j)
                    if what == "u":
                        consumed(act, j, ("g", c))
                        nc.scalar.activation(SIL[c % 2], psum[:, 2 * (c % 2), :], ACT.Silu).then_inc(m_sil, 1)
                        if c >= 1:
                            turned(c - 1)
                turned(NEC - 1)
                act.wait_ge(m_xf, j + 2)
                nc.scalar.activation(xg_split[:, 0, :, :], r3(XG, KT), ACT.Copy).then_inc(m_xh, 1)
            outputs(J)
            norm_act(act, 4, s_at=J * 4 + 16)

        def moe_dve(dve):
            norm_dve(dve, 3)
            norm_cols(3, "o_norm_ffn")[1](dve)
            L, L2, eq, oh1, oh2, g2_, sel = (r3(tb_[x], TB) for x in ("L", "L2", "eq", "oh1", "oh2", "g2", "sel"))
            wide = lambda x: tb_[x].unsqueeze(2).to_broadcast([P, TB, NE])
            iota8 = C("iota")[:, 0:NE]
            io = iota8.unsqueeze(1).to_broadcast([P, TB, NE])
            go = lambda ins: link(dve, "dve", ins)
            V = nc.vector
            dve.wait_ge(r_mm, 1)
            go(V.tensor_copy(L, r3(psum[:, 4, 0:16], TB)))
            go(V.tensor_reduce(tb_["m1"], L, AX.X, ALU.max))
            go(V.tensor_tensor(eq, L, wide("m1"), ALU.is_equal))
            go(V.scalar_tensor_tensor(out=eq, in0=eq, scalar=-float(NE), in1=io, op0=ALU.mult, op1=ALU.add))
            go(V.tensor_reduce(tb_["i1"], eq, AX.X, ALU.min))
            go(V.tensor_tensor(oh1, eq, wide("i1"), ALU.is_equal))
            go(V.scalar_tensor_tensor(out=L2, in0=oh1, scalar=-1e30, in1=L, op0=ALU.mult, op1=ALU.add))
            go(V.tensor_reduce(tb_["m2"], L2, AX.X, ALU.max))
            go(V.tensor_tensor(eq, L2, wide("m2"), ALU.is_equal))
            go(V.scalar_tensor_tensor(out=eq, in0=eq, scalar=-float(NE), in1=io, op0=ALU.mult, op1=ALU.add))
            go(V.tensor_reduce(tb_["i2"], eq, AX.X, ALU.min))
            go(V.tensor_tensor(oh2, eq, wide("i2"), ALU.is_equal))
            V.tensor_tensor(tb_["d"], tb_["m2"], tb_["m1"], ALU.subtract).then_inc(r_ex, 1)
            V.tensor_tensor(sel, oh1, oh2, ALU.add).then_inc(r_sel, 1)
            dve.wait_ge(r_exd, 1)
            go(V.tensor_scalar(tb_["w2"], tb_["ex"], 1.0, None, ALU.add))
            go(V.reciprocal(tb_["w1"], tb_["w2"]))
            go(V.tensor_tensor(tb_["w2"], tb_["ex"], tb_["w1"], ALU.mult))
            go(V.tensor_tensor(oh1, oh1, wide("w1"), ALU.mult))
            go(V.tensor_tensor(oh2, oh2, wide("w2"), ALU.mult))
            gt, rk = r3(tb_["gt"], TB), r3(tb_["rk"], TB)
            V.tensor_tensor(gt[:, :, 0:NE], oh1, oh2, ALU.add)
            V.tensor_tensor(gt[:, :, NE:2 * NE], oh1, oh2, ALU.add)
            dve.wait_ge(r_mm, 2)
            dve.wait_ge(r_sel, 1)
            go(V.scalar_tensor_tensor(out=g2_, in0=r3(psum[:, 5, 0:16], TB), scalar=1.0, in1=sel, op0=ALU.add, op1=ALU.mult))
            V.tensor_scalar(rk[:, :, 0:NE], g2_, -1.0, None, ALU.add)
            V.tensor_scalar(rk[:, :, NE:2 * NE], g2_, -1.0 - P, None, ALU.add)
            A_, B_, O_ = tb_["ova"], tb_["ovb"], tb_["ovc"]
            V.memset(A_, 0.0)
            V.memset(B_, 0.0)
            go(V.memset(tb_["jf"], 0.0))
            go(V.tensor_scalar(O_[:, 4:12], psum[:, 5, 16:24], P + 0.5, None, ALU.is_gt))
            go(V.tensor_copy(A_[:, 4:12], O_[:, 4:12]))
            go(V.tensor_tensor(B_[:, 4:12], A_[:, 4:12], A_[:, 3:11], ALU.add))
            go(V.tensor_tensor(A_[:, 4:12], B_[:, 4:12], B_[:, 2:10], ALU.add))
            go(V.tensor_tensor(B_[:, 4:12], A_[:, 4:12], A_[:, 0:8], ALU.add))
            go(V.tensor_tensor(A_[:, 4:12], B_[:, 4:12], O_[:, 4:12], ALU.mult))
            jf, pick = tb_["jf"], tb_["pick"]
            V.tensor_copy(jf[:, 0:NE], iota8)
            V.tensor_copy(jf[:, 16:16 + NE], iota8)
            go(V.tensor_scalar(jf[:, 12:13], B_[:, 11:12], float(NE), None, ALU.add))
            for i in range(3):
                go(V.scalar_tensor_tensor(out=pick, in0=A_[:, 4:12], scalar=float(i + 1), in1=iota8, op0=ALU.is_equal, op1=ALU.mult))
                go(V.tensor_reduce(jf[:, 24 + i:25 + i], pick, AX.X, ALU.add))
                go(V.tensor_scalar(jf[:, NE + i:NE + i + 1], B_[:, 11:12], i + 0.5, float(NE), ALU.is_gt, ALU.mult))
                go(V.tensor_tensor(jf[:, NE + i:NE + i + 1], jf[:, NE + i:NE + i + 1], jf[:, 24 + i:25 + i], ALU.add))
            V.tensor_copy(jobs[:, :], jf).then_inc(r_jobs, 1)
            dve.wait_ge(r_jobs, 1)
            V.tensor_copy(jobs[:, 31:32], jf[:, 31:32]).then_inc(r_jobs, 1)
            dve.wait_ge(r_jobs, 2)

            def onehot(col_):
                for b in range(TB):
                    r_ = rk[:, b, bass.ds(col_, 1)]
                    g_ = gt[:, b, bass.ds(col_, 1)]
                    V.tensor_scalar(Pm[:, b * P:(b + 1) * P], C("iota"), r_, None, ALU.is_equal)
                    last = V.tensor_scalar(Pg[:, b * P:(b + 1) * P], C("iota"), r_, g_, ALU.is_equal, ALU.mult)
                last.then_inc(m_p, 1)

            def gathered(n, job):
                for k in range(KT):
                    if k % 4 == 0:
                        dve.wait_ge(m_ga, n + k // 4)
                    last = V.tensor_scalar(XG[:, k * P:(k + 1) * P], psum[:, 2 + k // 4, (k % 4) * P:(k % 4 + 1) * P],
                                           col("o_norm_ffn", k), None, ALU.mult)
                last.then_inc(m_xf, 1)
                dve.wait_ge(m_xh, job)
                V.tensor_tensor(xg_split[:, 1, :, :], r3(XG, KT), xg_split[:, 0, :, :].bitcast(F32),
                                ALU.subtract).then_inc(m_xg, 1)

            def scattered(j):
                for q in range(2):
                    for b in range(TB):
                        dve.wait_ge(m_sc, j * 4 + (2 * q + b + 1))
                        hs = h[:, b, 512 * q:512 * q + 512]
                        V.tensor_tensor(hs, hs, psum[:, 6 - 2 * q + b, :], ALU.add).then_inc(s_h, 1)

            onehot(0)
            gathered(1, 1)
            V.memset(PgT, 0.0).then_inc(m_pte, 1)
            for q in range(2):
                last = V.memset(psum[:, 4 + q, :], 0.0)
            last.then_inc(m_zero, 1)
            J = dve.value_load(jobs[0:1, 12:13], min_val=NE, max_val=NE + 3)
            with dve.Fori(0, J) as j:
                def turned(c):
                    dve.wait_ge(m_hh, j * NEC + (c + 1))
                    V.tensor_tensor(HT[c % 2][1], psum[:, 6, :], HT[c % 2][0].bitcast(F32), ALU.subtract).then_inc(m_hT, 1)
                for i, (what, c) in enumerate(LOADS):
                    for n in range(4):
                        dve.wait_ge(m_hi, j * NP + (4 * i + n + 1))
                        r = (4 * i + n) % 4
                        V.tensor_tensor(w_lo[:, r, :], piece(i, n), w_hi[:, r, :].bitcast(F32), ALU.subtract).then_inc(m_lo, 1)
                    if (what, c) == ("u", 0):
                        scattered(j)
                    if what == "u" and c >= 1:
                        turned(c - 1)
                    if i >= 1 and LOADS[i - 1][0] == "u":
                        c_ = LOADS[i - 1][1]
                        consumed(dve, j, ("u", c_))
                        dve.wait_ge(m_sil, j * NEC + (c_ + 1))
                        V.tensor_tensor(SIL[c_ % 2], SIL[c_ % 2], psum[:, 2 * (c_ % 2) + 1, :], ALU.mult).then_inc(m_h, 1)
                    if (what, c) == ("d", 1):
                        dve.wait_ge(m_pt, j + 1)
                        V.tensor_copy(PgT, psum[:, 7, 0:256]).then_inc(m_pte, 1)
                    if (what, c) == ("d", 3):
                        nxt = dve.value_load(jobs[0:1, bass.ds(j + 1, 1)], min_val=0, max_val=2 * NE - 1)
                        onehot(nxt)
                turned(NEC - 1)
                gathered(j * 2 + 3, j + 2)
            scattered(J)
            norm_dve(dve, 4)
            for b in range(TB):
                dve.wait_ge(n_xn, 9 + b)
                V.tensor_tensor(h[:, b, :], xn3[:, b, :], gain, ALU.mult).then_inc(y_done, 1)

        def moe_pool(pool):
            for b in range(TB):
                pool.wait_ge(y_done, b + 1)
                pool.dma_start(out[0, b * P:(b + 1) * P, :], h[:, b, :]).then_inc(s_out, 16)
            pool.wait_ge(s_out, 32)
        y_done = sem("y_done")



        @block.sync
        def _(sp):
            sp.dma_start(h[:, :, :], I["x"].rearrange("b (n p) d -> p (b n) d", p=P)).then_inc(s_x, 16)
            sp.dma_start(cst[:, :], cst_dram).then_inc(s_cst, 16)
            at = 0
            for group, base in ((COLUMNS, 0), (COLUMNS2, 1)):
                at = 0
                for name, n in group:
                    a = I[name]
                    dims = " ".join("abcd"[:len(a.shape)])
                    flat = a.rearrange(f"{dims} -> ({dims})").rearrange("(r c) -> r c", c=P)
                    sp.dma_start(colsrc[at:at + n, base * P:base * P + P], flat).then_inc(s_colsrc, 16)
                    at += n
            win = I["e_w_in"].rearrange("a (k p) n -> p (a k) n", p=P)
            for k in range(3):
                sp.dma_start(w8(k), win[:, :, 512 * k:512 * k + 512]).then_inc(slot_in[k], 16)
            wout = I["e_w_out"].rearrange("a (k p) n -> p (a k) n", p=P)
            for k in range(2):
                sp.dma_start(w8(3 + k), wout[:, :, 512 * k:512 * k + 512]).then_inc(slot_in[3 + k], 16)
            if not reached(2):
                return
            wg = I["e_ffn_wg"].rearrange("a (k p) f -> p (a k) f", p=P)
            wup = I["e_ffn_wu"].rearrange("a (k p) f -> p (a k) f", p=P)
            wd = I["e_ffn_wd"].rearrange("a (k p) n -> p (a k) n", p=P)
            for c in range(NFC):
                if c == 0:
                    sp.wait_ge(p_in, 8)
                if c == 1:
                    sp.wait_ge(p_in, 10)
                if c == 2:
                    sp.wait_ge(s_wo, 4)
                if c == 3:
                    sp.wait_ge(s_h, 4)
                if c >= 4:
                    ffn_split(sp, c - 4)
                if c == 4 and reached(3):
                    rwkv_lora_sp(sp)
                k = c % 4
                g, u, d = ffn_slot(k)
                sp.dma_start(g, wg[:, :, FC * c:FC * c + FC]).then_inc(ffn_in[k], 16)
                sp.dma_start(u, wup[:, :, FC * c:FC * c + FC]).then_inc(ffn_in[k], 16)
                sp.dma_start(d, wd[:, 2 * c:2 * c + 2, :]).then_inc(ffn_in[k], 16)
            if reached(3):
                rwkv_sp(sp)
            if reached(4):
                moe_sp(sp)

        @block.scalar
        def _(act):
            bc = lambda name, n: I[name].rearrange("a n -> (a n)").partition_broadcast(P)
            act.dma_start(E_["lng"], bc("e_sgu_ln_g", 512)).then_inc(s_small, 16)
            act.dma_start(E_["lnb"], bc("e_sgu_ln_b", 512)).then_inc(s_small, 16)
            act.dma_start(E_["bias"], I["e_sgu_bias"].rearrange("a h t -> (a h t)").partition_broadcast(P)).then_inc(s_small, 16)
            act.dma_start(r3(E_["ws"], 4), I["e_sgu_ws"].rearrange("a h t s -> t (a h) s")).then_inc(s_small, 16)
            act.dma_start(r3(E_["pw"], 4), I["e_pool_w"].rearrange("a g c d -> c (a g) d")).then_inc(s_small, 16)
            norm_act(act, 0)
            act.wait_ge(cols_done, 1)
            norm_cols(0, "e_norm_mix")[0](act)
            uT = r3(E_["uT"], 4)
            for g in range(4):
                act.wait_ge(p_in, 5 + g)
                nc.scalar.activation(uT[:, g, :], psum[:, 4 + g, 0:T], ACT.Gelu).then_inc(g_ev, 1)
            v = r3(E_["v"], 2)
            for b in range(TB):
                act.wait_ge(p_in, 9 + b)
                nc.scalar.activation(v[:, b, :], psum[:, b, :], ACT.Gelu).then_inc(g_ev, 1)
            act.wait_ge(s_vn, 1)
            nc.scalar.activation(small[:, 32:40], small[:, 24:32], ACT.Sqrt).then_inc(g_ev, 1)
            for g in range(4):
                act.wait_ge(s_ymm, g + 1)
                nc.scalar.activation(mixT[:, g, :], psum[:, 2 + g, 0:T], ACT.Copy, scale=col("e_pool_scale", g)).then_inc(s_yev, 1)
            if not reached(2):
                return
            norm_act(act, 1)
            norm_split_act(act)

            def hidden_hi(c):
                act.wait_ge(f_h, c + 1)
                if c >= 2:
                    ffn_product(act, "d", c - 2)
                nc.scalar.activation(fh_split[:, c % 2, 0, :], f_sil_buf[c % 2], ACT.Copy).then_inc(f_hh, 1)

            def silu(c):
                ffn_product(act, "g", c)
                if c >= 2:
                    act.wait_ge(f_hT, c - 1)
                nc.scalar.activation(f_sil_buf[c % 2], psum[:, 4 + 2 * (c % 2), :], ACT.Silu).then_inc(f_sil, 1)

            for i, (what, c, n) in enumerate(FPIECES):
                act.wait_ge(ffn_in[c % 4], 48 * (c // 4 + 1))
                if i >= 4:
                    act.wait_ge(f_pc, i - 3)
                nc.scalar.activation(as_piece(f_hi, i, what), ffn_piece(what, c, n), ACT.Copy).then_inc(f_phi, 1)
                if (what, n) == ("d", 0) and c + 1 < NFC:
                    silu(c + 1)
                if (what, c, n) == ("g", 1, 0):
                    silu(0)
                if (what, n) == ("g", 1) and c >= 1:
                    hidden_hi(c - 1)
                if (what, c, n) == ("d", NFC - 2, 1):
                    hidden_hi(NFC - 1)
            if reached(3):
                rwkv_act(act)
            if reached(4):
                moe_act(act)

        @block.vector
        def _(dve):
            a, s, t = (r3(E_[x], 4) for x in "ast")
            for x in (a, s, t):
                nc.vector.memset(x[:, :, 0:PAD], 0.0).then_inc(z_pad, 1)
            norm_dve(dve, 0)
            dve.wait_ge(colT, 2)
            nc.vector.tensor_copy(cols[:, :], psum[:, 7, 0:144]).then_inc(cols_done, 1)
            dve.wait_ge(cols_done, 1)
            norm_cols(0, "e_norm_mix")[1](dve)
            for g in range(4):
                dve.wait_ge(p_in, 1 + g)
                nc.vector.tensor_copy(a[:, g, PAD:], psum[:, g, 0:T]).then_inc(a_ev, 1)
            dve.wait_ge(a_ev, 4)
            dve.wait_ge(z_pad, 3)
            n = T + PAD
            link(dve, "dve", nc.vector.tensor_tensor(s[:, :, PAD:], a[:, :, PAD:], a[:, :, PAD - 1:n - 1], ALU.add))
            link(dve, "dve", nc.vector.tensor_tensor(t[:, 1:, PAD:], s[:, 1:, PAD:], s[:, 1:, PAD - 2:n - 2], ALU.add))
            link(dve, "dve", nc.vector.tensor_tensor(s[:, 2:, PAD:], t[:, 2:, PAD:], t[:, 2:, PAD - 4:n - 4], ALU.add))
            link(dve, "dve", nc.vector.tensor_tensor(t[:, 3:, PAD:], s[:, 3:, PAD:], s[:, 3:, PAD - 8:n - 8], ALU.add))
            inv = r3(C("invcnt"), 4)
            for g, src in enumerate((s, t, s, t)):
                last = nc.vector.tensor_tensor(pooled[:, g, :], src[:, g, PAD:], inv[:, g, :], ALU.mult)
            link(dve, "dve", last)
            nc.vector.tensor_tensor(pooled[:, :, :], pooled[:, :, :], a[:, :, PAD:], ALU.subtract).then_inc(s_pooled, 1)
            dve.wait_ge(s_wsT, 1)
            nc.vector.tensor_tensor(r3(E_["wsT"], 4), r3(psum[:, 6, :], 4),
                                    C("upto").unsqueeze(1).to_broadcast([P, 4, P]), ALU.mult).then_inc(s_wsTm, 1)
            dve.wait_ge(g_ev, 6)
            v8, c8, q8 = (r3(E_[x], 8) for x in ("v", "vc", "sq"))

            def per_head(x):
                return x.unsqueeze(2).to_broadcast([P, 8, P])
            link(dve, "dve", nc.vector.tensor_reduce(small[:, 8:16], v8, AX.X, ALU.add))
            link(dve, "dve", nc.vector.tensor_scalar(small[:, 8:16], small[:, 8:16], 1.0 / P, None, ALU.mult))
            link(dve, "dve", nc.vector.tensor_tensor(c8, v8, per_head(small[:, 8:16]), ALU.subtract))
            link(dve, "dve", nc.vector.tensor_tensor(q8, c8, c8, ALU.mult))
            link(dve, "dve", nc.vector.tensor_reduce(small[:, 16:24], q8, AX.X, ALU.add))
            nc.vector.tensor_scalar(small[:, 24:32], small[:, 16:24], 1.0 / P, LN_EPS, ALU.mult, ALU.add).then_inc(s_vn, 1)
            dve.wait_ge(g_ev, 7)
            link(dve, "dve", nc.vector.reciprocal(small[:, 40:48], small[:, 32:40]))
            link(dve, "dve", nc.vector.tensor_tensor(c8, c8, per_head(small[:, 40:48]), ALU.mult))
            c2 = r3(E_["vc"], 2)
            dve.wait_ge(s_small, 80)
            bc = lambda x: x.unsqueeze(1).to_broadcast([P, 2, 512])
            link(dve, "dve", nc.vector.tensor_tensor(c2, c2, bc(E_["lng"]), ALU.mult))
            nc.vector.tensor_tensor(c2, c2, bc(E_["lnb"]), ALU.add).then_inc(s_vn, 1)
            for q in range(2):
                dve.wait_ge(s_mm, q + 1)
                dst = mixT[:, 4 + 2 * q:6 + 2 * q, :].rearrange("p g (n t) -> p g n t", n=2)
                src = psum[:, 6 + q, :].rearrange("p (g n t) -> p g n t", g=2, n=2)
                b4 = r3(E_["bias"], 4)[:, 2 * q:2 * q + 2, :].unsqueeze(2).to_broadcast([P, 2, 2, P])
                link(dve, "dve", nc.vector.tensor_tensor(dst, src, b4, ALU.add))
                nc.vector.tensor_tensor(mixT[:, 4 + 2 * q:6 + 2 * q, :], mixT[:, 4 + 2 * q:6 + 2 * q, :],
                                        r3(E_["uT"], 4)[:, 2 * q:2 * q + 2, :], ALU.mult).then_inc(s_mix, 1)
            add_to_h(dve, s_wo, 0, 0)
            if not reached(2):
                return
            norm_dve(dve, 1)
            norm_split_dve(dve)

            def hidden(c):
                ffn_product(dve, "u", c)
                dve.wait_ge(f_sil, c + 1)
                nc.vector.tensor_tensor(f_sil_buf[c % 2], f_sil_buf[c % 2], psum[:, 5 + 2 * (c % 2), :],
                                        ALU.mult).then_inc(f_h, 1)

            def hidden_lo(c):
                dve.wait_ge(f_hh, c + 1)
                dve.wait_ge(f_h, c + 1)
                nc.vector.tensor_tensor(fh_split[:, c % 2, 1, :], f_sil_buf[c % 2], fh_split[:, c % 2, 0, :].bitcast(F32),
                                        ALU.subtract).then_inc(f_hT, 1)

            for i, (what, c, n) in enumerate(FPIECES):
                dve.wait_ge(f_phi, i + 1)
                nc.vector.tensor_tensor(as_piece(f_lo, i, what), ffn_piece(what, c, n),
                                        as_piece(f_hi, i, what).bitcast(F32), ALU.subtract).then_inc(f_plo, 1)
                if (what, n) == ("g", 0) and c >= 1:
                    hidden(c - 1)
                if (what, n) == ("g", 1) and c >= 1:
                    hidden_lo(c - 1)
                if (what, c, n) == ("d", NFC - 2, 1):
                    hidden(NFC - 1)
                    hidden_lo(NFC - 1)
            add_to_h(dve, f_pc, len(FPIECES) - 1, 0, one=True)
            if reached(3):
                rwkv_dve(dve)
            if reached(4):
                moe_dve(dve)

        @block.tensor
        def _(pe):
            pe.wait_ge(s_cst, 16)
            pe.wait_ge(s_colsrc, 16 * (len(COLUMNS) + len(COLUMNS2)))
            nc.tensor.transpose(psum[:, 7, 0:P], colsrc[:, 0:P], ident).then_inc(colT, 1)
            nc.tensor.transpose(psum[:, 7, P:P + 16], colsrc[0:16, P:2 * P], cst[0:16, 0:16]).then_inc(colT, 1)
            norm_pe(pe, 0)
            norm_ready(pe, 0)
            pe.wait_ge(slot_in[0], 16)
            pe.wait_ge(cols_done, 1)
            for g in range(8):
                if g == 4:
                    pe.wait_ge(slot_in[1], 16)
                for k in range(KT):
                    last = nc.tensor.matmul(psum[:, g, 0:T], w8(g // 4)[:, k, (g % 4) * P:(g % 4 + 1) * P],
                                            xnT[:, k, :], start=(k == 0), stop=(k == KT - 1))
                last.then_inc(p_in, 1)
            pe.wait_ge(slot_in[2], 16)
            for b in range(TB):
                pe.wait_ge(a_ev, b + 1)
                for k in range(KT):
                    last = nc.tensor.matmul(psum[:, b, :], xnT[:, k, b * P:(b + 1) * P], w8(2)[:, k, :],
                                            start=(k == 0), stop=(k == KT - 1))
                last.then_inc(p_in, 1)
            pe.wait_ge(s_small, 80)
            pe.wait_ge(g_ev, 4)
            for g in range(4):
                last = nc.tensor.transpose(psum[:, 6, g * P:(g + 1) * P], r3(E_["ws"], 4)[:, g, :], ident)
            last.then_inc(s_wsT, 1)
            pe.wait_ge(s_pooled, 1)
            pe.wait_ge(a_ev, 4)
            for g in range(4):
                nc.tensor.matmul(psum[:, 2 + g, 0:T], r3(E_["pw"], 4)[:, g, :], pooled[:, g, :],
                                 start=True, stop=True).then_inc(s_ymm, 1)
            pe.wait_ge(s_vn, 2)
            pe.wait_ge(s_wsTm, 1)
            for q in range(2):
                for g in (2 * q, 2 * q + 1):
                    for b in range(TB):
                        o = (g % 2) * T + b * P
                        last = nc.tensor.matmul(psum[:, 6 + q, o:o + P],
                                                E_["vc"][:, b * 512 + g * P:b * 512 + (g + 1) * P],
                                                r3(E_["wsT"], 4)[:, g, :], start=True, stop=True)
                last.then_inc(s_mm, 1)
            pe.wait_ge(slot_in[3], 16)
            pe.wait_ge(slot_in[4], 16)
            pe.wait_ge(s_mix, 2)
            pe.wait_ge(s_yev, 4)
            pe.wait_ge(g_ev, 6)
            rows_product(pe, mixT, lambda q: w8(3 + q), 0, s_wo)
            if not reached(2):
                return
            pe.wait_ge(s_h, 4)
            norm_pe(pe, 1)
            norm_ready(pe, 1)

            def three(dst, l_hi, l_lo, r_hi, r_lo, first, last_):
                nc.tensor.matmul(dst, l_hi, r_hi, start=first, stop=False)
                nc.tensor.matmul(dst, l_lo, r_hi, start=False, stop=False)
                return nc.tensor.matmul(dst, l_hi, r_lo, start=False, stop=last_)

            def gate_up(c):
                for w, bank in enumerate((4, 5)):
                    bank += 2 * (c % 2)
                    if c >= 2:
                        pe.wait_ge(f_sil if w == 0 else f_h, c - 1)
                    for j in range(2):
                        i = FAT["gu"[w], c, j]
                        pe.wait_ge(f_plo, i + 1)
                        hi, lo = as_piece(f_hi, i, "g"), as_piece(f_lo, i, "g")
                        for k in range(KT):
                            last = three(psum[:, bank, j * T:(j + 1) * T], hi[:, k, :], lo[:, k, :], x_split[:, 1, k, :],
                                         x_split[:, 0, k, :], k == 0, k == KT - 1)
                        last.then_inc(f_pc, 1)

            def down(c):
                pe.wait_ge(f_hT, c + 1)
                for j in range(2):
                    i = FAT["d", c, j]
                    pe.wait_ge(f_plo, i + 1)
                    for b in range(TB):
                        tok = slice(j * T + b * P, j * T + (b + 1) * P)
                        for q in range(2):
                            half = slice(512 * q, 512 * q + 512)
                            last = three(psum[:, 2 * b + q, :], fh_split[:, c % 2, 0, tok], fh_split[:, c % 2, 1, tok],
                                         f_hi[:, i % 4, half], f_lo[:, i % 4, half], c == 0 and j == 0,
                                         c == NFC - 1 and j == 1)
                    last.then_inc(f_pc, 1)

            for c in range(NFC + 1):
                if c < NFC:
                    gate_up(c)
                if c >= 1:
                    down(c - 1)
            if reached(3):
                rwkv_pe(pe)
            if reached(4):
                moe_pe(pe)

        @block.gpsimd
        def _(pool):
            if reached(3):
                rwkv_pool(pool)
            if reached(4):
                moe_pool(pool)
            if probe is not None:
                where, s_, v_ = probe(P_)
                pool.wait_ge(s_, v_)
                pool.dma_start(out, where).then_inc(s_dbg, 16)
                pool.wait_ge(s_dbg, 16)


_OUT = (1, T, D)


def kernel(**inputs):
    from concourse import bacc
    from concourse.bass_utils import run_bass_kernel_spmd
    nc = bacc.Bacc("TRN2", target_bir_lowering=False, num_devices=1)
    arrays, aps = {}, {}
    for name, a in inputs.items():
        if a.size:
            a = np.ascontiguousarray(a)
            arrays[name + "_dram"] = a
            aps[name] = nc.dram_tensor(name + "_dram", a.shape, mybir.dt.from_np(a.dtype), kind="ExternalInput").ap()
    arrays["constants_dram"] = constants()
    cst = nc.dram_tensor("constants_dram", (P, CW), F32, kind="ExternalInput").ap()
    out = nc.dram_tensor("out_dram", _OUT, F32, kind="ExternalOutput").ap()
    trunk(nc, aps, cst, out)
    return run_bass_kernel_spmd(nc, [arrays], core_ids=[0]).results[0]["out_dram"]
```

```python
from contextlib import ExitStack

import numpy as np
import concourse.bass as bass
from concourse import mybir

F32 = mybir.dt.float32
FR = mybir.dt.float32r
I32 = mybir.dt.int32
ALU = mybir.AluOpType
ACT = mybir.ActivationFunctionType
AX = mybir.AxisListType

P = 128
D = 1024
KT = D // P
T = 256
TB = T // P
WINDOWS = (2, 4, 8, 16)
PAD = 16
F = 2816
FC = 256
NFC = F // FC
NE = 8
FE = 3584
EC = 512
NEC = FE // EC
HD = 64
SQRT_E_INV = float(np.exp(-0.5))
RMS_EPS, LN_EPS, GN_EPS = 1e-6, 1e-5, 64e-5
LEVELS = (1, 2, 4, 8, 16, 32, 64)

CONST = {}
CW = 0
for _name, _w in (("ident", 128), ("upto", 128), ("before", 128), ("heads", 128), ("iota", 128),
                  ("cum", 256), ("level", 128 * len(LEVELS)), ("invcnt", 4 * T), ("ones", 128)):
    CONST[_name] = (CW, CW + _w)
    CW += _w

HSEL_AT = CW
HSPREAD_AT = CW + 16
CD = CW + 16 + 512


def constants():
    s = np.arange(P)[:, None]
    t = np.arange(P)[None, :]
    c = np.zeros((P, CD), np.float32)

    def put(name, v):
        c[:, CONST[name][0]:CONST[name][1]] = v

    put("ident", s == t)
    put("upto", s <= t)
    put("before", s < t)
    put("heads", s // HD == t // HD)
    put("iota", np.broadcast_to(t, (P, P)))
    mid = (s < P // 2).astype(np.float32)
    put("cum", np.concatenate([(s <= t) - mid, (s < t) - mid], 1))
    put("level", np.concatenate([(s // (2 * b) == t // (2 * b)) & (s // b % 2 == 0) & (t // b % 2 == 1)
                                 for b in LEVELS], 1))
    tok = np.arange(T)
    put("invcnt", np.concatenate([np.broadcast_to(1.0 / np.minimum(tok + 1, w), (P, T)) for w in WINDOWS], 1))
    put("ones", 1.0)
    c[0:HD, HSEL_AT + 6] = 1.0
    c[HD:P, HSEL_AT + 7] = 1.0
    c[0:8, HSPREAD_AT:] = np.arange(8)[:, None] == np.arange(4 * P)[None, :] // HD
    return c


COLUMNS = (("e_norm_mix", 8), ("e_norm_ffn", 8), ("o_norm_mix", 8), ("o_norm_ffn", 8), ("e_pool_scale", 4),
           ("e_sgu_bias", 4), ("o_mu", 48), ("o_w0", 8), ("o_a0", 8), ("o_k_k", 8), ("o_k_a", 8), ("o_r_k", 8))
COLUMNS2 = (("o_lnx_w", 8), ("o_lnx_b", 8))
COL = {}
for _group, _base in ((COLUMNS, 0), (COLUMNS2, 128)):
    for _name, _n in _group:
        COL[_name] = _base
        _base += _n


def trunk(nc, I, cst_dram, out):
    ctx = ExitStack()
    with ctx:
        def sb(name, shape, dt=F32):
            return ctx.enter_context(nc.sbuf_tensor(name, shape, dt))

        def sem(name):
            return ctx.enter_context(nc.semaphore(name))

        U = 2048
        cst = sb("cst", [P, CW])
        colsrc = sb("colsrc", [P, 256])
        cols = sb("cols", [P, 144])
        h = sb("h", [P, TB, D])
        with nc.sbuf_tensor("x_split", [P, 2, KT, T], FR) as x_split:
            pass
        xn = sb("xn", [P, TB * D])
        xnT = sb("xnT", [P, KT, T])
        with nc.sbuf_tensor("ffn_slots", [P, 12 * U], F32), nc.sbuf_tensor("f_hi", [P, 4, 1024], FR) as f_hi, \
                nc.sbuf_tensor("f_lo", [P, 4, 1024], FR) as f_lo, nc.sbuf_tensor("lora_place", [P, 4 * U], F32), \
                nc.sbuf_tensor("fh_split", [P, 2, 2, 512], FR) as fh_split:
            pass
        ring = sb("ring", [P, 14 * U])
        with nc.sbuf_tensor("w_hi", [P, 4, 1024], FR) as w_hi, nc.sbuf_tensor("w_lo", [P, 4, 1024], FR) as w_lo, \
                nc.sbuf_tensor("xg_split", [P, 2, KT, P], FR) as xg_split, \
                nc.sbuf_tensor("ht_split", [P, 2, 2, 512], FR) as ht_split:
            pass
        work = sb("work", [P, 7 * U])
        small = sb("small", [P, 512])
        psum = ctx.enter_context(nc.psum_tensor("psum", [P, 8, 512], F32))

        def C(name):
            return cst[:, CONST[name][0]:CONST[name][1]]

        def col(name, k, n=1, p=P):
            return cols[0:p, COL[name] + k:COL[name] + k + n]

        def ru(u, w=U, o=0):
            return ring[:, u * U + o:u * U + o + w]

        def wu(u, w=U, o=0):
            return work[:, u * U + o:u * U + o + w]

        def slot(k):
            return ring[:, 2 * U * k:2 * U * (k + 1)]

        def w8(k):
            return slot(k).rearrange("p (k n) -> p k n", k=KT)

        def r3(ap, a):
            return ap.rearrange("p (a b) -> p a b", a=a)

        ident = C("ident")
        xn3 = r3(xn[:, :], TB)

        E_ = {}
        o = 0
        for name, w in (("a", 4 * (T + PAD)), ("s", 4 * (T + PAD)), ("t", 4 * (T + PAD)), ("uT", 4 * T), ("v", 4 * T),
                        ("vc", 4 * T), ("sq", 4 * T), ("lng", 512), ("lnb", 512), ("bias", 512), ("ws", 512),
                        ("wsT", 512), ("pw", 512)):
            E_[name] = work[:, o:o + w]
            o += w
        mixT = ring[:, 10 * U:11 * U].rearrange("p (k t) -> p k t", k=KT)
        pooled = ring[:, 11 * U:11 * U + 4 * T].rearrange("p (g t) -> p g t", g=4)
        assert o <= 7 * U

        s_cst, s_colsrc, s_x, s_small = sem("cst_in"), sem("colsrc_in"), sem("x_in"), sem("small_in")
        slot_in = [sem(f"slot{k}_in") for k in range(7)]
        ffn_in = [sem(f"ffn{k}_in") for k in range(4)]
        cols_done = sem("cols_copied")
        colT = sem("cols_transposed")
        n_ss, n_ms, n_sd, n_xn = sem("norm_squares"), sem("norm_mean"), sem("norm_sqrt"), sem("norm_rows")
        n_r = sem("norm_recip")
        n_tr, n_eva, n_evd = sem("norm_transposed"), sem("norm_cols_act"), sem("norm_cols_dve")
        dvc = sem("dve_chain")
        acc_ = sem("act_chain")
        plc = sem("pool_chain")
        p_in, a_ev, g_ev = sem("in_proj"), sem("pool_in_copied"), sem("gelu_done")
        z_pad = sem("pads_zeroed")
        s_pooled, s_ymm, s_yev = sem("pooled"), sem("pool_mm"), sem("pool_out")
        s_wsT, s_wsTm, s_vn, s_mm, s_mix = sem("ws_transposed"), sem("ws_masked"), sem("v_normed"), sem("mixed"), sem("mix_out")
        s_wo, s_h = sem("out_proj"), sem("h_added")
        f_sil, f_h = sem("ffn_silu"), sem("ffn_hidden")
        f_hh, f_hT = sem("ffn_hidden_hi"), sem("ffn_hidden_split")
        f_phi, f_plo, f_pc = sem("ffn_pieces_hi"), sem("ffn_pieces_split"), sem("ffn_pieces_used")
        s_out = sem("out_written")

        chain = {"dve": 0, "act": 0, "pool": 0}
        CH = {"dve": dvc, "act": acc_, "pool": plc}

        def link(eng, which, ins):
            chain[which] += 1
            ins.then_inc(CH[which], 1)
            eng.wait_ge(CH[which], chain[which])

        def ffn_slot(k):
            b = ring[:, 3 * U * k:3 * U * (k + 1)]
            return (b[:, 0:U].rearrange("p (k f) -> p k f", k=KT), b[:, U:2 * U].rearrange("p (k f) -> p k f", k=KT),
                    b[:, 2 * U:3 * U].rearrange("p (j n) -> p j n", j=2))

        FPIECES = [(w, 0, n) for w in "gu" for n in range(2)]
        for c in range(1, NFC):
            FPIECES += [(w, c - (w == "d"), n) for w in "gud" for n in range(2)]
        FPIECES += [("d", NFC - 1, n) for n in range(2)]
        FAT = {x: i for i, x in enumerate(FPIECES)}
        f_sil_buf = [work[:, 2 * U + 1024 + 512 * i:2 * U + 1536 + 512 * i] for i in range(2)]

        def ffn_piece(what, c, n):
            g, u, d = ffn_slot(c % 4)
            return d[:, n, :] if what == "d" else (g if what == "g" else u)[:, :, n * P:(n + 1) * P]

        def as_piece(w, i, what):
            return w[:, i % 4, :] if what == "d" else w[:, i % 4, :].rearrange("p (k f) -> p k f", k=KT)

        def ffn_split(eng, c):
            eng.wait_ge(f_plo, FAT["d", c, 1] + 1)

        def ffn_product(eng, what, c):
            eng.wait_ge(f_pc, FAT[what, c, 1] + 1)

        block = ctx.enter_context(nc.Block())

        def norm_act(act, i, s_at=None):
            for b in range(TB):
                if i == 0:
                    act.wait_ge(s_x, 16)
                else:
                    act.wait_ge(s_h, (H_AT[i] if s_at is None else s_at) - 2 + 2 * b)
                if i >= 1:
                    act.wait_ge(n_tr, 4 * i)
                nc.scalar.activation(xn3[:, b, :], h[:, b, :], ACT.Square,
                                     accum_out=small[:, b:b + 1]).then_inc(n_ss, 1)
                act.wait_ge(n_ms, 2 * i + b + 1)
                nc.scalar.activation(small[:, 4 + b:5 + b], small[:, 2 + b:3 + b], ACT.Sqrt).then_inc(n_sd, 1)

        def norm_mean(dve, i, b):
            dve.wait_ge(n_ss, 2 * i + b + 1)
            nc.vector.tensor_scalar(small[:, 2 + b:3 + b], small[:, b:b + 1], 1.0 / D, RMS_EPS, ALU.mult, ALU.add).then_inc(n_ms, 1)

        def norm_rows(dve, i, b):
            dve.wait_ge(n_sd, 2 * i + b + 1)
            nc.vector.reciprocal(small[:, 6 + b:7 + b], small[:, 4 + b:5 + b]).then_inc(n_r, 1)
            dve.wait_ge(n_r, 2 * i + b + 1)
            nc.vector.tensor_scalar(xn3[:, b, :], h[:, b, :], small[:, 6 + b:7 + b], None, ALU.mult).then_inc(n_xn, 1)

        def norm_dve(dve, i):
            for b in range(TB):
                norm_mean(dve, i, b)
                norm_rows(dve, i, b)

        def norm_pe(pe, i):
            for b in range(TB):
                pe.wait_ge(n_xn, 2 * i + b + 1)
                for k in range(KT):
                    last = nc.tensor.transpose(psum[:, 4 + k // 2, (k % 2) * T + b * P:(k % 2) * T + b * P + P],
                                               xn3[:, b, k * P:(k + 1) * P], ident)
                    if b == TB - 1 and k % 2 == 1:
                        last.then_inc(n_tr, 1)

        def norm_cols(i, gain):
            def act_part(act):
                for q in (0, 2):
                    act.wait_ge(n_tr, 4 * i + q + 1)
                    for j in range(2):
                        k = 2 * q + j
                        nc.scalar.activation(xnT[:, k, :], psum[:, 4 + q, j * T:j * T + T], ACT.Copy,
                                             scale=col(gain, k)).then_inc(n_eva, 1)

            def dve_part(dve):
                for q in (1, 3):
                    dve.wait_ge(n_tr, 4 * i + q + 1)
                    for j in range(2):
                        k = 2 * q + j
                        nc.vector.tensor_scalar(xnT[:, k, :], psum[:, 4 + q, j * T:j * T + T], col(gain, k), None,
                                                ALU.mult).then_inc(n_evd, 1)
            return act_part, dve_part

        def norm_split_act(act):
            for q in range(4):
                act.wait_ge(n_tr, 4 + q + 1)
                for k in (2 * q, 2 * q + 1):
                    last = nc.scalar.activation(x_split[:, 1, k, :], psum[:, 4 + q, (k % 2) * T:(k % 2) * T + T], ACT.Copy,
                                                scale=col("e_norm_ffn", k))
                last.then_inc(n_eva, 1)

        def norm_split_dve(dve):
            dve.wait_ge(n_tr, 8)
            for q in range(4):
                dve.wait_ge(n_eva, 4 + q + 1)
                for k in (2 * q, 2 * q + 1):
                    last = nc.vector.scalar_tensor_tensor(
                        out=x_split[:, 0, k, :], in0=psum[:, 4 + q, (k % 2) * T:(k % 2) * T + T], scalar=col("e_norm_ffn", k),
                        in1=x_split[:, 1, k, :].bitcast(F32), op0=ALU.mult, op1=ALU.subtract)
                last.then_inc(n_evd, 1)

        def norm_ready(eng, i):
            eng.wait_ge(n_eva, 4 * i + 4)
            eng.wait_ge(n_evd, 4 * i + 4)

        H_AT = {0: 0, 1: 4, 2: 8, 3: 12, 4: 12}

        def add_to_h(dve, ready, counts, i):
            def add(q):
                dve.wait_ge(ready, counts[q])
                hs = h[:, q // 2, 512 * (q % 2):512 * (q % 2) + 512]
                nc.vector.tensor_tensor(hs, hs, psum[:, q, :], ALU.add).then_inc(s_h, 1)
            add(0)
            add(1)
            if counts[3] > counts[0]:
                norm_mean(dve, i, 0)
                norm_rows(dve, i, 0)
                add(2)
                add(3)
            else:
                add(2)
                norm_mean(dve, i, 0)
                add(3)
                norm_rows(dve, i, 0)
            norm_mean(dve, i, 1)
            norm_rows(dve, i, 1)

        def rows_product(pe, lhs, w, bank, done):
            for b in range(TB):
                for q in range(2):
                    for k in range(KT):
                        last = nc.tensor.matmul(psum[:, bank + 2 * b + q, :], lhs[:, k, b * P:(b + 1) * P],
                                                w(q)[:, k, :], start=(k == 0), stop=(k == KT - 1))
                    last.then_inc(done, 1)

        lora_in, mix_ready, mix_used = sem("lora_in"), sem("mix_ready"), sem("mix_used")
        o_mm, o_act, o_dve = sem("rwkv_product"), sem("rwkv_evac_act"), sem("rwkv_evac_dve")
        ones_row = sem("ones_row")
        k_sq, k_sd, rk_done, v_rows, bk_rows = sem("k_squares"), sem("k_norms"), sem("rk_done"), sem("v_rows"), sem("bk_rows")
        bk_cols = sem("bk_cols")
        ar_done = sem("scan_operands")
        v_tr, bk_tr = sem("v_transposed"), sem("bk_transposed")
        bonus_done = sem("bonus_done")
        a_mm, a_mask, x_seed, x_tr, x_ev = sem("scan_A"), sem("scan_A_masked"), sem("inverse_seed"), sem("inverse_seed_T"), sem("inverse_seed_copied")
        al_done = sem("level_mask")
        lv_y, lv_yc, lv_x, lv_xa = sem("level_Y"), sem("level_Y_copied"), sem("level_X"), sem("level_X_added")
        t_r, t_rc, t_u, t_uc, t_y, t_yc, t_s, t_sc = (sem(x) for x in (
            "R", "R_copied", "U", "U_copied", "Y", "Y_copied", "S", "S_copied"))
        gn_m, gn_c, gn_q, gn_v, gn_ve, gn_sd, gn_o = (sem(x) for x in (
            "gn_mean", "gn_centred", "gn_squares", "gn_var", "gn_var_copied", "gn_sqrt", "gn_out"))
        wo_done = sem("wo_product")
        k_ss, k_inv, k_sp, bonus_mm = sem("k_sums"), sem("k_inverse_norms"), sem("k_norms_spread"), sem("bonus_product")
        gn_r, gn_sp, gn_n = sem("gn_recip"), sem("gn_spread"), sem("gn_normed")

        w1s = wu(2, 512).rearrange("p (k n) -> p k n", k=KT)
        a1s = wu(2, 512, 512).rearrange("p (k n) -> p k n", k=KT)
        g1s = wu(3, 1280).rearrange("p (k n) -> p k n", k=KT)
        w2s, a2s = wu(5, 1024), wu(5, 1024, 1024)
        g2a, g2b = wu(4, 1024), wu(4, 1024, 1024)
        tw, ta, sga, sgb = (ru(13, 256, 256 * i) for i in range(4))
        mix = [r3(wu(u), KT) for u in (0, 1, 0, 1, 0, 4)]
        hsel = small[:, 96:112]
        hspread = C("invcnt")[0:8, 0:512]
        kn = xn[0:8, 0:512]
        gs = colsrc[0:8, :]
        xx = r3(xn[:, :], KT)
        rT, kT, vT, aT = (r3(wu(i), KT) for i in (2, 3, 5, 6))
        gT, Wi, We, Wv = (r3(ru(i), KT) for i in (8, 9, 10, 11))
        v_row = wu(4)
        sig = r3(ru(12), TB)
        kk, tmp = r3(ru(13), KT), r3(ru(12), KT)
        ARf = work[:, 0:2 * U]
        AR = ARf.rearrange("p (k c a t) -> p k c a t", k=KT, c=2, a=2)
        fac = small[:, 64:72]
        omk = small[:, 72:80]
        b_row, k_row = xn[:, 0:1024], xn[:, 1024:2048]
        A_sb = [ru(9).rearrange("p (l m t) -> p l m t", l=4, m=4), ru(10).rearrange("p (l m t) -> p l m t", l=4, m=4)]
        Xs, XTs, Ys = ([r3(ru(11 + q, 512, 512 * i), 4) for q in range(2)] for i in range(3))
        ALs = [[r3(ru(11 + q, 512, 1536), 4), r3(ru(q, 512), 4)] for q in range(2)]
        Rs = [wu(2, 256, 256 * q) for q in range(2)]
        Us = [wu(2, 256, 512 + 256 * q) for q in range(2)]
        ST = wu(2, 1024, 1024).rearrange("p (k i) -> p k i", k=KT)
        YT = aT
        sqT = xnT[:, :, :]
        MIX = (1, 4, 5, 0, 2, 3)

        def evacuated(eng, n):
            if n < 16:
                eng.wait_ge(o_act, n + 1)
            elif n < 24:
                eng.wait_ge(o_dve, n - 15)
            elif n < 40:
                eng.wait_ge(o_act, n - 7)
            elif n < 48:
                eng.wait_ge(o_dve, n - 31)
            else:
                eng.wait_ge(o_act, n - 15)

        def head_sums(src, half, dst):
            for j in range(4):
                last = nc.tensor.matmul(dst, hsel[:, 6 - 2 * j:14 - 2 * j], src[:, 4 * half + j, :], start=(j == 0), stop=(j == 3))
            return last

        def head_spread(src, dst):
            for j in range(4):
                last = nc.tensor.matmul(dst(j), hspread[:, j * P:(j + 1) * P], src, start=True, stop=True)
            return last

        def rwkv_lora_sp(sp):
            sp.wait_ge(s_h, 4)
            one = lambda name: I[name].rearrange("a (k p) n -> p (a k) n", p=P)
            two = lambda name: I[name].rearrange("a k n -> (a k) n")
            g2 = two("o_g2")
            for dst, src in ((w1s, one("o_w1")), (a1s, one("o_a1")), (g1s, one("o_g1")), (w2s[0:64, :], two("o_w2")),
                             (w2s[64:65, :], I["o_w0"]), (a2s[0:64, :], two("o_a2")), (g2a, g2[0:P, :]),
                             (g2b[0:32, :], g2[P:160, :]), (hsel, cst_dram[:, HSEL_AT:HSEL_AT + 16]),
                             (hspread, cst_dram[0:8, HSPREAD_AT:HSPREAD_AT + 512])):
                sp.dma_start(dst, src).then_inc(lora_in, 16)

        def rwkv_sp(sp):
            for n, (name, q) in enumerate((("o_wr", 0), ("o_wr", 1), ("o_wk", 0), ("o_wk", 1),
                                           ("o_wv", 0), ("o_wv", 1), ("o_wo", 0), ("o_wo", 1))):
                if n < 4:
                    ffn_split(sp, (8, 9, 9, 10)[n])
                else:
                    sp.wait_ge(o_mm, 32 + 4 * (n - 3))
                w = I[name].rearrange("a (k p) n -> p (a k) n", p=P)
                sp.dma_start(w8(n % 4), w[:, :, 512 * q:512 * q + 512]).then_inc(slot_in[n % 4], 16)

        def rwkv_pe(pe):
            pe.wait_ge(s_h, 8)
            norm_pe(pe, 2)
            norm_ready(pe, 2)
            pe.wait_ge(lora_in, 16 * 10)
            pe.wait_ge(f_h, NFC)

            def product(n, lhs_rhs, rows=P, width=T):
                if n >= 8:
                    evacuated(pe, n - 8)
                for i, (l, r) in enumerate(lhs_rhs):
                    last = nc.tensor.matmul(psum[0:rows, n % 8, 0:width], l, r, start=(i == 0), stop=(i == len(lhs_rhs) - 1))
                last.then_inc(o_mm, 1)
                return last

            pe.wait_ge(mix_ready, 1)
            product(0, [(w1s[:, k, :], mix[0][:, k, :]) for k in range(KT)], 64)
            pe.wait_ge(mix_ready, 2)
            product(1, [(a1s[:, k, :], mix[1][:, k, :]) for k in range(KT)], 64)
            pe.wait_ge(mix_ready, 3)
            product(2, [(g1s[:, k, 0:P], mix[2][:, k, :]) for k in range(KT)])
            product(3, [(g1s[:, k, P:160], mix[2][:, k, :]) for k in range(KT)], 32)
            pe.wait_ge(o_act, 1)
            pe.wait_ge(ones_row, 1)
            for b in range(TB):
                for q in range(2):
                    product(4 + 2 * b + q, [(tw[0:65, b * P:(b + 1) * P], w2s[0:65, 512 * q:512 * q + 512])], width=512)
            pe.wait_ge(o_act, 4)
            for k in range(KT):
                product(8 + k, [(a2s[0:64, k * P:(k + 1) * P], ta[0:64, :])])
            for k in range(KT):
                product(16 + k, [(g2a[:, k * P:(k + 1) * P], sga), (g2b[0:32, k * P:(k + 1) * P], sgb[0:32, :])])
            pe.wait_ge(o_act, 8)
            for k in range(KT):
                evacuated(pe, 16 + k)
                for b in range(TB):
                    last = nc.tensor.matmul(psum[:, k, b * T:(b + 1) * T], sig[:, b, k * P:(k + 1) * P], C("cum"),
                                            start=True, stop=True)
                last.then_inc(o_mm, 1)
            for i in range(3):
                pe.wait_ge(mix_ready, 4 + i)
                for q in range(2):
                    s_ = (2 * i + q) % 4
                    pe.wait_ge(slot_in[s_], 32 + 16 * (i == 2))
                    for m in range(4):
                        if 32 + 8 * i + 4 * q + m == 55:
                            pe.wait_ge(k_sd, 1)
                        product(32 + 8 * i + 4 * q + m,
                                [(w8(s_)[:, k, m * P:(m + 1) * P], mix[3 + i][:, k, :]) for k in range(KT)])
                    if (i, q) == (2, 0):
                        pe.wait_ge(k_sq, 1)
                        evacuated(pe, 47)
                        for half in range(2):
                            last = head_sums(sqT, half, psum[0:8, 7, half * T:(half + 1) * T])
                        last.then_inc(k_ss, 1)
            pe.wait_ge(k_inv, 1)
            evacuated(pe, 51)
            for half in range(2):
                head_spread(kn[:, half * T:(half + 1) * T],
                            lambda j: psum[:, 2 * half + j // 2, (j % 2) * T:(j % 2 + 1) * T]).then_inc(k_sp, 1)
            evacuated(pe, 55)
            for n in range(4):
                for j in range(4):
                    last = nc.tensor.transpose(psum[:, 4 + n, j * P:(j + 1) * P],
                                               vT[:, 4 * (n % 2) + j, (n // 2) * P:(n // 2 + 1) * P], ident)
                last.then_inc(v_tr, 1)
            pe.wait_ge(rk_done, 1)
            for k in range(KT):
                pe.wait_ge(v_rows, k // 2 + 1)
                last = nc.tensor.matmul(psum[:, 4 + k // 2, (k % 2) * T:(k % 2 + 1) * T], C("heads"), tmp[:, k, :],
                                        start=True, stop=True)
                if k % 2 == 1:
                    last.then_inc(bonus_mm, 1)
            pe.wait_ge(bk_cols, 3)
            for i, src in enumerate((kk, kT)):
                pe.wait_ge(ar_done, 2 + i)
                for q in range(2):
                    for j in range(4):
                        last = nc.tensor.transpose(psum[:, 2 * i + q, j * P:(j + 1) * P], src[:, 4 * q + j, 0:P], ident)
                    last.then_inc(bk_tr, 1)
            pe.wait_ge(bk_rows, 4)
            pe.wait_ge(ar_done, 3)

            for s_ in range(4):
                c = s_ // 2
                heads_ = [[(2 * (2 * s_ % 4 + q) + l // 2, HD * (l % 2)) for l in range(4)] for q in range(2)]
                for q in range(2):
                    if s_ >= 1:
                        pe.wait_ge(t_yc, 2 * (s_ - 1) + q + 1)
                        if c == 0 or s_ == 2:
                            pe.wait_ge(t_sc, 2 * min(s_ - 1, 1) + q + 1)
                    elif q == 1:
                        pe.wait_ge(bonus_done, 4)
                    for l, (k, o) in enumerate(heads_[q]):
                        rhs = AR[o:o + HD, k, c, :, :]
                        nc.tensor.matmul(psum[:, 4 * q + l, 0:T], kk[o:o + HD, k, c * P:(c + 1) * P], rhs, start=True, stop=True)
                        last = nc.tensor.matmul(psum[:, 4 * q + l, T:2 * T], kT[o:o + HD, k, c * P:(c + 1) * P], rhs,
                                                start=True, stop=True)
                    last.then_inc(a_mm, 1)
                for q in range(2):
                    g = 2 * s_ + q
                    pe.wait_ge(x_seed, g + 1)
                    pe.wait_ge(a_mask, g + 1)
                    for l in range(4):
                        last = nc.tensor.transpose(psum[:, 4 * q, l * P:(l + 1) * P], XTs[q][:, l, :], ident)
                    last.then_inc(x_tr, 1)
                for li in range(1, 7):
                    if s_ == 3 and li in (2, 4, 6):
                        if li == 2:
                            pe.wait_ge(t_yc, 6)
                            pe.wait_ge(x_ev, 8)
                            gn_mean(0, 0, 4)
                        elif li == 4:
                            pe.wait_ge(gn_q, 1)
                            head_sums(sqT, 0, psum[0:8, 0, 0:T]).then_inc(gn_v, 1)
                        else:
                            pe.wait_ge(gn_r, 1)
                            head_spread(gs, lambda j: psum[:, 4 * (j // 2), (j % 2) * T:(j % 2 + 1) * T]).then_inc(gn_sp, 1)
                    for q in range(2):
                        g = 2 * s_ + q
                        pe.wait_ge(al_done, lev(s_, li, q))
                        if li == 1:
                            pe.wait_ge(x_ev, g + 1)
                        else:
                            pe.wait_ge(lv_xa, lev(s_, li - 1, q))
                        for l in range(4):
                            last = nc.tensor.matmul(psum[:, 4 * q + 1, l * P:(l + 1) * P], ALs[q][li % 2][:, l, :],
                                                    Xs[q][:, l, :], start=True, stop=True)
                        last.then_inc(lv_y, 1)
                    for q in range(2):
                        pe.wait_ge(lv_yc, lev(s_, li, q))
                        for l in range(4):
                            last = nc.tensor.matmul(psum[:, 4 * q + 2, l * P:(l + 1) * P], Ys[q][:, l, :], XTs[q][:, l, :],
                                                    start=True, stop=True)
                        if li < 6:
                            for l in range(4):
                                last = nc.tensor.matmul(psum[:, 4 * q + 3, l * P:(l + 1) * P], XTs[q][:, l, :],
                                                        Ys[q][:, l, :], start=True, stop=True)
                        last.then_inc(lv_x, 1)
                if c == 1:
                    pe.wait_ge(t_sc, 4)
                if s_ == 3:
                    pe.wait_ge(gn_n, 1)
                for q in range(2):
                    for l, (k, o) in enumerate(heads_[q]):
                        last = nc.tensor.matmul(psum[:, 4 * q, l * P:(l + 1) * P], A_sb[q][:, l, 2, :],
                                                v_row[:, c * D + k * P:c * D + (k + 1) * P], start=True, stop=(c == 0))
                        if c == 1:
                            last = nc.tensor.matmul(psum[:, 4 * q, l * P:(l + 1) * P], AR[:, k, c, 0, :], ST[:, k, :],
                                                    start=False, stop=True)
                    last.then_inc(t_r, 1)
                for q in range(2):
                    g = 2 * s_ + q
                    pe.wait_ge(t_rc, g + 1)
                    pe.wait_ge(lv_xa, lev(s_, 6, q))
                    for l in range(4):
                        last = nc.tensor.matmul(psum[:, 4 * q + 1, l * P:(l + 1) * P], XTs[q][:, l, :],
                                                Rs[q][:, (l // 2) * P:(l // 2 + 1) * P], start=True, stop=True)
                    last.then_inc(t_u, 1)
                for q in range(2):
                    g = 2 * s_ + q
                    pe.wait_ge(t_uc, g + 1)
                    for l, (k, o) in enumerate(heads_[q]):
                        dst = psum[o:o + HD, 4 * q + 2, (l // 2) * P:(l // 2 + 1) * P]
                        vv = v_row[:, c * D + k * P + o:c * D + k * P + o + HD]
                        uu = Us[q][:, l * HD:(l + 1) * HD]
                        if c == 1:
                            nc.tensor.matmul(dst, ST[:, k, o:o + HD], AR[:, k, c, 1, :], start=True, stop=False)
                        nc.tensor.matmul(dst, uu, A_sb[q][:, l, 1, :], start=(c == 0), stop=False)
                        last = nc.tensor.matmul(dst, vv, A_sb[q][:, l, 3, :], start=False, stop=True)
                    last.then_inc(t_y, 1)
                    if c == 0:
                        for l in (0, 2):
                            k = heads_[q][l][0]
                            dst = psum[:, 4 * q + 3, (l // 2) * P:(l // 2 + 1) * P]
                            tile = slice(k * P, (k + 1) * P)
                            nc.tensor.matmul(dst, b_row[:, tile], Us[q][:, l * HD:(l + 2) * HD], start=True, stop=False)
                            last = nc.tensor.matmul(dst, k_row[:, tile], v_row[:, tile], start=False, stop=True)
                        last.then_inc(t_s, 1)
            pe.wait_ge(t_yc, 8)
            pe.wait_ge(lv_xa, lev(3, 6, 1))
            gn_mean(1, 4, 1)
            pe.wait_ge(gn_o, 1)
            for n in (2, 3):
                pe.wait_ge(slot_in[n], 48)

            def wo(k, n):
                return nc.tensor.matmul(psum[:, n, :], YT[:, k, (n // 2) * P:(n // 2 + 1) * P], w8(2 + n % 2)[:, k, :],
                                        start=(k == 0), stop=(k == KT - 1))
            for k in range(4):
                if k == 2:
                    pe.wait_ge(gn_q, 2)
                    head_sums(sqT, 1, psum[0:8, 6, 0:T]).then_inc(gn_v, 1)
                for n in range(4):
                    wo(k, n)
            pe.wait_ge(gn_r, 2)
            head_spread(gs, lambda j: psum[:, (7, 4)[j // 2], (j % 2) * T:(j % 2 + 1) * T]).then_inc(gn_sp, 1)
            pe.wait_ge(gn_o, 2)
            for n in range(4):
                for k in range(4, KT):
                    last = wo(k, n)
                last.then_inc(wo_done, 1)

        def gn_mean(half, bank, step):
            for j in range(4):
                last = nc.tensor.matmul(psum[:, bank + step * (j // 2), (j % 2) * T:(j % 2 + 1) * T], C("heads"),
                                        YT[:, 4 * half + j, :], start=True, stop=True)
            last.then_inc(gn_m, 1)

        def lev(s_, li, q):
            return 12 * s_ + 2 * (li - 1) + q + 1

        def rwkv_act(act):
            norm_act(act, 2)
            norm_cols(2, "o_norm_mix")[0](act)
            for n in range(16):
                act.wait_ge(o_mm, n + 1)
                ps = psum[:, n, :] if n < 8 else psum[:, n - 8, 0:T]
                if n == 0:
                    i_ = nc.scalar.activation(tw[0:64, :], ps[0:64, 0:T], ACT.Tanh)
                elif n == 1:
                    i_ = nc.scalar.activation(ta[0:64, :], ps[0:64, 0:T], ACT.Copy)
                elif n == 2:
                    i_ = nc.scalar.activation(sga, ps[:, 0:T], ACT.Sigmoid)
                elif n == 3:
                    i_ = nc.scalar.activation(sgb[0:32, :], ps[0:32, 0:T], ACT.Sigmoid)
                elif n < 8:
                    i_ = nc.scalar.activation(sig[:, (n - 4) // 2, (n % 2) * 512:(n % 2) * 512 + 512], ps, ACT.Sigmoid)
                else:
                    i_ = nc.scalar.activation(aT[:, n - 8, :], ps, ACT.Sigmoid, bias=col("o_a0", n - 8))
                i_.then_inc(o_act, 1)
            for k in range(KT):
                act.wait_ge(o_mm, 25 + k)
                ps = psum[:, k, :].rearrange("p (b a t) -> p b a t", b=TB, a=2)
                two = lambda x: x[:, k, :].rearrange("p (b t) -> p b t", b=TB)
                nc.scalar.activation(two(Wi), ps[:, :, 0, :], ACT.Exp, scale=-SQRT_E_INV)
                nc.scalar.activation(two(We), ps[:, :, 1, :], ACT.Exp, scale=-SQRT_E_INV)
                nc.scalar.activation(two(Wv), ps[:, :, 0, :], ACT.Exp, scale=SQRT_E_INV).then_inc(o_act, 1)
            def copies(dst, n0, ks):
                for k in ks:
                    act.wait_ge(o_mm, n0 + k + 1)
                    nc.scalar.activation(dst[:, k, :], psum[:, k, 0:T], ACT.Copy).then_inc(o_act, 1)
            copies(rT, 32, range(KT))
            copies(vT, 48, range(4))
            act.wait_ge(k_ss, 1)
            nc.scalar.activation(kn, psum[0:8, 7, :], ACT.Sqrt).then_inc(k_sd, 1)
            copies(vT, 48, range(4, KT))
            for n in range(4):
                act.wait_ge(v_tr, n + 1)
                nc.scalar.activation(v_row[:, 512 * n:512 * n + 512], psum[:, 4 + n, :], ACT.Copy).then_inc(v_rows, 1)
            for n in range(4):
                act.wait_ge(bk_tr, n + 1)
                nc.scalar.activation(xn[:, 512 * n:512 * n + 512], psum[:, n, :], ACT.Copy).then_inc(bk_rows, 1)
            for s_ in range(4):
                c = s_ // 2
                for q in range(2):
                    act.wait_ge(x_tr, 2 * s_ + q + 1)
                    if s_ >= 1:
                        act.wait_ge(lv_x, lev(s_ - 1, 6, q))
                    nc.scalar.activation(Xs[q], r3(psum[:, 4 * q, :], 4), ACT.Copy).then_inc(x_ev, 1)
                for li in range(1, 7):
                    for q in range(2):
                        act.wait_ge(lv_y, lev(s_, li, q))
                        nc.scalar.activation(Ys[q], r3(psum[:, 4 * q + 1, :], 4), ACT.Copy).then_inc(lv_yc, 1)
                    if (s_, li) == (3, 3):
                        act.wait_ge(gn_c, 1)
                        nc.scalar.activation(sqT[:, 0:4, :], YT[:, 0:4, :], ACT.Square).then_inc(gn_q, 1)
                    if (s_, li) == (3, 5):
                        act.wait_ge(gn_ve, 1)
                        nc.scalar.activation(gs, gs, ACT.Sqrt).then_inc(gn_sd, 1)
                for q in range(2):
                    act.wait_ge(t_r, 2 * s_ + q + 1)
                    for e in range(2):
                        last = nc.scalar.activation(Rs[q].rearrange("p (j e i) -> p e j i", j=2, e=2)[:, e],
                                                    halves(4 * q, e), ACT.Copy)
                    last.then_inc(t_rc, 1)
                for q in range(2):
                    act.wait_ge(t_y, 2 * s_ + q + 1)
                    k = 2 * (2 * s_ % 4 + q)
                    nc.scalar.activation(YT[:, k:k + 2, c * P:(c + 1) * P], r3(psum[:, 4 * q + 2, 0:256], 2),
                                         ACT.Copy).then_inc(t_yc, 1)
            act.wait_ge(gn_c, 2)
            nc.scalar.activation(sqT[:, 4:KT, :], YT[:, 4:KT, :], ACT.Square).then_inc(gn_q, 1)
            act.wait_ge(gn_ve, 2)
            nc.scalar.activation(gs, gs, ACT.Sqrt).then_inc(gn_sd, 1)

        def halves(bank, e):
            return psum[:, bank, :].rearrange("p (j x i) -> p j x i", j=2, i=HD)[:, :, 3 * e, :]

        def rwkv_dve(dve):
            norm_cols(2, "o_norm_mix")[1](dve)
            nc.vector.tensor_scalar(omk, col("o_k_a", 0, 8), -1.0, 1.0, ALU.mult, ALU.add)
            nc.vector.memset(tw[64:65, :], 1.0).then_inc(ones_row, 1)
            norm_ready(dve, 2)
            nc.vector.tensor_tensor(xx[:, :, 1:], xnT[:, :, 0:T - 1], xnT[:, :, 1:], ALU.subtract)
            link(dve, "dve", nc.vector.tensor_scalar(xx[:, :, 0:1], xnT[:, :, 0:1], -1.0, None, ALU.mult))
            ffn_product(dve, "d", NFC - 1)

            def mixed(j):
                if j >= 2:
                    dve.wait_ge(o_mm, (1, 2, 4, 24)[j - 2])
                for k in range(KT):
                    last = nc.vector.scalar_tensor_tensor(out=mix[j][:, k, :], in0=xx[:, k, :],
                                                          scalar=col("o_mu", 8 * MIX[j] + k), in1=xnT[:, k, :],
                                                          op0=ALU.mult, op1=ALU.add)
                last.then_inc(mix_ready, 1)

            def copies(dst, n0):
                for k in range(KT):
                    dve.wait_ge(o_mm, n0 + k + 1)
                    nc.vector.tensor_copy(dst[:, k, :], psum[:, k, 0:T]).then_inc(o_dve, 1)

            V = nc.vector
            for j in range(5):
                mixed(j)
            copies(gT, 16)
            mixed(5)
            dve.wait_ge(o_act, 24)
            for k in range(KT):
                last = V.tensor_scalar(tmp[:, k, :], aT[:, k, :], col("o_k_a", k), omk[:, k:k + 1], ALU.mult, ALU.add)
            link(dve, "dve", last)
            link(dve, "dve", V.tensor_tensor(aT, aT, Wv, ALU.mult))
            copies(kT, 40)
            dve.wait_ge(o_dve, 16)
            for k in range(KT):
                last = V.tensor_scalar(kk[:, k, :], kT[:, k, :], col("o_k_k", k), None, ALU.mult)
            link(dve, "dve", last)
            dve.wait_ge(mix_ready, 6)
            V.tensor_tensor(sqT, kk, kk, ALU.mult).then_inc(k_sq, 1)
            link(dve, "dve", V.tensor_tensor(kT, kT, tmp, ALU.mult))
            dve.wait_ge(o_act, 32)
            for k in range(KT):
                last = V.scalar_tensor_tensor(out=tmp[:, k, :], in0=rT[:, k, :], scalar=col("o_r_k", k),
                                              in1=kT[:, k, :], op0=ALU.mult, op1=ALU.mult)
            last.then_inc(rk_done, 1)
            dve.wait_ge(k_sd, 1)
            link(dve, "dve", V.tensor_scalar(kn, kn, 1e-12, None, ALU.max))
            V.reciprocal(kn, kn).then_inc(k_inv, 1)
            for c in range(2):
                sl = slice(c * P, (c + 1) * P)
                V.scalar_tensor_tensor(out=AR[:, :, c, 0, :], in0=kk[:, :, sl], scalar=-1.0, in1=We[:, :, sl],
                                       op0=ALU.mult, op1=ALU.mult)
                last = V.tensor_tensor(AR[:, :, c, 1, :], rT[:, :, sl], Wi[:, :, sl], ALU.mult)
            last.then_inc(ar_done, 1)
            dve.wait_ge(ar_done, 1)
            link(dve, "dve", V.tensor_tensor(kk, kk, aT, ALU.mult))
            dve.wait_ge(rk_done, 1)
            V.tensor_tensor(kT, kT, Wv, ALU.mult).then_inc(bk_cols, 1)
            for half in range(2):
                dve.wait_ge(k_sp, half + 1)
                for i in range(2):
                    k = 4 * half + 2 * i
                    inv = psum[:, 2 * half + i, :]
                    last = V.tensor_tensor(kk[:, k:k + 2, :], kk[:, k:k + 2, :], r3(inv, 2), ALU.mult)
                last.then_inc(bk_cols, 1)
                for i in range(2):
                    k = 4 * half + 2 * i
                    inv = psum[:, 2 * half + i, :].rearrange("p (k c t) -> p k c t", k=2, c=2)
                    last = V.tensor_tensor(AR[:, k:k + 2, :, 0, :], AR[:, k:k + 2, :, 0, :], inv, ALU.mult)
                last.then_inc(ar_done, 1)
            for i in range(4):
                dve.wait_ge(bonus_mm, i + 1)
                V.tensor_tensor(vT[:, 2 * i:2 * i + 2, :], vT[:, 2 * i:2 * i + 2, :], r3(psum[:, 4 + i, :], 2),
                                ALU.mult).then_inc(bonus_done, 1)
            link(dve, "dve", nc.vector.reciprocal(fac, We[:, :, P]))
            link(dve, "dve", nc.vector.tensor_tensor(fac, fac, Wi[:, :, P - 1], ALU.mult))

            def gn_centre(half, banks):
                dve.wait_ge(gn_m, half + 1)
                for i in range(2):
                    y = YT[:, 4 * half + 2 * i:4 * half + 2 * i + 2, :]
                    last = V.scalar_tensor_tensor(out=y, in0=r3(psum[:, banks[i], :], 2), scalar=-1.0 / HD, in1=y,
                                                  op0=ALU.mult, op1=ALU.add)
                last.then_inc(gn_c, 1)

            def gn_var(half, bank):
                dve.wait_ge(gn_v, half + 1)
                V.tensor_scalar(gs, psum[0:8, bank, 0:T], 1.0 / HD, GN_EPS, ALU.mult, ALU.add).then_inc(gn_ve, 1)

            def gn_recip(half):
                dve.wait_ge(gn_sd, half + 1)
                V.reciprocal(gs, gs).then_inc(gn_r, 1)

            def gn_scale(half, banks):
                dve.wait_ge(gn_sp, half + 1)
                for i in range(2):
                    y = YT[:, 4 * half + 2 * i:4 * half + 2 * i + 2, :]
                    last = V.tensor_tensor(y, y, r3(psum[:, banks[i], :], 2), ALU.mult)
                last.then_inc(gn_n, 1)

            def gn_affine(half):
                dve.wait_ge(gn_n, half + 1)
                ks = slice(4 * half, 4 * half + 4)
                for k in range(4 * half, 4 * half + 4):
                    last = V.tensor_scalar(YT[:, k, :], YT[:, k, :], col("o_lnx_w", k), col("o_lnx_b", k), ALU.mult, ALU.add)
                link(dve, "dve", last)
                link(dve, "dve", V.tensor_tensor(YT[:, ks, :], YT[:, ks, :], vT[:, ks, :], ALU.add))
                V.tensor_tensor(YT[:, ks, :], YT[:, ks, :], gT[:, ks, :], ALU.mult).then_inc(gn_o, 1)

            for s_ in range(4):
                c = s_ // 2
                for q in range(2):
                    g = 2 * s_ + q
                    dve.wait_ge(a_mm, g + 1)
                    if s_ >= 1:
                        dve.wait_ge(al_done, lev(s_ - 1, 6, q))
                        dve.wait_ge(t_y, 2 * (s_ - 1) + q + 1)
                    for l in range(4):
                        for m, name in ((0, "before"), (1, "upto")):
                            src = psum[:, 4 * q + l, :].rearrange("p (a m t) -> p a m t", a=2, m=2)[:, :, m, :]
                            dst = A_sb[q][:, l, :, :].rearrange("p (a m) t -> p a m t", a=2)[:, :, m, :]
                            last = nc.vector.tensor_tensor(dst, src, C(name).unsqueeze(1).to_broadcast([P, 2, P]), ALU.mult)
                    last.then_inc(a_mask, 1)
                    dve.wait_ge(a_mask, g + 1)
                    four = lambda x: x.unsqueeze(1).to_broadcast([P, 4, P])
                    lv = C("level")[:, 0:P]
                    if s_ >= 1:
                        dve.wait_ge(t_u, 2 * (s_ - 1) + q + 1)
                    link(dve, "dve", nc.vector.tensor_tensor(XTs[q], A_sb[q][:, :, 0, :], four(lv), ALU.mult))
                    nc.vector.tensor_tensor(XTs[q], XTs[q], four(ident), ALU.add).then_inc(x_seed, 1)
                for li in range(1, 7):
                    for q in range(2):
                        dve.wait_ge(lv_x, lev(s_, li, q))
                        if li < 6:
                            nc.vector.tensor_tensor(Xs[q], Xs[q], r3(psum[:, 4 * q + 3, :], 4), ALU.add)
                        nc.vector.tensor_tensor(XTs[q], XTs[q], r3(psum[:, 4 * q + 2, :], 4), ALU.add).then_inc(lv_xa, 1)
                    if s_ == 3 and li in (2, 4, 5, 6):
                        if li == 2:
                            gn_centre(0, (0, 4))
                        elif li == 4:
                            gn_var(0, 0)
                        elif li == 5:
                            gn_recip(0)
                        else:
                            gn_scale(0, (0, 4))
                for q in range(2):
                    g = 2 * s_ + q
                    dve.wait_ge(t_u, g + 1)
                    for e in range(2):
                        last = nc.vector.tensor_copy(Us[q].rearrange("p (j e i) -> p e j i", j=2, e=2)[:, e], halves(4 * q + 1, e))
                    last.then_inc(t_uc, 1)
                if s_ == 3:
                    gn_affine(0)
                if c == 0:
                    for q in range(2):
                        g = 2 * s_ + q
                        dve.wait_ge(t_s, g + 1)
                        for j in range(2):
                            k = 2 * (2 * s_ % 4 + q) + j
                            last = nc.vector.scalar_tensor_tensor(
                                out=ST[:, k, :], in0=psum[:, 4 * q + 3, j * P:(j + 1) * P], scalar=fac[:, k:k + 1],
                                in1=C("heads"), op0=ALU.mult, op1=ALU.mult)
                        last.then_inc(t_sc, 1)
            gn_centre(1, (4, 5))
            gn_var(1, 6)
            gn_recip(1)
            gn_scale(1, (7, 4))
            gn_affine(1)
            add_to_h(dve, wo_done, (1, 2, 3, 4), 3)

        def rwkv_pool(pool):
            for s_ in range(4):
                for li in range(1, 7):
                    for q in range(2):
                        if li == 1:
                            pool.wait_ge(a_mask, 2 * s_ + q + 1)
                        if li >= 3:
                            pool.wait_ge(lv_y, lev(s_, li - 2, q))
                        elif s_ >= 1:
                            pool.wait_ge(lv_y, lev(s_ - 1, li + 4, q))
                        m = C("level")[:, li * P:(li + 1) * P].unsqueeze(1).to_broadcast([P, 4, P])
                        nc.gpsimd.tensor_tensor(ALs[q][li % 2], A_sb[q][:, :, 0, :], m, ALU.mult).then_inc(al_done, 1)
        r_in, r_mm, r_lg, r_ex, r_exd, r_sel, r_rank, r_jobs = (sem(x) for x in (
            "router_in", "router_product", "logits", "gate_exp_in", "gate_exp", "selected", "ranks", "jobs_ready"))
        m_hi, m_lo, m_pc = sem("pieces_hi"), sem("pieces_split"), sem("pieces_used")
        m_zero = sem("outputs_zeroed")
        m_xf, m_xh, m_hh = sem("gathered_full"), sem("gathered_hi"), sem("expert_hidden_hi")
        m_sil, m_h, m_T, m_hT = (sem(x) for x in ("expert_silu", "expert_hidden", "expert_hidden_T", "expert_hidden_cols"))
        m_p, m_pt, m_pte, m_ga, m_xg, m_yc, m_sc = (sem(x) for x in (
            "onehot_ready", "gates_transposed", "gates_copied", "gathered", "gathered_split", "expert_out_copied",
            "scattered"))
        jobs = sb("jobs", [P, 32], I32)
        spare = xnT[:, :, :].rearrange("p k t -> p (k t)")
        Pm, Pg, PgT = spare[:, 0:256], spare[:, 256:512], spare[:, 512:768]
        XG = spare[:, 768:1792]
        SIL = [wu(6, 512, 512 * i) for i in range(2)]
        Ysb = wu(6, 1024, 1024)
        HT = [[ht_split[:, i, w, :] for w in range(2)] for i in range(2)]
        gain = C("invcnt")
        tb_ = {}
        o = 128
        for name, w in (("rw", 64), ("L", 16), ("L2", 16), ("m1", 2), ("m2", 2), ("i1", 2), ("i2", 2), ("eq", 16), ("oh1", 16),
                        ("oh2", 16), ("ex", 2), ("w1", 2), ("w2", 2), ("g2", 16), ("sel", 16), ("rk", 32), ("gt", 32),
                        ("ova", 12), ("ovb", 12), ("ovc", 12), ("pick", 8), ("jf", 32), ("d", 2)):
            tb_[name] = small[:, o:o + w]
            o += w
        assert o <= 512
        router = tb_["rw"].rearrange("p (k e) -> p k e", k=KT)

        LOADS = [("g", 0), ("u", 0)]
        for c in range(1, NEC):
            LOADS += [("g", c), ("u", c), ("d", c - 1)]
        LOADS += [("d", NEC - 1)]
        NL = len(LOADS)
        assert NL % 7 == 0
        AT = {x: i for i, x in enumerate(LOADS)}
        LANDED = (48, 48, 48, 48, 16, 0, 0)
        SLOTS = (1, 0, 5, 6, 4, 2, 3)

        NP = 4 * NL

        def loaded(eng, j, i):
            k = SLOTS[i % 7]
            eng.wait_ge(slot_in[k], LANDED[k] + 16 * (i // 7 + 1) + j * (16 * NL // 7))

        def piece(i, n):
            return slot(SLOTS[i % 7])[:, 1024 * n:1024 * n + 1024]

        def consumed(eng, j, x):
            eng.wait_ge(m_pc, j * NP + (4 + 4 * AT[x] + 4))

        def moe_sp(sp):
            sp.wait_ge(o_mm, 56)
            sp.dma_start(router, I["o_router"].rearrange("a (k p) e -> p (a k) e", p=P)).then_inc(r_in, 16)
            wg = I["o_moe_wg"].rearrange("a e (k p) f -> (a e) p k f", p=P)
            wup = I["o_moe_wu"].rearrange("a e (k p) f -> (a e) p k f", p=P)
            wd = I["o_moe_wd"].rearrange("a e (k p) n -> (a e) p k n", p=P)

            def load(i, e):
                what, c = LOADS[i]
                if what == "d":
                    src = wd[bass.ds(e, 1), :, 4 * c:4 * c + 4, :]
                    dst = slot(SLOTS[i % 7]).rearrange("p (k n) -> p k n", k=4)
                else:
                    src = (wg if what == "g" else wup)[bass.ds(e, 1), :, :, EC * c:EC * c + EC]
                    dst = w8(SLOTS[i % 7])
                sp.dma_start(dst, src.rearrange("o p k n -> (o p) k n")).then_inc(slot_in[SLOTS[i % 7]], 16)

            def free(i, j):
                sp.wait_ge(m_lo, j * NP + 4 * (i + 1))

            for i in range(NL):
                if i == 3:
                    sp.wait_ge(gn_o, 2)
                    sp.dma_start(gain, I["final_norm"].partition_broadcast(P)).then_inc(r_in, 16)
                if i == 1:
                    sp.wait_ge(lv_y, lev(3, 6, 1))
                if i == 2:
                    sp.wait_ge(t_yc, 8)
                if i == 3:
                    sp.wait_ge(gn_o, 2)
                if i == 5:
                    sp.wait_ge(wo_done, 4)
                if i >= 7:
                    free(i - 7, 0)
                load(i, 0)
            sp.wait_ge(r_jobs, 2)
            J = sp.value_load(jobs[0:1, 12:13], min_val=NE, max_val=NE + 3)
            with sp.Fori(1, J) as j:
                e = sp.value_load(jobs[0:1, bass.ds(j + 16, 1)], min_val=0, max_val=NE - 1)
                for i in range(NL):
                    free(i - 7, j)
                    load(i, e)

        def gather(pe, q):
            for kk_ in range(4):
                k = 4 * q + kk_
                for b in range(TB):
                    last = nc.tensor.matmul(psum[:, 2 + q, kk_ * P:(kk_ + 1) * P], xn3[:, b, k * P:(k + 1) * P],
                                            Pm[:, b * P:(b + 1) * P], start=(b == 0), stop=(b == TB - 1))
            last.then_inc(m_ga, 1)

        def moe_pe(pe):
            pe.wait_ge(s_h, 12)
            norm_pe(pe, 3)
            norm_ready(pe, 3)
            pe.wait_ge(r_in, 32)
            for b in range(TB):
                for k in range(KT):
                    last = nc.tensor.matmul(psum[:, 4, 8 * b:8 * b + 8], xnT[:, k, b * P:(b + 1) * P], router[:, k, :],
                                            start=(k == 0), stop=(k == KT - 1))
            last.then_inc(r_mm, 1)
            pe.wait_ge(r_sel, 1)
            sel = r3(tb_["sel"], TB)
            nc.tensor.matmul(psum[:, 5, 0:8], C("before"), sel[:, 0, :], start=True, stop=True).then_inc(m_pc, 1)
            nc.tensor.matmul(psum[:, 5, 8:16], C("before"), sel[:, 1, :], start=True, stop=False).then_inc(m_pc, 1)
            nc.tensor.matmul(psum[:, 5, 8:16], C("ones"), sel[:, 0, :], start=False, stop=True).then_inc(m_pc, 1)
            nc.tensor.matmul(psum[:, 5, 16:24], C("ones"), sel[:, 0, :], start=True, stop=False).then_inc(m_pc, 1)
            nc.tensor.matmul(psum[:, 5, 16:24], C("ones"), sel[:, 1, :], start=False, stop=True).then_inc(r_mm, 1)
            pe.wait_ge(m_p, 1)
            for q in range(2):
                gather(pe, q)

            def three(dst, x_hi, x_lo, n, first, last_):
                hi, lo = n
                nc.tensor.matmul(dst, x_hi, hi, start=first, stop=False)
                nc.tensor.matmul(dst, x_lo, hi, start=False, stop=False)
                return nc.tensor.matmul(dst, x_hi, lo, start=False, stop=last_)

            def hidden(j, x, c):
                i = AT["gu"[x], c]
                for n in range(4):
                    pe.wait_ge(m_lo, j * NP + (4 * i + n + 1))
                    for m in range(2):
                        k = 2 * n + m
                        last = three(psum[:, 2 * (c % 2) + x, :], xg_split[:, 0, k, :], xg_split[:, 1, k, :],
                                     [w[:, (4 * i + n) % 4, 512 * m:512 * m + 512] for w in (w_hi, w_lo)], k == 0, k == KT - 1)
                    last.then_inc(m_pc, 1)

            def turned(j, c):
                pe.wait_ge(m_h, j * NEC + (c + 1))
                for f in range(4):
                    last = nc.tensor.transpose(psum[:, 6, f * P:(f + 1) * P], SIL[c % 2][:, f * P:(f + 1) * P], ident)
                last.then_inc(m_T, 1)

            def down(j, c):
                i = AT["d", c]
                pe.wait_ge(m_hT, j * NEC + (c + 1))
                for f in range(4):
                    pe.wait_ge(m_lo, j * NP + (4 * i + f + 1))
                    for q in range(2):
                        last = three(psum[:, 4 + q, :], HT[c % 2][0][:, f * P:(f + 1) * P], HT[c % 2][1][:, f * P:(f + 1) * P],
                                     [w[:, (4 * i + f) % 4, 512 * q:512 * q + 512] for w in (w_hi, w_lo)],
                                     c == 0 and f == 0, c == NEC - 1 and f == 3)
                    last.then_inc(m_pc, 1)

            def scattered(j):
                pe.wait_ge(m_pte, j + 1)
                pe.wait_ge(m_yc, j * 2 + 2)
                for b in range(TB):
                    for q in range(2):
                        nc.tensor.matmul(psum[:, 6 - 2 * q + b, :], PgT[:, b * P:(b + 1) * P],
                                         Ysb[:, 512 * q:512 * q + 512], start=True, stop=True).then_inc(m_sc, 1)

            pe.wait_ge(r_jobs, 2)
            J = pe.value_load(jobs[0:1, 12:13], min_val=NE, max_val=NE + 3)
            with pe.Fori(0, J) as j:
                pe.wait_ge(m_xg, j + 1)
                for c in range(NEC):
                    hidden(j, 0, c)
                    if c == 0:
                        scattered(j)
                    if c == 1:
                        pe.wait_ge(s_h, j * 4 + 16)
                        for b in range(TB):
                            last = nc.tensor.transpose(psum[:, 7, b * P:(b + 1) * P], Pg[:, b * P:(b + 1) * P], ident)
                        last.then_inc(m_pt, 1)
                    if c >= 1:
                        turned(j, c - 1)
                    hidden(j, 1, c)
                    if c >= 1:
                        down(j, c - 1)
                turned(j, NEC - 1)
                pe.wait_ge(m_p, j + 2)
                gather(pe, 0)
                gather(pe, 1)
                down(j, NEC - 1)
            scattered(J)

        def moe_act(act):
            norm_act(act, 3)
            norm_cols(3, "o_norm_ffn")[0](act)
            act.wait_ge(r_ex, 1)
            nc.scalar.activation(tb_["ex"], tb_["d"], ACT.Exp).then_inc(r_exd, 1)
            act.wait_ge(r_jobs, 2)
            J = act.value_load(jobs[0:1, 12:13], min_val=NE, max_val=NE + 3)
            act.wait_ge(m_xf, 1)
            nc.scalar.activation(xg_split[:, 0, :, :], r3(XG, KT), ACT.Copy).then_inc(m_xh, 1)

            def outputs(j):
                act.wait_ge(m_pc, j * NP + 4)
                for q in range(2):
                    nc.scalar.activation(Ysb[:, 512 * q:512 * q + 512], psum[:, 4 + q, :], ACT.Copy).then_inc(m_yc, 1)

            act.wait_ge(m_zero, 1)
            with act.Fori(0, J) as j:
                def turned(c):
                    act.wait_ge(m_T, j * NEC + (c + 1))
                    nc.scalar.activation(HT[c % 2][0], psum[:, 6, :], ACT.Copy).then_inc(m_hh, 1)
                for i, (what, c) in enumerate(LOADS):
                    loaded(act, j, i)
                    for n in range(4):
                        act.wait_ge(m_pc, j * NP + (4 * i + n + 1))
                        nc.scalar.activation(w_hi[:, (4 * i + n) % 4, :], piece(i, n), ACT.Copy).then_inc(m_hi, 1)
                    if i == 0:
                        outputs(j)
                    if what == "u":
                        consumed(act, j, ("g", c))
                        nc.scalar.activation(SIL[c % 2], psum[:, 2 * (c % 2), :], ACT.Silu).then_inc(m_sil, 1)
                        if c >= 1:
                            turned(c - 1)
                turned(NEC - 1)
                act.wait_ge(m_xf, j + 2)
                nc.scalar.activation(xg_split[:, 0, :, :], r3(XG, KT), ACT.Copy).then_inc(m_xh, 1)
            outputs(J)
            norm_act(act, 4, s_at=J * 4 + 16)

        def moe_dve(dve):
            norm_cols(3, "o_norm_ffn")[1](dve)
            L, L2, eq, oh1, oh2, g2_, sel = (r3(tb_[x], TB) for x in ("L", "L2", "eq", "oh1", "oh2", "g2", "sel"))
            wide = lambda x: tb_[x].unsqueeze(2).to_broadcast([P, TB, NE])
            iota8 = C("iota")[:, 0:NE]
            io = iota8.unsqueeze(1).to_broadcast([P, TB, NE])
            go = lambda ins: link(dve, "dve", ins)
            V = nc.vector
            dve.wait_ge(r_mm, 1)
            go(V.tensor_copy(L, r3(psum[:, 4, 0:16], TB)))
            go(V.tensor_reduce(tb_["m1"], L, AX.X, ALU.max))
            go(V.tensor_tensor(eq, L, wide("m1"), ALU.is_equal))
            go(V.scalar_tensor_tensor(out=eq, in0=eq, scalar=-float(NE), in1=io, op0=ALU.mult, op1=ALU.add))
            go(V.tensor_reduce(tb_["i1"], eq, AX.X, ALU.min))
            go(V.tensor_tensor(oh1, eq, wide("i1"), ALU.is_equal))
            go(V.scalar_tensor_tensor(out=L2, in0=oh1, scalar=-1e30, in1=L, op0=ALU.mult, op1=ALU.add))
            go(V.tensor_reduce(tb_["m2"], L2, AX.X, ALU.max))
            go(V.tensor_tensor(eq, L2, wide("m2"), ALU.is_equal))
            go(V.scalar_tensor_tensor(out=eq, in0=eq, scalar=-float(NE), in1=io, op0=ALU.mult, op1=ALU.add))
            go(V.tensor_reduce(tb_["i2"], eq, AX.X, ALU.min))
            go(V.tensor_tensor(oh2, eq, wide("i2"), ALU.is_equal))
            V.tensor_tensor(tb_["d"], tb_["m2"], tb_["m1"], ALU.subtract).then_inc(r_ex, 1)
            V.tensor_tensor(sel, oh1, oh2, ALU.add).then_inc(r_sel, 1)
            dve.wait_ge(r_exd, 1)
            go(V.tensor_scalar(tb_["w2"], tb_["ex"], 1.0, None, ALU.add))
            go(V.reciprocal(tb_["w1"], tb_["w2"]))
            go(V.tensor_tensor(tb_["w2"], tb_["ex"], tb_["w1"], ALU.mult))
            go(V.tensor_tensor(oh1, oh1, wide("w1"), ALU.mult))
            go(V.tensor_tensor(oh2, oh2, wide("w2"), ALU.mult))
            gt, rk = r3(tb_["gt"], TB), r3(tb_["rk"], TB)
            V.tensor_tensor(gt[:, :, 0:NE], oh1, oh2, ALU.add)
            V.tensor_tensor(gt[:, :, NE:2 * NE], oh1, oh2, ALU.add)
            dve.wait_ge(r_mm, 2)
            dve.wait_ge(r_sel, 1)
            go(V.scalar_tensor_tensor(out=g2_, in0=r3(psum[:, 5, 0:16], TB), scalar=1.0, in1=sel, op0=ALU.add, op1=ALU.mult))
            V.tensor_scalar(rk[:, :, 0:NE], g2_, -1.0, None, ALU.add)
            V.tensor_scalar(rk[:, :, NE:2 * NE], g2_, -1.0 - P, None, ALU.add)
            A_, B_, O_ = tb_["ova"], tb_["ovb"], tb_["ovc"]
            V.memset(A_, 0.0)
            V.memset(B_, 0.0)
            go(V.memset(tb_["jf"], 0.0))
            go(V.tensor_scalar(O_[:, 4:12], psum[:, 5, 16:24], P + 0.5, None, ALU.is_gt))
            go(V.tensor_copy(A_[:, 4:12], O_[:, 4:12]))
            go(V.tensor_tensor(B_[:, 4:12], A_[:, 4:12], A_[:, 3:11], ALU.add))
            go(V.tensor_tensor(A_[:, 4:12], B_[:, 4:12], B_[:, 2:10], ALU.add))
            go(V.tensor_tensor(B_[:, 4:12], A_[:, 4:12], A_[:, 0:8], ALU.add))
            go(V.tensor_tensor(A_[:, 4:12], B_[:, 4:12], O_[:, 4:12], ALU.mult))
            jf, pick = tb_["jf"], tb_["pick"]
            V.tensor_copy(jf[:, 0:NE], iota8)
            V.tensor_copy(jf[:, 16:16 + NE], iota8)
            go(V.tensor_scalar(jf[:, 12:13], B_[:, 11:12], float(NE), None, ALU.add))
            for i in range(3):
                go(V.scalar_tensor_tensor(out=pick, in0=A_[:, 4:12], scalar=float(i + 1), in1=iota8, op0=ALU.is_equal, op1=ALU.mult))
                go(V.tensor_reduce(jf[:, 24 + i:25 + i], pick, AX.X, ALU.add))
                go(V.tensor_scalar(jf[:, NE + i:NE + i + 1], B_[:, 11:12], i + 0.5, float(NE), ALU.is_gt, ALU.mult))
                go(V.tensor_tensor(jf[:, NE + i:NE + i + 1], jf[:, NE + i:NE + i + 1], jf[:, 24 + i:25 + i], ALU.add))
            V.tensor_copy(jobs[:, :], jf).then_inc(r_jobs, 1)
            dve.wait_ge(r_jobs, 1)
            V.tensor_copy(jobs[:, 31:32], jf[:, 31:32]).then_inc(r_jobs, 1)
            dve.wait_ge(r_jobs, 2)

            def onehot(col_):
                for b in range(TB):
                    r_ = rk[:, b, bass.ds(col_, 1)]
                    g_ = gt[:, b, bass.ds(col_, 1)]
                    V.tensor_scalar(Pm[:, b * P:(b + 1) * P], C("iota"), r_, None, ALU.is_equal)
                    last = V.tensor_scalar(Pg[:, b * P:(b + 1) * P], C("iota"), r_, g_, ALU.is_equal, ALU.mult)
                last.then_inc(m_p, 1)

            def gathered(n, job):
                for k in range(KT):
                    if k % 4 == 0:
                        dve.wait_ge(m_ga, n + k // 4)
                    last = V.tensor_scalar(XG[:, k * P:(k + 1) * P], psum[:, 2 + k // 4, (k % 4) * P:(k % 4 + 1) * P],
                                           col("o_norm_ffn", k), None, ALU.mult)
                last.then_inc(m_xf, 1)
                dve.wait_ge(m_xh, job)
                V.tensor_tensor(xg_split[:, 1, :, :], r3(XG, KT), xg_split[:, 0, :, :].bitcast(F32),
                                ALU.subtract).then_inc(m_xg, 1)

            def scattered(j):
                for b in range(TB):
                    for q in range(2):
                        dve.wait_ge(m_sc, j * 4 + (2 * b + q + 1))
                        hs = h[:, b, 512 * q:512 * q + 512]
                        V.tensor_tensor(hs, hs, psum[:, 6 - 2 * q + b, :], ALU.add).then_inc(s_h, 1)

            onehot(0)
            gathered(1, 1)
            V.memset(PgT, 0.0).then_inc(m_pte, 1)
            for q in range(2):
                last = V.memset(psum[:, 4 + q, :], 0.0)
            last.then_inc(m_zero, 1)
            J = dve.value_load(jobs[0:1, 12:13], min_val=NE, max_val=NE + 3)
            with dve.Fori(0, J) as j:
                def turned(c):
                    dve.wait_ge(m_hh, j * NEC + (c + 1))
                    V.tensor_tensor(HT[c % 2][1], psum[:, 6, :], HT[c % 2][0].bitcast(F32), ALU.subtract).then_inc(m_hT, 1)
                for i, (what, c) in enumerate(LOADS):
                    for n in range(4):
                        dve.wait_ge(m_hi, j * NP + (4 * i + n + 1))
                        r = (4 * i + n) % 4
                        V.tensor_tensor(w_lo[:, r, :], piece(i, n), w_hi[:, r, :].bitcast(F32), ALU.subtract).then_inc(m_lo, 1)
                    if (what, c) == ("u", 0):
                        scattered(j)
                    if what == "u" and c >= 1:
                        turned(c - 1)
                    if i >= 1 and LOADS[i - 1][0] == "u":
                        c_ = LOADS[i - 1][1]
                        consumed(dve, j, ("u", c_))
                        dve.wait_ge(m_sil, j * NEC + (c_ + 1))
                        V.tensor_tensor(SIL[c_ % 2], SIL[c_ % 2], psum[:, 2 * (c_ % 2) + 1, :], ALU.mult).then_inc(m_h, 1)
                    if (what, c) == ("d", 1):
                        dve.wait_ge(m_pt, j + 1)
                        V.tensor_copy(PgT, psum[:, 7, 0:256]).then_inc(m_pte, 1)
                    if (what, c) == ("d", 3):
                        nxt = dve.value_load(jobs[0:1, bass.ds(j + 1, 1)], min_val=0, max_val=2 * NE - 1)
                        onehot(nxt)
                turned(NEC - 1)
                gathered(j * 2 + 3, j + 2)
            scattered(J)
            norm_dve(dve, 4)
            for b in range(TB):
                dve.wait_ge(n_xn, 9 + b)
                V.tensor_tensor(h[:, b, :], xn3[:, b, :], gain, ALU.mult).then_inc(y_done, 1)

        def moe_pool(pool):
            for b in range(TB):
                pool.wait_ge(y_done, b + 1)
                pool.dma_start(out[0, b * P:(b + 1) * P, :], h[:, b, :]).then_inc(s_out, 16)
            pool.wait_ge(s_out, 32)
        y_done = sem("y_done")



        @block.sync
        def _(sp):
            sp.dma_start(h[:, :, :], I["x"].rearrange("b (n p) d -> p (b n) d", p=P)).then_inc(s_x, 16)
            sp.dma_start(cst[:, :], cst_dram[:, 0:CW]).then_inc(s_cst, 16)
            at = 0
            for group, base in ((COLUMNS, 0), (COLUMNS2, 1)):
                at = 0
                for name, n in group:
                    a = I[name]
                    dims = " ".join("abcd"[:len(a.shape)])
                    flat = a.rearrange(f"{dims} -> ({dims})").rearrange("(r c) -> r c", c=P)
                    sp.dma_start(colsrc[at:at + n, base * P:base * P + P], flat).then_inc(s_colsrc, 16)
                    at += n
            win = I["e_w_in"].rearrange("a (k p) n -> p (a k) n", p=P)
            for k in range(3):
                sp.dma_start(w8(k), win[:, :, 512 * k:512 * k + 512]).then_inc(slot_in[k], 16)
            wout = I["e_w_out"].rearrange("a (k p) n -> p (a k) n", p=P)
            for k in range(2):
                sp.dma_start(w8(3 + k), wout[:, :, 512 * k:512 * k + 512]).then_inc(slot_in[3 + k], 16)
            wg = I["e_ffn_wg"].rearrange("a (k p) f -> p (a k) f", p=P)
            wup = I["e_ffn_wu"].rearrange("a (k p) f -> p (a k) f", p=P)
            wd = I["e_ffn_wd"].rearrange("a (k p) n -> p (a k) n", p=P)
            for c in range(NFC):
                if c == 0:
                    sp.wait_ge(p_in, 8)
                if c == 1:
                    sp.wait_ge(p_in, 10)
                if c == 2:
                    sp.wait_ge(s_wo, 4)
                if c == 3:
                    sp.wait_ge(s_h, 4)
                if c >= 4:
                    ffn_split(sp, c - 4)
                if c == 4:
                    rwkv_lora_sp(sp)
                k = c % 4
                g, u, d = ffn_slot(k)
                sp.dma_start(g, wg[:, :, FC * c:FC * c + FC]).then_inc(ffn_in[k], 16)
                sp.dma_start(u, wup[:, :, FC * c:FC * c + FC]).then_inc(ffn_in[k], 16)
                sp.dma_start(d, wd[:, 2 * c:2 * c + 2, :]).then_inc(ffn_in[k], 16)
            rwkv_sp(sp)
            moe_sp(sp)

        @block.scalar
        def _(act):
            bc = lambda name, n: I[name].rearrange("a n -> (a n)").partition_broadcast(P)
            act.dma_start(E_["lng"], bc("e_sgu_ln_g", 512)).then_inc(s_small, 16)
            act.dma_start(E_["lnb"], bc("e_sgu_ln_b", 512)).then_inc(s_small, 16)
            act.dma_start(E_["bias"], I["e_sgu_bias"].rearrange("a h t -> (a h t)").partition_broadcast(P)).then_inc(s_small, 16)
            act.dma_start(r3(E_["ws"], 4), I["e_sgu_ws"].rearrange("a h t s -> t (a h) s")).then_inc(s_small, 16)
            act.dma_start(r3(E_["pw"], 4), I["e_pool_w"].rearrange("a g c d -> c (a g) d")).then_inc(s_small, 16)
            norm_act(act, 0)
            act.wait_ge(cols_done, 1)
            norm_cols(0, "e_norm_mix")[0](act)
            uT = r3(E_["uT"], 4)
            for g in range(4):
                act.wait_ge(p_in, 5 + g)
                nc.scalar.activation(uT[:, g, :], psum[:, 4 + g, 0:T], ACT.Gelu).then_inc(g_ev, 1)
            v = r3(E_["v"], 2)
            for b in range(TB):
                act.wait_ge(p_in, 9 + b)
                nc.scalar.activation(v[:, b, :], psum[:, b, :], ACT.Gelu).then_inc(g_ev, 1)
            act.wait_ge(s_vn, 1)
            nc.scalar.activation(small[:, 32:40], small[:, 24:32], ACT.Sqrt).then_inc(g_ev, 1)
            for g in range(4):
                act.wait_ge(s_ymm, g + 1)
                nc.scalar.activation(mixT[:, g, :], psum[:, 2 + g, 0:T], ACT.Copy, scale=col("e_pool_scale", g)).then_inc(s_yev, 1)
            norm_act(act, 1)
            norm_split_act(act)

            def hidden_hi(c):
                act.wait_ge(f_h, c + 1)
                if c >= 2:
                    ffn_product(act, "d", c - 2)
                nc.scalar.activation(fh_split[:, c % 2, 0, :], f_sil_buf[c % 2], ACT.Copy).then_inc(f_hh, 1)

            def silu(c):
                ffn_product(act, "g", c)
                if c >= 2:
                    act.wait_ge(f_hT, c - 1)
                nc.scalar.activation(f_sil_buf[c % 2], psum[:, 4 + 2 * (c % 2), :], ACT.Silu).then_inc(f_sil, 1)

            for i, (what, c, n) in enumerate(FPIECES):
                act.wait_ge(ffn_in[c % 4], 48 * (c // 4 + 1))
                if i >= 4:
                    act.wait_ge(f_pc, i - 3)
                nc.scalar.activation(as_piece(f_hi, i, what), ffn_piece(what, c, n), ACT.Copy).then_inc(f_phi, 1)
                if (what, n) == ("d", 0) and c + 1 < NFC:
                    silu(c + 1)
                if (what, c, n) == ("g", 1, 0):
                    silu(0)
                if (what, n) == ("g", 1) and c >= 1:
                    hidden_hi(c - 1)
                if (what, c, n) == ("d", NFC - 2, 1):
                    hidden_hi(NFC - 1)
            rwkv_act(act)
            moe_act(act)

        @block.vector
        def _(dve):
            a, s, t = (r3(E_[x], 4) for x in "ast")
            for x in (a, s, t):
                nc.vector.memset(x[:, :, 0:PAD], 0.0).then_inc(z_pad, 1)
            norm_dve(dve, 0)
            dve.wait_ge(colT, 2)
            nc.vector.tensor_copy(cols[:, :], psum[:, 3, 0:144]).then_inc(cols_done, 1)
            dve.wait_ge(cols_done, 1)
            norm_cols(0, "e_norm_mix")[1](dve)
            for g in range(4):
                dve.wait_ge(p_in, 1 + g)
                nc.vector.tensor_copy(a[:, g, PAD:], psum[:, g, 0:T]).then_inc(a_ev, 1)
            dve.wait_ge(a_ev, 4)
            dve.wait_ge(z_pad, 3)
            n = T + PAD
            link(dve, "dve", nc.vector.tensor_tensor(s[:, :, PAD:], a[:, :, PAD:], a[:, :, PAD - 1:n - 1], ALU.add))
            link(dve, "dve", nc.vector.tensor_tensor(t[:, 1:, PAD:], s[:, 1:, PAD:], s[:, 1:, PAD - 2:n - 2], ALU.add))
            link(dve, "dve", nc.vector.tensor_tensor(s[:, 2:, PAD:], t[:, 2:, PAD:], t[:, 2:, PAD - 4:n - 4], ALU.add))
            link(dve, "dve", nc.vector.tensor_tensor(t[:, 3:, PAD:], s[:, 3:, PAD:], s[:, 3:, PAD - 8:n - 8], ALU.add))
            inv = r3(C("invcnt"), 4)
            for g, src in enumerate((s, t, s, t)):
                last = nc.vector.tensor_tensor(pooled[:, g, :], src[:, g, PAD:], inv[:, g, :], ALU.mult)
            link(dve, "dve", last)
            nc.vector.tensor_tensor(pooled[:, :, :], pooled[:, :, :], a[:, :, PAD:], ALU.subtract).then_inc(s_pooled, 1)
            dve.wait_ge(s_wsT, 1)
            nc.vector.tensor_tensor(r3(E_["wsT"], 4), r3(psum[:, 6, :], 4),
                                    C("upto").unsqueeze(1).to_broadcast([P, 4, P]), ALU.mult).then_inc(s_wsTm, 1)
            dve.wait_ge(g_ev, 6)
            v8, c8, q8 = (r3(E_[x], 8) for x in ("v", "vc", "sq"))

            def per_head(x):
                return x.unsqueeze(2).to_broadcast([P, 8, P])
            link(dve, "dve", nc.vector.tensor_reduce(small[:, 8:16], v8, AX.X, ALU.add))
            link(dve, "dve", nc.vector.tensor_scalar(small[:, 8:16], small[:, 8:16], 1.0 / P, None, ALU.mult))
            link(dve, "dve", nc.vector.tensor_tensor(c8, v8, per_head(small[:, 8:16]), ALU.subtract))
            link(dve, "dve", nc.vector.tensor_tensor(q8, c8, c8, ALU.mult))
            link(dve, "dve", nc.vector.tensor_reduce(small[:, 16:24], q8, AX.X, ALU.add))
            nc.vector.tensor_scalar(small[:, 24:32], small[:, 16:24], 1.0 / P, LN_EPS, ALU.mult, ALU.add).then_inc(s_vn, 1)
            dve.wait_ge(g_ev, 7)
            link(dve, "dve", nc.vector.reciprocal(small[:, 40:48], small[:, 32:40]))
            link(dve, "dve", nc.vector.tensor_tensor(c8, c8, per_head(small[:, 40:48]), ALU.mult))
            c2 = r3(E_["vc"], 2)
            dve.wait_ge(s_small, 80)
            bc = lambda x: x.unsqueeze(1).to_broadcast([P, 2, 512])
            link(dve, "dve", nc.vector.tensor_tensor(c2, c2, bc(E_["lng"]), ALU.mult))
            nc.vector.tensor_tensor(c2, c2, bc(E_["lnb"]), ALU.add).then_inc(s_vn, 1)
            for q in range(2):
                dve.wait_ge(s_mm, q + 1)
                dst = mixT[:, 4 + 2 * q:6 + 2 * q, :].rearrange("p g (n t) -> p g n t", n=2)
                src = psum[:, 6 + q, :].rearrange("p (g n t) -> p g n t", g=2, n=2)
                b4 = r3(E_["bias"], 4)[:, 2 * q:2 * q + 2, :].unsqueeze(2).to_broadcast([P, 2, 2, P])
                link(dve, "dve", nc.vector.tensor_tensor(dst, src, b4, ALU.add))
                nc.vector.tensor_tensor(mixT[:, 4 + 2 * q:6 + 2 * q, :], mixT[:, 4 + 2 * q:6 + 2 * q, :],
                                        r3(E_["uT"], 4)[:, 2 * q:2 * q + 2, :], ALU.mult).then_inc(s_mix, 1)
            add_to_h(dve, s_wo, (1, 2, 3, 4), 1)
            norm_split_dve(dve)

            def hidden(c):
                ffn_product(dve, "u", c)
                dve.wait_ge(f_sil, c + 1)
                nc.vector.tensor_tensor(f_sil_buf[c % 2], f_sil_buf[c % 2], psum[:, 5 + 2 * (c % 2), :],
                                        ALU.mult).then_inc(f_h, 1)

            def hidden_lo(c):
                dve.wait_ge(f_hh, c + 1)
                dve.wait_ge(f_h, c + 1)
                nc.vector.tensor_tensor(fh_split[:, c % 2, 1, :], f_sil_buf[c % 2], fh_split[:, c % 2, 0, :].bitcast(F32),
                                        ALU.subtract).then_inc(f_hT, 1)

            for i, (what, c, n) in enumerate(FPIECES):
                dve.wait_ge(f_phi, i + 1)
                nc.vector.tensor_tensor(as_piece(f_lo, i, what), ffn_piece(what, c, n),
                                        as_piece(f_hi, i, what).bitcast(F32), ALU.subtract).then_inc(f_plo, 1)
                if (what, n) == ("g", 0) and c >= 1:
                    hidden(c - 1)
                if (what, n) == ("g", 1) and c >= 1:
                    hidden_lo(c - 1)
                if (what, c, n) == ("d", NFC - 2, 1):
                    hidden(NFC - 1)
                    hidden_lo(NFC - 1)
            add_to_h(dve, f_pc, (len(FPIECES),) * 4, 2)
            rwkv_dve(dve)
            moe_dve(dve)

        @block.tensor
        def _(pe):
            pe.wait_ge(s_cst, 16)
            pe.wait_ge(s_colsrc, 16 * (len(COLUMNS) + len(COLUMNS2)))
            nc.tensor.transpose(psum[:, 3, 0:P], colsrc[:, 0:P], ident).then_inc(colT, 1)
            nc.tensor.transpose(psum[:, 3, P:P + 16], colsrc[0:16, P:2 * P], cst[0:16, 0:16]).then_inc(colT, 1)
            norm_pe(pe, 0)
            norm_ready(pe, 0)
            pe.wait_ge(slot_in[0], 16)
            pe.wait_ge(cols_done, 1)
            for g in range(8):
                if g == 4:
                    pe.wait_ge(slot_in[1], 16)
                for k in range(KT):
                    last = nc.tensor.matmul(psum[:, g, 0:T], w8(g // 4)[:, k, (g % 4) * P:(g % 4 + 1) * P],
                                            xnT[:, k, :], start=(k == 0), stop=(k == KT - 1))
                last.then_inc(p_in, 1)
            pe.wait_ge(slot_in[2], 16)
            for b in range(TB):
                pe.wait_ge(a_ev, b + 1)
                for k in range(KT):
                    last = nc.tensor.matmul(psum[:, b, :], xnT[:, k, b * P:(b + 1) * P], w8(2)[:, k, :],
                                            start=(k == 0), stop=(k == KT - 1))
                last.then_inc(p_in, 1)
            pe.wait_ge(s_small, 80)
            pe.wait_ge(g_ev, 4)
            for g in range(4):
                last = nc.tensor.transpose(psum[:, 6, g * P:(g + 1) * P], r3(E_["ws"], 4)[:, g, :], ident)
            last.then_inc(s_wsT, 1)
            pe.wait_ge(s_pooled, 1)
            pe.wait_ge(a_ev, 4)
            for g in range(4):
                nc.tensor.matmul(psum[:, 2 + g, 0:T], r3(E_["pw"], 4)[:, g, :], pooled[:, g, :],
                                 start=True, stop=True).then_inc(s_ymm, 1)
            pe.wait_ge(s_vn, 2)
            pe.wait_ge(s_wsTm, 1)
            for q in range(2):
                for g in (2 * q, 2 * q + 1):
                    for b in range(TB):
                        o = (g % 2) * T + b * P
                        last = nc.tensor.matmul(psum[:, 6 + q, o:o + P],
                                                E_["vc"][:, b * 512 + g * P:b * 512 + (g + 1) * P],
                                                r3(E_["wsT"], 4)[:, g, :], start=True, stop=True)
                last.then_inc(s_mm, 1)
            pe.wait_ge(slot_in[3], 16)
            pe.wait_ge(slot_in[4], 16)
            pe.wait_ge(s_mix, 2)
            pe.wait_ge(s_yev, 4)
            pe.wait_ge(g_ev, 6)
            rows_product(pe, mixT, lambda q: w8(3 + q), 0, s_wo)
            pe.wait_ge(s_h, 4)
            norm_pe(pe, 1)
            norm_ready(pe, 1)

            def three(dst, l_hi, l_lo, r_hi, r_lo, first, last_):
                nc.tensor.matmul(dst, l_hi, r_hi, start=first, stop=False)
                nc.tensor.matmul(dst, l_lo, r_hi, start=False, stop=False)
                return nc.tensor.matmul(dst, l_hi, r_lo, start=False, stop=last_)

            def gate_up(c):
                for w, bank in enumerate((4, 5)):
                    bank += 2 * (c % 2)
                    if c >= 2:
                        pe.wait_ge(f_sil if w == 0 else f_h, c - 1)
                    for j in range(2):
                        i = FAT["gu"[w], c, j]
                        pe.wait_ge(f_plo, i + 1)
                        hi, lo = as_piece(f_hi, i, "g"), as_piece(f_lo, i, "g")
                        for k in range(KT):
                            last = three(psum[:, bank, j * T:(j + 1) * T], hi[:, k, :], lo[:, k, :], x_split[:, 1, k, :],
                                         x_split[:, 0, k, :], k == 0, k == KT - 1)
                        last.then_inc(f_pc, 1)

            def down(c):
                pe.wait_ge(f_hT, c + 1)
                for j in range(2):
                    i = FAT["d", c, j]
                    pe.wait_ge(f_plo, i + 1)
                    for b in range(TB):
                        tok = slice(j * T + b * P, j * T + (b + 1) * P)
                        for q in range(2):
                            half = slice(512 * q, 512 * q + 512)
                            last = three(psum[:, 2 * b + q, :], fh_split[:, c % 2, 0, tok], fh_split[:, c % 2, 1, tok],
                                         f_hi[:, i % 4, half], f_lo[:, i % 4, half], c == 0 and j == 0,
                                         c == NFC - 1 and j == 1)
                    last.then_inc(f_pc, 1)

            for c in range(NFC + 1):
                if c < NFC:
                    gate_up(c)
                if c >= 1:
                    down(c - 1)
            rwkv_pe(pe)
            moe_pe(pe)

        @block.gpsimd
        def _(pool):
            rwkv_pool(pool)
            moe_pool(pool)


_OUT = (1, T, D)


def kernel(**inputs):
    from concourse import bacc
    from concourse.bass_utils import run_bass_kernel_spmd
    nc = bacc.Bacc("TRN2", target_bir_lowering=False, num_devices=1)
    arrays, aps = {}, {}
    for name, a in inputs.items():
        if a.size:
            a = np.ascontiguousarray(a)
            arrays[name + "_dram"] = a
            aps[name] = nc.dram_tensor(name + "_dram", a.shape, mybir.dt.from_np(a.dtype), kind="ExternalInput").ap()
    arrays["constants_dram"] = constants()
    cst = nc.dram_tensor("constants_dram", (P, CD), F32, kind="ExternalInput").ap()
    out = nc.dram_tensor("out_dram", _OUT, F32, kind="ExternalOutput").ap()
    trunk(nc, aps, cst, out)
    return run_bass_kernel_spmd(nc, [arrays], core_ids=[0]).results[0]["out_dram"]
```
